# Optimizing a Trainium2 kernel written in Bass

```python
import math
import jax
import jax.numpy as jnp
from jax import lax
import numpy as np

D_MODEL = 1024
BATCH = 1
SEQ = 256
DEPTH = 2

MIX = D_MODEL
A_WIDTH = MIX // 2
M_WIDTH = MIX - A_WIDTH
A_HEADS = 4
A_DH = A_WIDTH // (2 * A_HEADS)
A_DV = 2 * A_DH
M_HEADS = 4
M_DH = M_WIDTH // M_HEADS
CONV_K = 4
CHUNK = 64
Q_BLOCK = 128
N_BUCKETS = 32
MAX_DIST = 128
D_FF = (7 * D_MODEL) // 2
N_EXPERTS = 8
TOP_K = 2
EPS = 1e-6
IN_SIZES = (A_WIDTH, A_WIDTH, A_WIDTH, M_WIDTH, M_WIDTH, M_WIDTH, M_WIDTH, M_HEADS, M_HEADS)
IN_W = sum(IN_SIZES)
IN_SPLITS = tuple(int(s) for s in np.cumsum(IN_SIZES)[:-1])

kernel_name = "hymba_diffattn_mlstm_moe_trunk"

F32 = jnp.float32

def rmsnorm(x, g):
    xf = x.astype(F32)
    y = xf * lax.rsqrt(jnp.mean(xf * xf, axis=-1, keepdims=True) + EPS)
    return (y * g.astype(F32)).astype(x.dtype)

def t5_bucket(n):
    max_exact = N_BUCKETS // 2
    nf = jnp.maximum(n, 1).astype(F32)
    large = max_exact + (jnp.log(nf / max_exact) / math.log(MAX_DIST / max_exact)
                         * (N_BUCKETS - max_exact)).astype(jnp.int32)
    large = jnp.minimum(large, N_BUCKETS - 1)
    return jnp.where(n < max_exact, n, large)

def causal_dwconv(x, w, b):
    S = x.shape[1]
    xp = jnp.pad(x, ((0, 0), (CONV_K - 1, 0), (0, 0)))
    y = b
    for j in range(CONV_K):
        y = y + xp[:, j:j + S] * w[j]
    return y

def diff_attention(q, k, v, lam, lam_init, dist_bias, norm_g):
    B, S = q.shape[0], q.shape[1]
    nb = S // Q_BLOCK
    q = q * (A_DH ** -0.5)
    kpos = jnp.arange(S)

    def block(i):
        q0 = i * Q_BLOCK
        qb = lax.dynamic_slice_in_dim(q, q0, Q_BLOCK, axis=1)
        dist = (q0 + jnp.arange(Q_BLOCK))[:, None] - kpos[None, :]
        bias = jnp.take(dist_bias, jnp.clip(dist, 0, S - 1), axis=1)
        s = jnp.einsum('bqhcd,bkhcd->bhcqk', qb, k).astype(F32) + bias[None, :, None]
        s = jnp.where(dist >= 0, s, -jnp.inf)
        p = jax.nn.softmax(s, axis=-1)
        a = p[:, :, 0] - lam * p[:, :, 1]
        return jnp.einsum('bhqk,bkhe->bqhe', a.astype(v.dtype), v)

    o = lax.map(block, jnp.arange(nb))
    o = jnp.moveaxis(o, 0, 1).reshape(B, S, A_HEADS, A_DV)
    return rmsnorm(o, norm_g) * (1.0 - lam_init)

def mlstm_chunkwise(q, k, v, i_pre, f_pre):
    B, S, H, d = q.shape
    nc = S // CHUNK

    def chunks(t):
        t = t.astype(F32).reshape((B, nc, CHUNK, H) + t.shape[3:])
        return jnp.moveaxis(t, 3, 1)

    qc, kc, vc = chunks(q), chunks(k * (d ** -0.5)), chunks(v)
    ig = chunks(i_pre)
    lf = jax.nn.log_sigmoid(chunks(f_pre))
    b = jnp.cumsum(lf, axis=-1)
    b_last = b[..., -1]
    a = b_last[..., None] - b + ig

    def step(carry, xs):
        C, n, m = carry
        a_c, bl_c, k_c, v_c = xs
        m_new = jnp.maximum(bl_c + m, jnp.max(a_c, axis=-1))
        decay = jnp.exp(bl_c + m - m_new)
        w = jnp.exp(a_c - m_new[..., None])
        C_new = decay[..., None, None] * C + jnp.einsum('bhl,bhlk,bhlv->bhkv', w, k_c, v_c)
        n_new = decay[..., None] * n + jnp.einsum('bhl,bhlk->bhk', w, k_c)
        return (C_new, n_new, m_new), (C, n, m)

    init = (jnp.zeros((B, H, d, d), F32), jnp.zeros((B, H, d), F32), jnp.zeros((B, H), F32))
    xs = (jnp.moveaxis(a, 2, 0), jnp.moveaxis(b_last, 2, 0),
          jnp.moveaxis(kc, 2, 0), jnp.moveaxis(vc, 2, 0))
    _, (C_prev, n_prev, m_prev) = lax.scan(step, init, xs)
    C_prev = jnp.moveaxis(C_prev, 0, 2)
    n_prev = jnp.moveaxis(n_prev, 0, 2)
    m_prev = jnp.moveaxis(m_prev, 0, 2)

    tri = jnp.tril(jnp.ones((CHUNK, CHUNK), dtype=bool))
    Dm = jnp.where(tri, b[..., :, None] - b[..., None, :] + ig[..., None, :], -jnp.inf)
    inter = b + m_prev[..., None]
    m_t = jnp.maximum(inter, jnp.max(Dm, axis=-1))
    Sw = jnp.einsum('bhnld,bhnsd->bhnls', qc, kc) * jnp.exp(Dm - m_t[..., None])
    dec = jnp.exp(inter - m_t)
    num = (dec[..., None] * jnp.einsum('bhnld,bhnde->bhnle', qc, C_prev)
           + jnp.einsum('bhnls,bhnse->bhnle', Sw, vc))
    den = dec * jnp.einsum('bhnld,bhnd->bhnl', qc, n_prev) + jnp.sum(Sw, axis=-1)
    h = num / jnp.maximum(jnp.abs(den), jnp.exp(-m_t))[..., None]
    return jnp.moveaxis(h, 1, 3).reshape(B, S, H, d)

def swiglu(t, w1, w3, w2):
    return (jax.nn.silu(t @ w1) * (t @ w3)) @ w2

def moe_swiglu(h, router_w, w1, w3, w2):
    B, S, D = h.shape
    t = h.reshape(B * S, D)
    logits = (t @ router_w).astype(F32)
    top_v, top_i = lax.top_k(logits, TOP_K)
    wts = jax.nn.softmax(top_v, axis=-1)
    gates = jnp.sum(jax.nn.one_hot(top_i, N_EXPERTS, dtype=F32) * wts[..., None], axis=1)
    out = jnp.zeros_like(t)
    for e in range(N_EXPERTS):
        out = out + gates[:, e:e + 1].astype(t.dtype) * swiglu(t, w1[e], w3[e], w2[e])
    return out.reshape(B, S, D)

def setup_inputs(seed: int = 0) -> dict:
    key = jax.random.key(seed)
    ks = jax.random.split(key, 24)
    n_dense = (DEPTH + 1) // 2
    n_moe = DEPTH // 2
    D = D_MODEL
    nrm = jax.random.normal
    gate_b = jnp.stack([
        0.1 * nrm(ks[8], (DEPTH, M_HEADS), F32),
        jnp.linspace(3.0, 6.0, M_HEADS, dtype=F32)[None, :] + 0.1 * nrm(ks[9], (DEPTH, M_HEADS), F32),
    ], axis=1)
    return {
        "x": nrm(ks[0], (BATCH, SEQ, D), F32),
        "c": nrm(ks[1], (BATCH, D), F32),
        "rel_bias": 0.5 * nrm(ks[2], (N_BUCKETS, A_HEADS), F32),
        "ada_w": 0.5 * D ** -0.5 * nrm(ks[3], (DEPTH, D, 6 * D), F32),
        "ada_b": 0.02 * nrm(ks[4], (DEPTH, 6 * D), F32),
        "norm_g": 1.0 + 0.05 * nrm(ks[5], (DEPTH, 4, D), F32),
        "w_in": D ** -0.5 * nrm(ks[6], (DEPTH, D, IN_W), F32),
        "gate_b": gate_b,
        "conv_w": CONV_K ** -0.5 * nrm(ks[10], (DEPTH, CONV_K, 2 * M_WIDTH), F32),
        "conv_b": 0.02 * nrm(ks[11], (DEPTH, 2 * M_WIDTH), F32),
        "lam_vec": 0.1 * nrm(ks[12], (DEPTH, 4, A_DH), F32),
        "attn_norm_g": 1.0 + 0.05 * nrm(ks[13], (DEPTH, A_DV), F32),
        "mlstm_norm_g": 1.0 + 0.05 * nrm(ks[14], (DEPTH, M_WIDTH), F32),
        "w_out": MIX ** -0.5 * nrm(ks[15], (DEPTH, MIX, D), F32),
        "ffn_w1": D ** -0.5 * nrm(ks[16], (n_dense, D, D_FF), F32),
        "ffn_w3": D ** -0.5 * nrm(ks[17], (n_dense, D, D_FF), F32),
        "ffn_w2": D_FF ** -0.5 * nrm(ks[18], (n_dense, D_FF, D), F32),
        "router_w": D ** -0.5 * nrm(ks[19], (n_moe, D, N_EXPERTS), F32),
        "moe_w1": D ** -0.5 * nrm(ks[20], (n_moe, N_EXPERTS, D, D_FF), F32),
        "moe_w3": D ** -0.5 * nrm(ks[21], (n_moe, N_EXPERTS, D, D_FF), F32),
        "moe_w2": D_FF ** -0.5 * nrm(ks[22], (n_moe, N_EXPERTS, D_FF, D), F32),
    }

def reference(x, c, rel_bias, ada_w, ada_b, norm_g, w_in, gate_b, conv_w, conv_b, lam_vec,
              attn_norm_g, mlstm_norm_g, w_out, ffn_w1, ffn_w3, ffn_w2, router_w,
              moe_w1, moe_w3, moe_w2):
    B, S, D = x.shape
    dist_bias = rel_bias[t5_bucket(jnp.arange(S, dtype=jnp.int32))].T.astype(F32)
    c_act = jax.nn.silu(c)
    for i in range(DEPTH):
        mod = c_act @ ada_w[i] + ada_b[i]
        sh1, sc1, g1, sh2, sc2, g2 = jnp.split(mod, 6, axis=-1)

        h = rmsnorm(x, norm_g[i, 0]) * (1.0 + sc1[:, None]) + sh1[:, None]
        proj = h @ w_in[i]
        aq, ak, av, mq, mk, mv, mo, mi, mf = jnp.split(proj, IN_SPLITS, axis=-1)

        lv = lam_vec[i].astype(F32)
        lam_init = 0.8 - 0.6 * math.exp(-0.3 * i)
        lam = jnp.exp(jnp.sum(lv[0] * lv[1])) - jnp.exp(jnp.sum(lv[2] * lv[3])) + lam_init
        a_out = diff_attention(aq.reshape(B, S, A_HEADS, 2, A_DH),
                               ak.reshape(B, S, A_HEADS, 2, A_DH),
                               av.reshape(B, S, A_HEADS, A_DV),
                               lam, lam_init, dist_bias, attn_norm_g[i])

        qk = jax.nn.silu(causal_dwconv(jnp.concatenate([mq, mk], axis=-1), conv_w[i], conv_b[i]))
        mq_c, mk_c = jnp.split(qk, 2, axis=-1)
        h_t = mlstm_chunkwise(mq_c.reshape(B, S, M_HEADS, M_DH),
                              mk_c.reshape(B, S, M_HEADS, M_DH),
                              mv.reshape(B, S, M_HEADS, M_DH),
                              mi + gate_b[i, 0], mf + gate_b[i, 1])
        h_m = jax.nn.sigmoid(mo.astype(F32)).reshape(B, S, M_HEADS, M_DH) * h_t
        h_m = rmsnorm(h_m, mlstm_norm_g[i].reshape(M_HEADS, M_DH)).astype(x.dtype)

        mixed = jnp.concatenate([a_out.reshape(B, S, A_WIDTH), h_m.reshape(B, S, M_WIDTH)], axis=-1)
        y = mixed @ w_out[i]
        x = x + g1[:, None] * rmsnorm(y, norm_g[i, 1])

        h = rmsnorm(x, norm_g[i, 2]) * (1.0 + sc2[:, None]) + sh2[:, None]
        if i % 2 == 0:
            j = i // 2
            y = swiglu(h, ffn_w1[j], ffn_w3[j], ffn_w2[j])
        else:
            j = i // 2
            y = moe_swiglu(h, router_w[j], moe_w1[j], moe_w3[j], moe_w2[j])
        x = x + g2[:, None] * rmsnorm(y, norm_g[i, 3])
    return x


_drawn_inputs = setup_inputs


def setup_inputs(seed=0):
    import zlib

    import numpy as np

    out = dict(_drawn_inputs(seed))
    spreads = {}
    factors = {'conv_b': 5.485}
    for name, (base, spread) in spreads.items():
        noise = np.random.default_rng([zlib.crc32(name.encode()), seed]).standard_normal(out[name].shape)
        drawn = base * np.exp(spread * noise) if base else spread * noise
        out[name] = jnp.asarray(drawn.astype(out[name].dtype))
    for name, factor in factors.items():
        out[name] = (out[name] * factor).astype(out[name].dtype)
    return out
```

```python
import math
from contextlib import ExitStack

import numpy as np
import concourse.bass as bass
from concourse import mybir

F32 = mybir.dt.float32
F32R = mybir.dt.float32r
I32 = mybir.dt.int32
U32 = mybir.dt.uint32
ACT = mybir.ActivationFunctionType
ALU = mybir.AluOpType
AX = mybir.AxisListType.X

P = 128
S = 256
NT = S // P
D = 1024
KT = D // P
L = 2
H = 4
DH = 64
DFF = 3584
NE = 8
NC = 512
NCH = DFF // NC
N_BUCKETS, MAX_DIST = 32, 128
EPS = 1e-6
NEG = -1e30

RAW = 14
SPLIT = 4
QW = 1024

GROUPS = [("gate", 0), ("up", 0)]
for _c in range(1, NCH):
    GROUPS += [("gate", _c), ("up", _c), ("down", _c - 1)]
GROUPS += [("down", NCH - 1)]
PASS_Q = 4 * len(GROUPS)
LAST_Q = {g: 4 * i + 3 for i, g in enumerate(GROUPS)}
assert PASS_Q % RAW == 0 and PASS_Q % SPLIT == 0


def turn_after(c):
    return LAST_Q[("up", 0)] if c == 0 else LAST_Q[("down", c - 1)]


W_IN = [("mq", 1536), ("mk", 2048), ("mv", 2560), ("mo", 3072), ("aq", 0), ("ak", 512), ("av", 1024)]
GATE_COL = 3584
FEATURE_MAJOR = ("mq", "mk", "aq", "ak")

PLAN = [("ada", 0, n) for n in range(4)]
for _i, (_n, _) in enumerate(W_IN):
    PLAN += [("in", 0, _i), ("ada", 0, 4 + _i)]
PLAN += [("ada", 0, 11), ("out", 0, 0), ("out", 0, 1)]
_a = 0
for _i in range(len(GROUPS)):
    PLAN += [("ffn", 0, _i)]
    if _i % 7 in (0, 2, 4, 6) and _a < 12:
        PLAN += [("ada", 1, _a)]
        _a += 1
assert _a == 12
PLAN += [("in", 1, i) for i in range(len(W_IN))] + [("out", 1, 0), ("out", 1, 1)]
RAW_AT, SPLIT_AT = {}, {}
_r = _w = 0
for _p in PLAN:
    RAW_AT[_p] = _r
    _r += 4
    if _p[0] != "ada":
        SPLIT_AT[_p] = _w
        _w += 4
RAW_MOE, SPLIT_MOE = _r, _w


def shape_constants():
    k = np.zeros((P, 1536), np.float32)
    p = np.arange(P)
    k[:, 0:128] = np.eye(P)
    k[:, 128:256] = np.where(p[:, None] > p[None, :], NEG, 0.0)
    k[:, 256:384] = (p[:, None] < p[None, :])
    k[:, 384:512] = p[None, :]
    k[:, 512:640] = 1.0
    dist = 255 - np.arange(384)
    n = np.maximum(dist, 0)
    exact = N_BUCKETS // 2
    nf = np.maximum(n, 1).astype(np.float32)
    large = exact + (np.log(nf / np.float32(exact)) / np.float32(math.log(MAX_DIST / exact))
                     * np.float32(N_BUCKETS - exact)).astype(np.int32)
    bucket = np.where(n < exact, n, np.minimum(large, N_BUCKETS - 1))
    for j in range(384):
        if dist[j] >= 0:
            k[bucket[j], 640 + j] = 1.0
        else:
            k[N_BUCKETS, 640 + j] = NEG
    for h in range(H):
        k[h, 1024 + h * P:1024 + (h + 1) * P] = 1.0
    return k


def trunk(nc, x, c, rel_bias, ada_w, ada_b, norm_g, w_in, gate_b, conv_w, conv_b, lam_vec, attn_norm_g,
          mlstm_norm_g, w_out, ffn_w1, ffn_w3, ffn_w2, router_w, moe_w1, moe_w3, moe_w2, tables, out):
    with ExitStack() as ctx:
        def sb(name, shape, dt=F32):
            return ctx.enter_context(nc.sbuf_tensor(name, shape, dt))

        sems = {}

        def sem(name):
            if name not in sems:
                sems[name] = ctx.enter_context(nc.semaphore(name))
            return sems[name]

        raw = sb("raw", [P, RAW, QW])
        w_hi = sb("w_hi", [P, SPLIT, QW], F32R)
        w_lo = sb("w_lo", [P, SPLIT, QW], F32R)
        hT_hi = sb("hT_hi", [P, KT, S], F32R)
        hT_lo = sb("hT_lo", [P, KT, S], F32R)
        sT_hi = sb("sT_hi", [P, 4, S], F32R)
        sT_lo = sb("sT_lo", [P, 4, S], F32R)
        xs = sb("xs", [P, NT, D])
        xn = sb("xn", [P, NT, D])
        K = sb("K", [P, 1536])
        grow = sb("grow", [P, 2, D])
        biasT = sb("biasT", [P, H, S])
        colT = sb("colT", [P, 3, P])
        cact = sb("cact", [P, KT])
        modcol = sb("modcol", [P, 48])
        modA = sb("modA", [P, 2, KT])
        mixA = sb("mixA", [P, KT])
        gw = sb("gw", [P, KT, 8])
        gw_hi = sb("gw_hi", [P, KT, 8], F32R)
        gw_lo = sb("gw_lo", [P, KT, 8], F32R)
        gbias = sb("gbias", [H, 4])
        lamc = sb("lamc", [P, 8])
        eps = sb("eps", [P, 1])
        small = sb("small", [P, 64])
        area = sb("area", [P, 13568])

        ident, negm, before, iota, ones = (K[:, i * P:(i + 1) * P] for i in range(5))
        onehot = K[0:N_BUCKETS + 1, 640:1024]
        headsel = K[0:H, 1024:1536]

        def part(at, *shape):
            n = int(np.prod(shape))
            v = area[:, at:at + n]
            if len(shape) == 2:
                v = v.rearrange("p (a b) -> p a b", a=shape[0])
            if len(shape) == 3:
                v = v.rearrange("p (a b c) -> p a b c", a=shape[0], b=shape[1])
            return v

        qk = part(0, 2 * H, S)
        aqT, akT = part(2048, H, S), part(3072, H, S)
        av, mv, so = part(4096, NT, NC), part(5120, NT, NC), part(6144, NT, NC)
        E = part(7168, 2, 384)
        Sw = part(7936, 2, 384)
        pr = part(8704, 2, 2, 384)
        aT = part(10240, 2, 384)
        sq = part(11008, NC)
        ngb = part(11520, 2, D)
        hidden = part(7168, NT, NC)
        htmp = part(8192, 2, NC)
        acc0 = part(7168, 2, NC)
        acc1 = part(0, 12, NC)
        ytmp = part(10240, D)
        tabs = part(9216, 3, P)
        lamrow = part(9728, 8, DH)
        brows = part(0, H, 384)
        relb = area[0:N_BUCKETS + 1, 4096:4608].rearrange("p (a b) -> p a b", a=H)
        lamp = part(4608, 4, DH)
        y_sb = part(0, NT, D)
        ye_sb = part(2048, D)
        xg = part(3072, D)
        disp = part(4096, NT, P)
        comb = part(4352, NT, P)
        combT = part(4608, S)
        routing = sb("routing", [P, 160])
        midx = sb("midx", [P, NT, 8], U32)
        flag = sb("flag", [P, 1], I32)
        ranks = routing[:, 0:18].rearrange("p (a b) -> p a b", a=NT)
        sel = routing[:, 18:36].rearrange("p (a b) -> p a b", a=NT)
        gates = routing[:, 36:54].rearrange("p (a b) -> p a b", a=NT)
        lg = routing[:, 54:70].rearrange("p (a b) -> p a b", a=NT)
        top = routing[:, 70:86].rearrange("p (a b) -> p a b", a=NT)
        topi = routing[:, 86:102].rearrange("p (a b) -> p a b", a=NT)
        pick = routing[:, 102:134].rearrange("p (n a b) -> p n a b", n=2, a=NT)
        tw = routing[:, 134:150]
        grows = area[0:H, 8704:8704 + 8 * S].rearrange("p (a b) -> p a b", a=8)
        gsb = sb("gsb", [P, NT, 8])
        acol = sb("acol", [P, NT, 8])

        PS = ctx.enter_context(nc.psum_tensor("PS", [P, 8, 512], F32))
        scratch = nc.dram_tensor("bias_rows_dram", [H, P, 384], F32)

        for i in range(RAW):
            sem(f"raw_loaded{i}")

        def source(p, q):
            kind, l, n = p
            if kind == "ada":
                return ada_w[l].rearrange("(k p) n -> p k n", p=P)[:, 2 * q:2 * q + 2, n * NC:(n + 1) * NC]
            if kind == "in":
                at = W_IN[n][1]
                return w_in[l].rearrange("(k p) n -> p k n", p=P)[:, 2 * q:2 * q + 2, at:at + NC]
            if kind == "out":
                return w_out[l].rearrange("(k p) n -> p k n", p=P)[:, 2 * q:2 * q + 2, n * NC:(n + 1) * NC]
            return hidden_source(ffn_w1[0], ffn_w3[0], ffn_w2[0], n, q)

        def hidden_source(w1, w3, w2, n, q):
            what, ch = GROUPS[n]
            if what == "down":
                return w2[ch * NC + q * P:ch * NC + (q + 1) * P, :]
            w = w1 if what == "gate" else w3
            return w.rearrange("(k p) n -> p k n", p=P)[:, 2 * q:2 * q + 2, ch * NC:(ch + 1) * NC]

        def raw_slot(i, wide):
            v = raw[:, i % RAW, :]
            return v if wide else v.rearrange("p (k n) -> p k n", k=2)

        class Pass:

            def __init__(self, blocks, chunks_before, e=None, round_=0):
                self.blocks, self.e, self.round = blocks, e, round_
                self.chunks_before = chunks_before

            def _v(self, base, per):
                base += per * NE * self.round
                return base if self.e is None else self.e * per + base

            def raw(self, q):
                if self.e is None:
                    return RAW_AT[("ffn", 0, q // 4)] + q % 4 + 1
                return self._v(RAW_MOE + q + 1, PASS_Q)

            def raw_static(self, q):
                return RAW_AT[("ffn", 0, q // 4)] + q % 4 if self.e is None else RAW_MOE + q

            def raw_round(self, q):
                r = self.raw_static(q) // RAW + 1
                return 16 * r if self.e is None else self._v(16 * r, 16 * PASS_Q // RAW)

            def split(self, q):
                if self.e is None:
                    return SPLIT_AT[("ffn", 0, q // 4)] + q % 4 + 1
                return self._v(SPLIT_MOE + q + 1, PASS_Q)

            def split_static(self, q):
                return (SPLIT_AT[("ffn", 0, 0)] if self.e is None else SPLIT_MOE) + q

            def chunk(self, ch):
                return self._v(self.chunks_before + ch + 1, NCH)

            def expert(self, n=1):
                return self._v(n, 1)

            def gate_bank(self, b):
                return b if self.blocks == 2 else 0

            def up_bank(self, b):
                return 2 + b if self.blocks == 2 else 1

        dense = Pass(NT, 0)

        def moe_pass(e, r):
            return Pass(1, NCH, e, r)

        def raw_load(sync, r, src, wide, free, landed=None):
            if free is not None:
                sync.wait_ge(sem("raw_used"), free)
            sync.dma_start(raw_slot(r, wide), src).then_inc(sem(f"raw_loaded{r % RAW}"), 16)

        block = ctx.enter_context(nc.Block())

        @block.sync
        def _(sync):
            sync.dma_start(xs[:, 0, :], x[0, 0:P, :]).then_inc(sem("x_loaded"), 16)
            sync.dma_start(xs[:, 1, :], x[0, P:S, :]).then_inc(sem("x_loaded"), 16)
            for p in PLAN:
                for q in range(4):
                    r = RAW_AT[p] + q
                    wide = p[0] == "ffn" and GROUPS[p[2]][0] == "down"
                    raw_load(sync, r, source(p, q), wide, r - RAW + 1 if r >= RAW else None)

            def moe_round(r):
                with sync.Fori(0, NE) as e:
                    ps = moe_pass(e, r)
                    for q in range(PASS_Q):
                        w1, w3, w2 = (w[0, bass.ds(e, 1)].rearrange("o a b -> (o a) b")
                                      for w in (moe_w1, moe_w3, moe_w2))
                        sync.wait_ge(sem("raw_used"), ps.raw(q) - RAW)
                        sync.dma_start(raw_slot(ps.raw_static(q), GROUPS[q // 4][0] == "down"),
                                       hidden_source(w1, w3, w2, q // 4, q % 4)
                                       ).then_inc(sem(f"raw_loaded{ps.raw_static(q) % RAW}"), 16)

            moe_round(0)
            sync.wait_ge(sem("flag_ready"), 1)
            over = sync.value_load(flag[0:1, 0:1], min_val=0, max_val=1)
            with sync.If(over > 0):
                moe_round(1)
            for i in range(NT):
                sync.wait_ge(sem("x_final"), i + 1)
                sync.dma_start(out[0, i * P:(i + 1) * P, :], xs[:, i, :]).then_inc(sem("out_stored"), 16)
            sync.wait_ge(sem("out_stored"), 16 * NT)

        @block.gpsimd
        def _(pool):
            pool.dma_start(K[:], tables).then_inc(sem("tables_loaded"), 16)
            for src, t, at in (
                (c.rearrange("b (n p) -> (b n) p", p=P), 2, 0),
                (attn_norm_g, 2, 8),
                (mlstm_norm_g.rearrange("l (n p) -> (l n) p", p=P), 2, 10),
                (norm_g.rearrange("l f (n p) -> (l f n) p", p=P), 0, 0),
                (ada_b.rearrange("l (n p) -> (l n) p", p=P), 1, 0),
                (conv_w.rearrange("l f (n p) -> (l f n) p", p=P), 0, 64),
                (conv_b.rearrange("l (n p) -> (l n) p", p=P), 1, 96),
            ):
                n = src.shape[0]
                pool.dma_start(tabs[at:at + n, t, :], src).then_inc(sem("rows_loaded"), 16)
            pool.dma_start(lamc[0:N_BUCKETS, 4:4 + H], rel_bias).then_inc(sem("rel_loaded"), 16)
            pool.dma_start(lamrow, lam_vec.rearrange("l f d -> (l f) d").partition_broadcast(P)
                           ).then_inc(sem("lam_loaded"), 16)
            pool.dma_start(gbias[:], gate_b.rearrange("l t h -> h (l t)"), allow_slow_non_contiguous=True).then_inc(sem("gbias_loaded"), 16)
            for l in range(L):
                if l:
                    pool.wait_ge(sem("post_done"), 2)
                    pool.wait_ge(sem("gw_split"), 1)
                pool.dma_start(gw[:], w_in[l].rearrange("(k p) n -> p k n", p=P)[:, :, GATE_COL:GATE_COL + 8]
                               ).then_inc(sem("gw_loaded"), 16)
                for sub in range(2):
                    at = (2 + 3 * sub) * D
                    pool.dma_start(grow[:, sub, :], ada_b[l, at:at + D].partition_broadcast(P)
                                   ).then_inc(sem("grow_loaded"), 16)
                    pool.dma_start(ngb[:, sub, :], norm_g[l, 1 + 2 * sub, :].partition_broadcast(P)
                                   ).then_inc(sem("grow_loaded"), 16)
                if l == 0:
                    pool.wait_ge(sem("bias_rows_copied"), 1)
                    pool.dma_start(scratch[:, :, :].rearrange("h p n -> p h n"), brows).then_inc(sem("bias_stored"), 16)
                    pool.wait_ge(sem("bias_stored"), 16)
                    for h in range(H):
                        skew = bass.AP(scratch, h * P * 384 + P - 1, [[383, P], [1, S]])
                        pool.dma_start(biasT[:, h, :], skew).then_inc(sem("bias_loaded"), 16)
            pool.wait_ge(sem("gw_split"), 2)
            pool.dma_start(gw[:], router_w[0].rearrange("(k p) n -> p k n", p=P)).then_inc(sem("gw_loaded"), 16)

        @block.scalar
        def _(act):
            done = [0]

            def after(ins):
                done[0] += 1
                ins.then_inc(sem("act_step"), 1)
                act.wait_ge(sem("act_step"), done[0])

            def hi_quarter(r, w, loaded, w_free):
                act.wait_ge(sem(f"raw_loaded{r % RAW}"), loaded)
                if w_free is not None:
                    act.wait_ge(sem("w_used"), w_free)
                nc.scalar.activation(w_hi[:, w % SPLIT, :], raw[:, r % RAW, :], ACT.Copy).then_inc(sem("hi_ready"), 1)

            def plan_quarter(p, q):
                w = SPLIT_AT[p] + q
                r = RAW_AT[p] + q
                hi_quarter(r, w, 16 * (r // RAW + 1), w - SPLIT + 1 if w >= SPLIT else None)

            def root(dst, src, n, scale):
                nc.scalar.activation(dst, src, ACT.Sqrt, bias=eps[:, 0:1], scale=scale).then_inc(sem("root_done"), 1)

            roots = [0]

            def norm_tokens(src, junk, what, n):
                for i in range(NT):
                    if what is not None:
                        act.wait_ge(sem(what), n[i])
                    after(nc.scalar.activation(junk(i), src(i), ACT.Square, accum_out=small[:, i:i + 1]))
                    roots[0] += 1
                    root(small[:, 2 + i:3 + i], small[:, i:i + 1], roots[0], 1.0 / D)

            turns = [0]

            def split_turned(scale, bias, taken=None):
                if taken is not None:
                    act.wait_ge(sem("ada_taken"), taken)
                for b in range(4):
                    turns[0] += 1
                    t = turns[0]
                    act.wait_ge(sem("turned"), t)
                    if t > 2:
                        act.wait_ge(sem("hT_lo_done"), t - 2)
                    for j in range(2):
                        k = 2 * b + j
                        ins = nc.scalar.activation(htmp[:, b % 2, j * S:(j + 1) * S], PS[:, b, j * S:(j + 1) * S],
                                                   ACT.Identity, bias=bias(k), scale=scale(k))
                    after(ins)
                    nc.scalar.activation(hT_hi[:, 2 * b:2 * b + 2, :], htmp[:, b % 2, :].rearrange("p (k n) -> p k n", k=2),
                                         ACT.Copy).then_inc(sem("hT_hi_done"), 1)

            act.wait_ge(sem("cols_turned"), 1)
            after(nc.scalar.activation(colT[:].rearrange("p a b -> p (a b)")[:, 0:240], PS[:, 4, 0:240], ACT.Copy))
            after(nc.scalar.activation(colT[:, 2, 0:18], PS[:, 4, 2 * P:2 * P + 18], ACT.Copy))
            nc.scalar.activation(cact[:], colT[:, 2, 0:KT], ACT.Silu).then_inc(sem("cact_ready"), 1)
            act.wait_ge(sem("lam_sums"), 1)
            after(nc.scalar.activation(lamc[:, 0:4], small[:, 8:12], ACT.Exp))
            nc.scalar.activation(small[:, 12:13], eps[:, 0:1], ACT.Copy).then_inc(sem("lam_exp"), 1)
            act.wait_ge(sem("bias_rows"), 1)
            nc.scalar.activation(brows, PS[:, 0:4, 0:384], ACT.Copy).then_inc(sem("bias_rows_copied"), 1)
            act.wait_ge(sem("x_loaded"), 32)
            norm_tokens(lambda i: xs[:, i, :], lambda i: xn[:, i, :], "eps_ready", (1, 1))

            def evacuate(l, n):
                name = W_IN[n][0]
                b = 2 * (n % 2)
                act.wait_ge(sem("w_used"), SPLIT_AT[("in", l, n)] + 4)
                two = PS[:, b:b + 2, :]
                if name in ("mq", "mk"):
                    return silu_conv(l, 0 if name == "mq" else 1)
                if name == "aq":
                    ins = nc.scalar.activation(aqT.rearrange("p a b -> p (a b)").rearrange("p (a b) -> p a b", a=2),
                                               two, ACT.Copy, scale=float(DH) ** -0.5)
                elif name == "ak":
                    ins = nc.scalar.activation(akT.rearrange("p a b -> p (a b)").rearrange("p (a b) -> p a b", a=2),
                                               two, ACT.Copy)
                else:
                    dst = {"av": av, "mv": mv, "mo": so}[name]
                    ins = nc.scalar.activation(dst, two, ACT.Sigmoid if name == "mo" else ACT.Copy)
                ins.then_inc(sem("in_out"), 1)

            def silu_conv(l, half):
                act.wait_ge(sem("conv_done"), 2 * l + half + 1)
                v = qk[:, 4 * half:4 * half + 4, :]
                nc.scalar.activation(v, v, ACT.Silu).then_inc(sem("qk_ready"), 1)

            def log_forget(l):
                z, t = grows[:, 1, :], grows[:, 2, :]
                act.wait_ge(sem("gate_pre"), l + 1)
                after(nc.scalar.activation(t, z, ACT.Abs))
                after(nc.scalar.activation(t, t, ACT.Exp, scale=-1.0))
                nc.scalar.activation(t, t, ACT.Ln, bias=1.0).then_inc(sem("log_done"), 1)

            def mixer(l):
                for p in [("in", l, n) for n in range(len(W_IN))]:
                    for q in range(4):
                        if q == 3 and p[2] > 0:
                            evacuate(l, p[2] - 1)
                        if q == 0 and p[2] == 3:
                            log_forget(l)
                        plan_quarter(p, q)
                evacuate(l, len(W_IN) - 1)
                act.wait_ge(sem("gate_cols_copied"), l + 1)
                nc.scalar.activation(acol[:, :, 4:8], acol[:, :, 4:8], ACT.Exp, scale=-1.0).then_inc(sem("floor_ready"), 1)
                for h in range(H):
                    n = H * l + h
                    act.wait_ge(sem("decay_logits"), n + 1)
                    if n >= 2:
                        act.wait_ge(sem("sw_done"), n - 1)
                    nc.scalar.activation(E[:, h % 2, 0:S], PS[:, h % 2, 0:S], ACT.Exp, bias=acol[:, 0, h:h + 1])
                    nc.scalar.activation(E[:, h % 2, S:384], PS[:, h % 2, S:384], ACT.Exp,
                                         bias=acol[:, 1, h:h + 1]).then_inc(sem("decay_done"), 1)
                act.wait_ge(sem("head_squares"), 2 * l + 1)
                roots[0] += 1
                root(small[:, 24:32], small[:, 16:24], roots[0], 1.0 / P)
                for h in range(H + 1):
                    if h < H:
                        n = H * l + h
                        act.wait_ge(sem("scores_max"), n + 1)
                        for cc in range(2):
                            for i in range(NT):
                                at, w = (0, P) if i == 0 else (P, S)
                                ins = nc.scalar.activation(
                                    pr[:, h % 2, cc, at:at + w], pr[:, h % 2, cc, at:at + w], ACT.Exp,
                                    bias=small[:, 32 + 4 * (h % 2) + 2 * cc + i:33 + 4 * (h % 2) + 2 * cc + i],
                                    accum_out=small[:, 40 + 4 * (h % 2) + 2 * cc + i:41 + 4 * (h % 2) + 2 * cc + i])
                        ins.then_inc(sem("exp_done"), 1)
                    if h >= 1:
                        n = H * l + h - 1
                        act.wait_ge(sem("probs_turned"), n + 1)
                        if n >= 2:
                            act.wait_ge(sem("attn_out"), n - 1)
                        nc.scalar.activation(aT[:, (h - 1) % 2, :], PS[:, 7, 0:384], ACT.Copy
                                             ).then_inc(sem("aT_ready"), 1)
                act.wait_ge(sem("attn_out"), H * (l + 1))
                for i in range(NT):
                    if i or l:
                        act.wait_ge(sem("attn_squares"), NT * l + i)
                    nc.scalar.activation(sq, PS[:, 4 + i, :], ACT.Square).then_inc(sem("attn_squared"), 1)
                act.wait_ge(sem("attn_squares"), NT * (l + 1))
                roots[0] += 1
                root(small[:, 24:32], small[:, 16:24], roots[0], 1.0 / P)
                split_turned(lambda k: mixA[:, k:k + 1], lambda k: 0.0)
                for n in range(2):
                    for q in range(4):
                        plan_quarter(("out", l, n), q)
                act.wait_ge(sem("w_used"), SPLIT_AT[("out", l, 1)] + 4)
                norm_tokens(lambda i: PS[:, 4 + 2 * i:6 + 2 * i, :], lambda i: xn[:, i, :].rearrange("p (a b) -> p a b", a=2),
                            None, None)
                norm_tokens(lambda i: xs[:, i, :], lambda i: xn[:, i, :], "x_added", (4 * l + 1, 4 * l + 2))
                split_turned(lambda k: modA[:, 1, k:k + 1], lambda k: modcol[:, 24 + k:25 + k],
                             12 * (l + 1))

            def extras(ps, q):
                for ch in range(NCH):
                    if q == LAST_Q[("gate", ch)] + SPLIT:
                        act.wait_ge(sem("w_used"), ps.split(LAST_Q[("gate", ch)]))
                        for b in range(ps.blocks):
                            ins = nc.scalar.activation(hidden[:, b, :], PS[:, ps.gate_bank(b), :], ACT.Silu)
                        ins.then_inc(sem("silu_done"), 1)
                    if q == turn_after(ch) + SPLIT:
                        act.wait_ge(sem("hidden_turned"), ps.chunk(ch))
                        for b in range(ps.blocks):
                            ins = nc.scalar.activation(sT_hi[:, :, b * P:(b + 1) * P],
                                                       PS[:, ps.up_bank(b), :].rearrange("p (a b) -> p a b", a=4), ACT.Copy)
                        ins.then_inc(sem("sT_hi_done"), 1)

            split_turned(lambda k: modA[:, 0, k:k + 1], lambda k: modcol[:, k:k + 1], 4)
            mixer(0)
            for q in range(PASS_Q):
                extras(dense, q)
                plan_quarter(("ffn", 0, q // 4), q % 4)
            act.wait_ge(sem("w_used"), dense.split(PASS_Q - 1))
            norm_tokens(lambda i: PS[:, 4 + 2 * i:6 + 2 * i, :], lambda i: xn[:, i, :].rearrange("p (a b) -> p a b", a=2),
                        None, None)
            norm_tokens(lambda i: xs[:, i, :], lambda i: xn[:, i, :], "x_added", (3, 4))
            split_turned(lambda k: modA[:, 0, k:k + 1], lambda k: modcol[:, k:k + 1], 24)
            mixer(1)
            act.wait_ge(sem("top_gap"), 1)
            nc.scalar.activation(tw[:, 2:4], tw[:, 0:2], ACT.Exp).then_inc(sem("top_exp"), 1)

            def modulate(k, n):
                if k == 0:
                    act.wait_ge(sem("gathered"), n)
                ins = nc.scalar.activation(xg[:, k * P:(k + 1) * P], PS[:, 2 + k // 4, (k % 4) * P:(k % 4 + 1) * P],
                                           ACT.Identity, bias=modcol[:, 24 + k:25 + k], scale=modA[:, 1, k:k + 1])
                if k == KT - 1:
                    ins.then_inc(sem("xg_ready"), 1)

            def expert_hi(n):
                act.wait_ge(sem("xg_ready"), n)
                nc.scalar.activation(hT_hi[:, :, 0:P], xg.rearrange("p (a b) -> p a b", a=KT), ACT.Copy
                                     ).then_inc(sem("xT_hi_done"), 1)

            def moe_round(r):
                g0 = (NE + 1) * r
                for k in range(KT):
                    modulate(k, g0 + 1)
                expert_hi(g0 + 1)
                with act.Fori(0, NE) as e:
                    ps = moe_pass(e, r)
                    for q in range(PASS_Q):
                        extras(ps, q)
                        if q == 20:
                            act.wait_ge(sem("comb_turned"), ps.expert())
                            nc.scalar.activation(combT, PS[:, 6, 0:S], ACT.Copy).then_inc(sem("combT_ready"), 1)
                        if 52 <= q < 52 + KT:
                            modulate(q - 52, e + g0 + 2)
                        if q == LAST_Q[("up", NCH - 1)] + SPLIT:
                            act.wait_ge(sem("w_used"), ps.split(LAST_Q[("up", NCH - 1)]))
                            expert_hi(e + g0 + 2)
                        hi_quarter(ps.raw_static(q), ps.split_static(q), ps.raw_round(q), ps.split(q) - SPLIT)
                    act.wait_ge(sem("w_used"), ps.split(PASS_Q - 1))
                    nc.scalar.activation(ye_sb.rearrange("p (a b) -> p a b", a=2), PS[:, 4:6, :], ACT.Copy
                                         ).then_inc(sem("ye_ready"), 1)

            moe_round(0)
            act.wait_ge(sem("flag_ready"), 1)
            over = act.value_load(flag[0:1, 0:1], min_val=0, max_val=1)
            with act.If(over > 0):
                moe_round(1)
            norm_tokens(lambda i: y_sb[:, i, :], lambda i: ye_sb, "y_complete", (1, 1))

        @block.vector
        def _(dve):
            done = [0]

            def after(ins):
                done[0] += 1
                ins.then_inc(sem("dve_step"), 1)
                dve.wait_ge(sem("dve_step"), done[0])

            def lo_quarter(r, w, hi):
                dve.wait_ge(sem("hi_ready"), hi)
                nc.vector.tensor_tensor(w_lo[:, w % SPLIT, :], raw[:, r % RAW, :], w_hi[:, w % SPLIT, :],
                                        ALU.subtract).then_inc(sem("raw_used"), 1)

            def plan_quarter(p, q):
                lo_quarter(RAW_AT[p] + q, SPLIT_AT[p] + q, SPLIT_AT[p] + q + 1)

            roots = [0]

            def invert_root(dst, src):
                roots[0] += 1
                dve.wait_ge(sem("root_done"), roots[0])
                after(nc.vector.reciprocal(dst, src))

            def normalise(first):
                for i in range(NT):
                    invert_root(small[:, 4 + i:5 + i], small[:, 2 + i:3 + i])
                    nc.vector.tensor_scalar(xn[:, i, :], xs[:, i, :], small[:, 4 + i:5 + i], None,
                                            ALU.mult).then_inc(sem("xn_ready"), 1)

            turns = [0]

            def split_turned():
                for b in range(4):
                    turns[0] += 1
                    dve.wait_ge(sem("hT_hi_done"), turns[0])
                    nc.vector.tensor_tensor(hT_lo[:, 2 * b:2 * b + 2, :], htmp[:, b % 2, :].rearrange("p (k n) -> p k n", k=2),
                                            hT_hi[:, 2 * b:2 * b + 2, :], ALU.subtract).then_inc(sem("hT_lo_done"), 1)

            def ada_sum(l, n):
                acc = acc1[:, n, :] if l else acc0[:, n % 2, :]
                if l == 0 and n >= 2:
                    dve.wait_ge(sem("ada_summed"), n - 1)
                for q in range(4):
                    r = RAW_AT[("ada", l, n)] + q
                    dve.wait_ge(sem(f"raw_loaded{r % RAW}"), 16 * (r // RAW + 1))
                    v = raw_slot(r, False)
                    for j in range(2):
                        k = 2 * q + j
                        if k == 0:
                            ins = nc.vector.tensor_scalar(acc, v[:, j, :], cact[:, k:k + 1], None, ALU.mult)
                        else:
                            ins = nc.vector.scalar_tensor_tensor(acc, v[:, j, :], cact[:, k:k + 1], acc, ALU.mult, ALU.add)
                        if j == 0:
                            after(ins)
                    ins.then_inc(sem("raw_used"), 1)
                    dve.wait_ge(sem("raw_used"), r + 1)
                nc.vector.memset(small[:, 63:64], 0.0).then_inc(sem("ada_acc"), 1)

            def ada_take(l, n):
                dve.wait_ge(sem("ada_summed"), 12 * l + n + 1)
                s = n // 2
                if s in (2, 5):
                    sub = 0 if s == 2 else 1
                    v = grow[:, sub, (n % 2) * NC:(n % 2 + 1) * NC]
                    dve.wait_ge(sem("grow_loaded"), 64 * (l + 1))
                    after(nc.vector.tensor_tensor(v, PS[:, 5, :], v, ALU.add))
                    after(nc.vector.tensor_tensor(v, v, ngb[:, sub, (n % 2) * NC:(n % 2 + 1) * NC], ALU.mult))
                else:
                    after(nc.vector.tensor_tensor(modcol[:, 4 * n:4 * n + 4], PS[:, 4, 4 * n:4 * n + 4],
                                                  colT[:, 1, 48 * l + 4 * n:48 * l + 4 * n + 4], ALU.add))
                    if n in (3, 9):
                        sub = 0 if n == 3 else 1
                        at = 8 * (4 * l + 2 * sub)
                        after(nc.vector.scalar_tensor_tensor(modA[:, sub, :], modcol[:, 8 * s:8 * s + 8], 1.0,
                                                             colT[:, 0, at:at + 8], ALU.add, ALU.mult))
                nc.vector.memset(small[:, 62:63], 0.0).then_inc(sem("ada_taken"), 1)

            def conv(l, half):
                dve.wait_ge(sem("w_used"), SPLIT_AT[("in", l, half)] + 4)
                if l == 0:
                    dve.wait_ge(sem("bias_stored"), 16)
                for tap in range(4):
                    for j in range(4):
                        n = 4 * half + j
                        psv = PS[:, 2 * half + j // 2, (j % 2) * S:(j % 2 + 1) * S]
                        wt = colT[:, 0, 64 + (4 * l + 3 - tap) * 8 + n:65 + (4 * l + 3 - tap) * 8 + n]
                        if tap == 0:
                            ins = nc.vector.tensor_scalar(qk[:, n, :], psv, wt, colT[:, 1, 96 + 8 * l + n:97 + 8 * l + n],
                                                          ALU.mult, ALU.add)
                        else:
                            ins = nc.vector.scalar_tensor_tensor(qk[:, n, tap:S], psv[:, 0:S - tap], wt, qk[:, n, tap:S],
                                                                 ALU.mult, ALU.add)
                    if tap < 3:
                        after(ins)
                ins.then_inc(sem("conv_done"), 1)

            def split_gates(n, l):
                dve.wait_ge(sem("gw_loaded"), 16 * (n + 1))
                if n:
                    dve.wait_ge(sem("gates_done"), n)
                after(nc.vector.tensor_copy(gw_hi[:], gw[:]))
                nc.vector.tensor_tensor(gw_lo[:], gw[:], gw_hi[:], ALU.subtract).then_inc(sem("gw_split"), 1)

            zi, zf, lnf, cum, a_row, run_max, stab = (grows[:, i, :] for i in (0, 1, 2, 3, 4, 5, 6))

            def gate_rows_in(l):
                dve.wait_ge(sem("gate_rows"), l + 1)
                after(nc.vector.memset(grows[:, 7, :], 1.0))
                nc.vector.tensor_scalar(zi, PS[0:H, 7, 0:S], gbias[:, 2 * l:2 * l + 1], None, ALU.add)
                nc.vector.tensor_scalar(zf, PS[0:H, 7, S:2 * S], gbias[:, 2 * l + 1:2 * l + 2], None, ALU.add
                                        ).then_inc(sem("gate_pre"), 1)

            def gate_chain(l):
                dve.wait_ge(sem("log_done"), l + 1)
                after(nc.vector.scalar_tensor_tensor(lnf, zf, 0.0, lnf, ALU.min, ALU.subtract))
                after(nc.vector.tensor_tensor_scan(cum, grows[:, 7, :], lnf, 0.0, ALU.mult, ALU.add))
                after(nc.vector.tensor_tensor(a_row, zi, cum, ALU.subtract))
                after(nc.vector.tensor_tensor_scan(run_max, a_row, a_row, 0.0, ALU.max, ALU.max))
                nc.vector.tensor_tensor(stab, cum, run_max, ALU.add)
                after(nc.vector.tensor_scalar(zi, run_max, -1.0, None, ALU.mult))
                nc.vector.memset(small[:, 61:62], 0.0).then_inc(sem("gate_ready"), 1)

            def post(l, sub, y, n):
                for i in range(NT):
                    invert_root(small[:, 4 + i:5 + i], small[:, 2 + i:3 + i])
                    after(nc.vector.scalar_tensor_tensor(ytmp.rearrange("p (a b) -> p a b", a=2), y(i), small[:, 4 + i:5 + i],
                                                         grow[:, sub, :].rearrange("p (a b) -> p a b", a=2),
                                                         ALU.mult, ALU.mult))
                    nc.vector.tensor_tensor(xs[:, i, :], xs[:, i, :], ytmp, ALU.add).then_inc(
                        sem("x_final" if n == 3 else "x_added"), 1)
                    if n < 3:
                        dve.wait_ge(sem("x_added"), NT * n + i + 1)

            def heads(v):
                return v.rearrange("p (h d) -> p h d", h=H)

            def wide(v):
                return v.unsqueeze(2).to_broadcast([P, H, P])

            def mlstm_out(l):
                dve.wait_ge(sem("mlstm_sums"), H * (l + 1))
                dve.wait_ge(sem("floor_ready"), l + 1)
                dve.wait_ge(sem("in_out"), 5 * (l + 1))
                dn = small[:, 48:56]
                after(nc.vector.tensor_copy(dn, PS[:, 6, 0:8]))
                after(nc.vector.scalar_tensor_tensor(dn, dn, -1.0, dn, ALU.mult, ALU.max))
                dn3 = dn.rearrange("p (i h) -> p i h", i=NT)
                after(nc.vector.tensor_tensor(dn3, dn3, acol[:, :, 4:8], ALU.max))
                after(nc.vector.reciprocal(dn, dn))
                for i in range(NT):
                    v = xn[:, i, NC:D]
                    after(nc.vector.tensor_tensor(heads(v), heads(PS[:, 4 + i, :]), wide(dn[:, 4 * i:4 * i + 4]), ALU.mult))
                    after(nc.vector.tensor_tensor(v, v, so[:, i, :], ALU.mult))
                    after(nc.vector.tensor_tensor(sq, v, v, ALU.mult))
                    after(nc.vector.tensor_reduce(small[:, 16 + 4 * i:20 + 4 * i], heads(sq), AX, ALU.add))
                nc.vector.memset(small[:, 60:61], 0.0).then_inc(sem("head_squares"), 1)
                invert_root(small[:, 24:32], small[:, 24:32])
                for i in range(NT):
                    v = xn[:, i, NC:D]
                    after(nc.vector.tensor_tensor(heads(v), heads(v), wide(small[:, 24 + 4 * i:28 + 4 * i]), ALU.mult))
                nc.vector.memset(small[:, 60:61], 0.0).then_inc(sem("head_squares"), 1)

            def softmax_in(l, h):
                n = H * l + h
                dve.wait_ge(sem("scores_done"), n + 1)
                if n >= 2:
                    dve.wait_ge(sem("probs_turned"), n - 1)
                pv = pr[:, h % 2, :, :]
                b = 2 * (h % 2)
                two = lambda v: v.unsqueeze(1).to_broadcast([P, 2, v.shape[1]])
                if n == 0:
                    dve.wait_ge(sem("bias_loaded"), 16 * H)
                nc.vector.tensor_tensor(pv[:, :, 0:P], PS[:, b:b + 2, 0:P], two(biasT[:, h, P:S]), ALU.add)
                after(nc.vector.tensor_tensor(pv[:, :, P:384], PS[:, b:b + 2, P:384], two(biasT[:, h, :]), ALU.add))
                at = 32 + 4 * (h % 2)
                mx = small[:, at:at + 4].rearrange("p (c i) -> p c i", c=2)
                nc.vector.tensor_reduce(mx[:, :, 0], pv[:, :, 0:P], AX, ALU.max)
                after(nc.vector.tensor_reduce(mx[:, :, 1], pv[:, :, P:384], AX, ALU.max))
                nc.vector.tensor_scalar(small[:, at:at + 4], small[:, at:at + 4], -1.0, None, ALU.mult
                                        ).then_inc(sem("scores_max"), 1)

            def softmax_mix(l, h):
                n = H * l + h
                at = 40 + 4 * (h % 2)
                dve.wait_ge(sem("exp_done"), n + 1)
                after(nc.vector.reciprocal(small[:, at:at + 4], small[:, at:at + 4]))
                after(nc.vector.tensor_scalar(small[:, at + 2:at + 4], small[:, at + 2:at + 4], lamc[:, l:l + 1], None, ALU.mult))
                for i in range(NT):
                    o, w = (0, P) if i == 0 else (P, S)
                    p0, p1 = pr[:, h % 2, 0, o:o + w], pr[:, h % 2, 1, o:o + w]
                    after(nc.vector.tensor_scalar(p1, p1, small[:, at + 2 + i:at + 3 + i], None, ALU.mult))
                    ins = nc.vector.scalar_tensor_tensor(p0, p0, small[:, at + i:at + i + 1], p1, ALU.mult, ALU.subtract)
                ins.then_inc(sem("probs_ready"), 1)

            def mixer(l):
                split_gates(l, l)
                for n in range(len(W_IN)):
                    for q in range(4):
                        if q == 3 and n in (1, 2):
                            conv(l, n - 1)
                        if q == 0 and n == 1:
                            dve.wait_ge(sem("gates_done"), l + 1)
                            nc.vector.tensor_copy(gsb[:], PS[:, 6, 0:16].rearrange("p (a b) -> p a b", a=NT)
                                                  ).then_inc(sem("gates_copied"), 1)
                        if q == 0 and n == 3:
                            gate_rows_in(l)
                        if q == 0 and n == 4:
                            gate_chain(l)
                        if l == 0 and q == 3 and n > 0:
                            ada_take(0, 4 + n - 1)
                        plan_quarter(("in", l, n), q)
                    if l == 0:
                        ada_sum(0, 4 + n)
                if l == 0:
                    ada_take(0, 10)
                    ada_sum(0, 11)
                    ada_take(0, 11)
                nc.vector.tensor_scalar(mixA[:, 0:H], colT[:, 2, 8 + l:9 + l].to_broadcast([P, H]),
                                        float(1.0 - (0.8 - 0.6 * math.exp(-0.3 * l))), None, ALU.mult)
                after(nc.vector.tensor_copy(mixA[:, H:2 * H], colT[:, 2, 10 + 4 * l:14 + 4 * l]))
                dve.wait_ge(sem("gate_cols"), l + 1)
                nc.vector.tensor_copy(acol[:], PS[:, 7, 0:16].rearrange("p (a b) -> p a b", a=NT)
                                      ).then_inc(sem("gate_cols_copied"), 1)
                for h in range(H):
                    n = H * l + h
                    dve.wait_ge(sem("decay_done"), n + 1)
                    dve.wait_ge(sem("mqk_done"), n + 1)
                    if n >= 2:
                        dve.wait_ge(sem("mlstm_sums"), n - 1)
                    nc.vector.scalar_tensor_tensor(Sw[:, h % 2, :], PS[:, 2 + h % 2, 0:384], float(P) ** -0.5,
                                                   E[:, h % 2, :], ALU.mult, ALU.mult).then_inc(sem("sw_done"), 1)
                mlstm_out(l)
                for h in range(H + 1):
                    if h < H:
                        softmax_in(l, h)
                    if h >= 1:
                        softmax_mix(l, h - 1)
                for i in range(NT):
                    dve.wait_ge(sem("attn_squared"), NT * l + i + 1)
                    nc.vector.tensor_reduce(small[:, 16 + 4 * i:20 + 4 * i], heads(sq), AX, ALU.add
                                            ).then_inc(sem("attn_squares"), 1)
                invert_root(small[:, 24:32], small[:, 24:32])
                for i in range(NT):
                    nc.vector.tensor_tensor(heads(xn[:, i, 0:NC]), heads(PS[:, 4 + i, :]),
                                            wide(small[:, 24 + 4 * i:28 + 4 * i]), ALU.mult).then_inc(sem("mixed_ready"), 1)
                split_turned()
                for n in range(2):
                    for q in range(4):
                        plan_quarter(("out", l, n), q)
                post(l, 0, lambda i: PS[:, 4 + 2 * i:6 + 2 * i, :], 2 * l)
                normalise(False)
                split_turned()

            def extras(ps, q):
                for ch in range(NCH):
                    if q == LAST_Q[("up", ch)] + SPLIT:
                        dve.wait_ge(sem("w_used"), ps.split(LAST_Q[("up", ch)]))
                        dve.wait_ge(sem("silu_done"), ps.chunk(ch))
                        for b in range(ps.blocks):
                            ins = nc.vector.tensor_tensor(hidden[:, b, :], PS[:, ps.up_bank(b), :], hidden[:, b, :], ALU.mult)
                        ins.then_inc(sem("hidden_ready"), 1)
                    if q == turn_after(ch) + SPLIT:
                        dve.wait_ge(sem("sT_hi_done"), ps.chunk(ch))
                        for b in range(ps.blocks):
                            ins = nc.vector.tensor_tensor(sT_lo[:, :, b * P:(b + 1) * P],
                                                          PS[:, ps.up_bank(b), :].rearrange("p (a b) -> p a b", a=4),
                                                          sT_hi[:, :, b * P:(b + 1) * P], ALU.subtract)
                        ins.then_inc(sem("sT_lo_done"), 1)

            nc.vector.memset(eps[:], EPS).then_inc(sem("eps_ready"), 1)
            nc.vector.memset(relb[32:33, :, :], 1.0)
            dve.wait_ge(sem("rel_loaded"), 16)
            nc.vector.tensor_copy(relb[0:N_BUCKETS, :, :],
                                  lamc[0:N_BUCKETS, 4:4 + H].unsqueeze(2).to_broadcast([N_BUCKETS, H, P])
                                  ).then_inc(sem("relb_ready"), 1)
            dve.wait_ge(sem("lam_loaded"), 16)
            lv = lamrow.rearrange("p (a b) d -> p a b d", b=2)
            after(nc.vector.tensor_tensor(lamp, lv[:, :, 0, :], lv[:, :, 1, :], ALU.mult))
            nc.vector.tensor_reduce(small[:, 8:12], lamp, AX, ALU.add).then_inc(sem("lam_sums"), 1)
            normalise(True)
            dve.wait_ge(sem("cact_ready"), 1)
            for n in range(4):
                ada_sum(0, n)
                if n:
                    ada_take(0, n - 1)
            ada_take(0, 3)
            dve.wait_ge(sem("lam_exp"), 1)
            for l in range(L):
                lam_init = 0.8 - 0.6 * math.exp(-0.3 * l)
                after(nc.vector.scalar_tensor_tensor(lamc[:, 4 + l:5 + l], lamc[:, 2 * l:2 * l + 1], float(lam_init),
                                                     lamc[:, 2 * l + 1:2 * l + 2], ALU.add, ALU.subtract))
            after(nc.vector.tensor_copy(lamc[:, 0:2], lamc[:, 4:6]))
            split_turned()
            nc.vector.memset(small[:, 59:60], 0.0).then_inc(sem("post_done"), 1)
            mixer(0)
            nxt = 0
            for g in range(len(GROUPS)):
                for q in range(4):
                    extras(dense, 4 * g + q)
                    plan_quarter(("ffn", 0, g), q)
                if g % 7 in (0, 2, 4, 6):
                    ada_sum(1, nxt)
                    nxt += 1
            post(0, 1, lambda i: PS[:, 4 + 2 * i:6 + 2 * i, :], 1)
            nc.vector.memset(small[:, 59:60], 0.0).then_inc(sem("post_done"), 1)
            for n in range(12):
                ada_take(1, n)
            normalise(False)
            split_turned()
            mixer(1)

            split_gates(2, None)
            dve.wait_ge(sem("gates_done"), 3)
            nc.vector.memset(routing[:, 0:54], 0.0)
            after(nc.vector.tensor_copy(lg, PS[:, 6, 0:16].rearrange("p (a b) -> p a b", a=NT)))
            for i in range(NT):
                after(nc.vector.max(top[:, i, :], lg[:, i, :]))
                after(nc.vector.max_index(midx[:, i, :], top[:, i, :], lg[:, i, :]))
            after(nc.vector.tensor_copy(topi, midx[:]))
            nc.vector.tensor_tensor(tw[:, 0:2], top[:, :, 1], top[:, :, 0], ALU.subtract).then_inc(sem("top_gap"), 1)
            for n in range(2):
                for i in range(NT):
                    ins = nc.vector.tensor_scalar(pick[:, n, i, :], iota[:, 0:NE], topi[:, i, n:n + 1], None, ALU.is_equal)
            after(ins)
            nc.vector.tensor_tensor(sel[:, :, 0:NE], pick[:, 0], pick[:, 1], ALU.add).then_inc(sem("sel_ready"), 1)
            dve.wait_ge(sem("top_exp"), 1)
            after(nc.vector.tensor_scalar(tw[:, 4:6], tw[:, 2:4], 1.0, None, ALU.add))
            after(nc.vector.reciprocal(tw[:, 6:8], tw[:, 4:6]))
            after(nc.vector.tensor_tensor(tw[:, 8:10], tw[:, 6:8], tw[:, 2:4], ALU.mult))
            for i in range(NT):
                after(nc.vector.tensor_scalar(gates[:, i, 0:NE], pick[:, 1, i, :], tw[:, 8 + i:9 + i], None, ALU.mult))
                after(nc.vector.scalar_tensor_tensor(gates[:, i, 0:NE], pick[:, 0, i, :], tw[:, 6 + i:7 + i],
                                                     gates[:, i, 0:NE], ALU.mult, ALU.add))
            dve.wait_ge(sem("ranks_done"), 1)
            after(nc.vector.tensor_copy(ranks[:, :, 0:NE], PS[:, 6, 16:32].rearrange("p (a b) -> p a b", a=NT)))
            after(nc.vector.tensor_reduce(tw[:, 10:11], PS[:, 6, 32:40], AX, ALU.max))
            after(nc.vector.tensor_scalar(tw[:, 11:12], tw[:, 10:11], float(P), None, ALU.is_gt))
            nc.vector.tensor_copy(flag[:], tw[:, 11:12]).then_inc(sem("flag_ready"), 1)
            after(nc.vector.memset(y_sb, 0.0))

            def onehots(dst, weight, col):
                for i in range(NT):
                    ins = nc.vector.tensor_scalar(dst[:, i, :], iota, ranks[:, i, col], weight[:, i, col],
                                                  ALU.is_equal, ALU.mult)
                return ins

            def expert_lo(n):
                dve.wait_ge(sem("xT_hi_done"), n)
                nc.vector.tensor_tensor(hT_lo[:, :, 0:P], xg.rearrange("p (a b) -> p a b", a=KT), hT_hi[:, :, 0:P],
                                        ALU.subtract).then_inc(sem("xT_ready"), 1)

            def add_scattered(n, m):
                dve.wait_ge(sem("scattered"), n)
                nc.vector.tensor_tensor(y_sb[:, 0, :].rearrange("p (a b) -> p a b", a=2), PS[:, 6:8, :],
                                        y_sb[:, 0, :].rearrange("p (a b) -> p a b", a=2), ALU.add)
                nc.vector.tensor_tensor(y_sb[:, 1, :].rearrange("p (a b) -> p a b", a=2), PS[:, 2:4, :],
                                        y_sb[:, 1, :].rearrange("p (a b) -> p a b", a=2), ALU.add).then_inc(sem("y_added"), 1)
                dve.wait_ge(sem("y_added"), m)

            def moe_round(r):
                g0 = (NE + 1) * r
                if r:
                    nc.vector.tensor_scalar(ranks, ranks, -float(P), None, ALU.add).then_inc(sem("ranks_moved"), 1)
                    dve.wait_ge(sem("ranks_moved"), 1)
                nc.vector.memset(combT, 0.0)
                nc.vector.memset(ye_sb, 0.0).then_inc(sem("zeros_ready"), 1)
                onehots(disp, sel, slice(0, 1)).then_inc(sem("disp_ready"), 1)
                expert_lo(g0 + 1)
                with dve.Fori(0, NE) as e:
                    ps = moe_pass(e, r)
                    for q in range(PASS_Q):
                        extras(ps, q)
                        if q == 2:
                            add_scattered(e + g0 + 1, e + g0 + 1)
                        if q == 4:
                            onehots(comb, gates, bass.ds(e, 1)).then_inc(sem("comb_ready"), 1)
                        if q == 36:
                            onehots(disp, sel, bass.ds(e + 1, 1)).then_inc(sem("disp_ready"), 1)
                        if q == LAST_Q[("up", NCH - 1)] + SPLIT:
                            expert_lo(e + g0 + 2)
                        lo_quarter(ps.raw_static(q), ps.split_static(q), ps.split(q))
                add_scattered(g0 + NE + 1, g0 + NE + 1)

            moe_round(0)
            over = dve.value_load(flag[0:1, 0:1], min_val=0, max_val=1)
            with dve.If(over > 0):
                moe_round(1)
            nc.vector.memset(small[:, 58:59], 0.0).then_inc(sem("y_complete"), 1)
            post(1, 1, lambda i: y_sb[:, i, :].rearrange("p (a b) -> p a b", a=2), 3)

        @block.tensor
        def _(pe):
            def three(dst, a_hi, a_lo, b_hi, b_lo, start, stop):
                nc.tensor.matmul(dst, a_hi, b_hi, start=start, stop=False, skip_group_check=True)
                nc.tensor.matmul(dst, a_hi, b_lo, start=False, stop=False, skip_group_check=True)
                return nc.tensor.matmul(dst, a_lo, b_hi, start=False, stop=stop, skip_group_check=True)

            def mm(dst, a, b, start=True, stop=True):
                return nc.tensor.matmul(dst, a, b, start=start, stop=stop, skip_group_check=True)

            def split_view(w):
                return (w_hi[:, w % SPLIT, :].rearrange("p (k n) -> p k n", k=2),
                        w_lo[:, w % SPLIT, :].rearrange("p (k n) -> p k n", k=2))

            turned = [0]

            def turn(src_sem, counts):
                for i in range(NT):
                    pe.wait_ge(sem(src_sem), counts[i])
                if turned[0]:
                    pe.wait_ge(sem("hT_lo_done"), turned[0])
                for b in range(4):
                    for j in range(2):
                        for i in range(NT):
                            k = 2 * b + j
                            ins = nc.tensor.transpose(PS[:, b, j * S + i * P:j * S + (i + 1) * P],
                                                      xn[:, i, k * P:(k + 1) * P], ident)
                    ins.then_inc(sem("turned"), 1)
                    turned[0] += 1

            def split_ready():
                pe.wait_ge(sem("hT_lo_done"), turned[0])

            def ada_columns(l, n):
                pe.wait_ge(sem("ada_acc"), 12 * l + n + 1)
                acc = acc1[:, n, :] if l else acc0[:, n % 2, :]
                before_it = 12 * l + n
                if before_it:
                    pe.wait_ge(sem("ada_taken"), before_it)
                if n // 2 in (2, 5):
                    mm(PS[:, 5, :], ones, acc).then_inc(sem("ada_summed"), 1)
                else:
                    for j in range(4):
                        ins = mm(PS[:, 4, 4 * n + j:4 * n + j + 1], acc[:, j * P:(j + 1) * P], ones[:, 0:1])
                    ins.then_inc(sem("ada_summed"), 1)

            def small_columns(l):
                pe.wait_ge(sem("gw_split"), l + 1)
                for i in range(NT):
                    for k in range(KT):
                        ins = three(PS[:, 6, 8 * i:8 * i + 8], hT_hi[:, k, i * P:(i + 1) * P], hT_lo[:, k, i * P:(i + 1) * P],
                                    gw_hi[:, k, :], gw_lo[:, k, :], k == 0, k == KT - 1)
                ins.then_inc(sem("gates_done"), 1)

            def token_quarter(w, q, banks):
                hi, lo = split_view(w)
                for i in range(NT):
                    for j in range(2):
                        k = 2 * q + j
                        ins = three(PS[:, banks[i], :], hT_hi[:, k, i * P:(i + 1) * P], hT_lo[:, k, i * P:(i + 1) * P],
                                    hi[:, j, :], lo[:, j, :], k == 0, k == KT - 1)
                return ins

            def feature_quarter(w, q, b):
                hi, lo = split_view(w)
                for j in range(2):
                    k = 2 * q + j
                    for f in range(4):
                        ins = three(PS[:, b + f // 2, (f % 2) * S:(f % 2 + 1) * S], hi[:, j, f * P:(f + 1) * P],
                                    lo[:, j, f * P:(f + 1) * P], hT_hi[:, k, :], hT_lo[:, k, :],
                                    k == 0 and f % 2 == 0, k == KT - 1)
                return ins

            def piece_free(l, n):
                if n < 2:
                    return
                m = n - 2
                if m < 2:
                    pe.wait_ge(sem("conv_done"), 2 * l + m + 1)
                else:
                    pe.wait_ge(sem("in_out"), 5 * l + m - 1)

            def mixer(l):
                split_ready()
                small_columns(l)
                for n, (name, _) in enumerate(W_IN):
                    piece_free(l, n)
                    b = 2 * (n % 2)
                    for q in range(4):
                        w = SPLIT_AT[("in", l, n)] + q
                        pe.wait_ge(sem("raw_used"), RAW_AT[("in", l, n)] + q + 1)
                        if name in FEATURE_MAJOR:
                            ins = feature_quarter(w, q, b)
                        else:
                            ins = token_quarter(w, q, (b, b + 1))
                        ins.then_inc(sem("w_used"), 1)
                    if n == 1:
                        pe.wait_ge(sem("gates_copied"), l + 1)
                        for t in range(2):
                            for i in range(NT):
                                ins = nc.tensor.transpose(PS[0:H, 7, t * S + i * P:t * S + (i + 1) * P],
                                                          gsb[:, i, 4 * t:4 * t + 4], ident)
                        ins.then_inc(sem("gate_rows"), 1)
                    if l == 0:
                        ada_columns(0, 4 + n)
                if l == 0:
                    ada_columns(0, 11)
                pe.wait_ge(sem("gate_ready"), l + 1)
                for i in range(NT):
                    mm(PS[:, 7, 8 * i:8 * i + 4], grows[:, 4, i * P:(i + 1) * P], ident[0:H, 0:H])
                    ins = mm(PS[:, 7, 8 * i + 4:8 * i + 8], grows[:, 6, i * P:(i + 1) * P], ident[0:H, 0:H])
                ins.then_inc(sem("gate_cols"), 1)
                pe.wait_ge(sem("in_out"), 5 * (l + 1))
                pe.wait_ge(sem("qk_ready"), 2 * (l + 1))
                for h in range(H + 1):
                    if h < H:
                        n = H * l + h
                        if h >= 2:
                            pe.wait_ge(sem("decay_done"), n - 1)
                            pe.wait_ge(sem("sw_done"), n - 1)
                        nm = grows[:, 0, :]
                        hs = headsel[:, h * P:(h + 1) * P]
                        mm(PS[:, h % 2, 0:S], hs, nm, True, False)
                        mm(PS[:, h % 2, 0:P], ident, negm, False, True)
                        mm(PS[:, h % 2, S:384], hs, nm[:, P:S], False, False)
                        mm(PS[:, h % 2, S:384], ident, negm, False, True).then_inc(sem("decay_logits"), 1)
                        mm(PS[:, 2 + h % 2, 0:S], qk[:, H + h, 0:P], qk[:, h, :])
                        mm(PS[:, 2 + h % 2, S:384], qk[:, H + h, P:S], qk[:, h, P:S]).then_inc(sem("mqk_done"), 1)
                    if h >= 1:
                        g = h - 1
                        pe.wait_ge(sem("sw_done"), H * l + g + 1)
                        s = Sw[:, g % 2, :]
                        vh = lambda i: mv[:, i, g * P:(g + 1) * P]
                        for i in range(NT):
                            for kind in range(2):
                                dst = PS[:, 4 + i, g * P:(g + 1) * P] if kind == 0 else PS[:, 6, 4 * i + g:4 * i + g + 1]
                                rhs = vh if kind == 0 else (lambda _: ones[:, 0:1])
                                if i == 0:
                                    ins = mm(dst, s[:, 0:P], rhs(0))
                                else:
                                    mm(dst, s[:, P:S], rhs(0), True, False)
                                    ins = mm(dst, s[:, S:384], rhs(1), False, True)
                        ins.then_inc(sem("mlstm_sums"), 1)
                for h in range(H + 1):
                    if h < H:
                        n = H * l + h
                        if h >= 2:
                            pe.wait_ge(sem("scores_max"), n - 1)
                        for cc in range(2):
                            b = 2 * (h % 2) + cc
                            a = slice(cc * DH, (cc + 1) * DH)
                            mm(PS[:, b, 0:P], aqT[a, h, 0:P], akT[a, h, 0:P])
                            ins = mm(PS[:, b, P:384], aqT[a, h, P:S], akT[a, h, :])
                        ins.then_inc(sem("scores_done"), 1)
                    if h >= 1:
                        g = h - 1
                        n = H * l + g
                        pe.wait_ge(sem("probs_ready"), n + 1)
                        if g >= 1:
                            pe.wait_ge(sem("aT_ready"), n)
                        for j in range(3):
                            ins = nc.tensor.transpose(PS[:, 7, j * P:(j + 1) * P], pr[:, g % 2, 0, j * P:(j + 1) * P], ident)
                        ins.then_inc(sem("probs_turned"), 1)
                        pe.wait_ge(sem("aT_ready"), n + 1)
                        if g == 0:
                            pe.wait_ge(sem("head_squares"), 2 * l + 2)
                        vh = lambda i: av[:, i, g * P:(g + 1) * P]
                        mm(PS[:, 4, g * P:(g + 1) * P], aT[:, g % 2, 0:P], vh(0))
                        mm(PS[:, 5, g * P:(g + 1) * P], aT[:, g % 2, P:S], vh(0), True, False)
                        mm(PS[:, 5, g * P:(g + 1) * P], aT[:, g % 2, S:384], vh(1), False, True
                           ).then_inc(sem("attn_out"), 1)
                turn("mixed_ready", (NT * l + 1, NT * l + 2))
                split_ready()
                for n in range(2):
                    for q in range(4):
                        w = SPLIT_AT[("out", l, n)] + q
                        pe.wait_ge(sem("raw_used"), RAW_AT[("out", l, n)] + q + 1)
                        token_quarter(w, q, (4 + n, 6 + n)).then_inc(sem("w_used"), 1)
                turn("xn_ready", (4 * l + 3, 4 * l + 4))
                split_ready()

            def hidden_quarter(ps, q):
                what, ch = GROUPS[q // 4]
                qq = q % 4
                w = ps.split_static(q)
                pe.wait_ge(sem("raw_used"), ps.raw(q))
                if qq == 0 and what == "up" and ch > 0:
                    pe.wait_ge(sem("sT_lo_done"), ps.chunk(ch - 1))
                if qq == 0 and what == "down" and ch == NCH - 1:
                    pe.wait_ge(sem("sT_lo_done"), ps.chunk(ch))
                if what == "down":
                    for b in range(ps.blocks):
                        for n in range(2):
                            ins = three(PS[:, 4 + 2 * b + n, :], sT_hi[:, qq, b * P:(b + 1) * P], sT_lo[:, qq, b * P:(b + 1) * P],
                                        w_hi[:, w % SPLIT, n * NC:(n + 1) * NC], w_lo[:, w % SPLIT, n * NC:(n + 1) * NC],
                                        ch == 0 and qq == 0, ch == NCH - 1 and qq == 3)
                else:
                    hi, lo = split_view(w)
                    for b in range(ps.blocks):
                        bank = ps.gate_bank(b) if what == "gate" else ps.up_bank(b)
                        for j in range(2):
                            k = 2 * qq + j
                            ins = three(PS[:, bank, :], hT_hi[:, k, b * P:(b + 1) * P], hT_lo[:, k, b * P:(b + 1) * P],
                                        hi[:, j, :], lo[:, j, :], k == 0, k == KT - 1)
                ins.then_inc(sem("w_used"), 1)
                for c2 in range(NCH):
                    if q == turn_after(c2):
                        pe.wait_ge(sem("hidden_ready"), ps.chunk(c2))
                        for b in range(ps.blocks):
                            for f in range(4):
                                ins = nc.tensor.transpose(PS[:, ps.up_bank(b), f * P:(f + 1) * P],
                                                          hidden[:, b, f * P:(f + 1) * P], ident)
                        ins.then_inc(sem("hidden_turned"), 1)

            pe.wait_ge(sem("tables_loaded"), 16)
            pe.wait_ge(sem("rows_loaded"), 16 * 7)
            for t, n in ((0, 128), (1, 112), (2, 18)):
                ins = nc.tensor.transpose(PS[:, 4, t * P:t * P + n], tabs[0:n, t, :], ident[0:n, 0:n])
            ins.then_inc(sem("cols_turned"), 1)
            pe.wait_ge(sem("relb_ready"), 1)
            for h in range(H):
                ins = mm(PS[:, h, 0:384], relb[:, h, :], onehot)
            ins.then_inc(sem("bias_rows"), 1)
            pe.wait_ge(sem("bias_rows_copied"), 1)
            turn("xn_ready", (1, 2))
            for n in range(4):
                ada_columns(0, n)
            mixer(0)
            for q in range(PASS_Q):
                hidden_quarter(dense, q)
            pe.wait_ge(sem("x_added"), 4)
            for n in range(12):
                ada_columns(1, n)
            turn("xn_ready", (5, 6))
            mixer(1)
            small_columns(2)
            pe.wait_ge(sem("sel_ready"), 1)
            mm(PS[:, 6, 16:24], before, sel[:, 0, 0:NE])
            mm(PS[:, 6, 24:32], ones, sel[:, 0, 0:NE], True, False)
            mm(PS[:, 6, 24:32], before, sel[:, 1, 0:NE], False, True)
            mm(PS[:, 6, 32:40], ones, sel[:, 0, 0:NE], True, False)
            mm(PS[:, 6, 32:40], ones, sel[:, 1, 0:NE], False, True).then_inc(sem("ranks_done"), 1)

            def gather():
                for k in range(KT):
                    for i in range(NT):
                        ins = mm(PS[:, 2 + k // 4, (k % 4) * P:(k % 4 + 1) * P], xn[:, i, k * P:(k + 1) * P], disp[:, i, :],
                                 k % 4 == 0 and i == 0, i == NT - 1)
                ins.then_inc(sem("gathered"), 1)

            def scatter():
                for i in range(NT):
                    for n in range(2):
                        ins = mm(PS[:, (6 if i == 0 else 2) + n, :], combT[:, i * P:(i + 1) * P], ye_sb[:, n * NC:(n + 1) * NC])
                ins.then_inc(sem("scattered"), 1)

            def moe_round(r):
                g0 = (NE + 1) * r
                if r:
                    pe.wait_ge(sem("y_added"), g0)
                pe.wait_ge(sem("disp_ready"), g0 + 1)
                gather()
                pe.wait_ge(sem("xg_ready"), g0 + 1)
                pe.wait_ge(sem("zeros_ready"), r + 1)
                scatter()
                with pe.Fori(0, NE) as e:
                    ps = moe_pass(e, r)
                    pe.wait_ge(sem("xT_ready"), e + g0 + 1)
                    for q in range(PASS_Q):
                        if q == 12:
                            pe.wait_ge(sem("comb_ready"), ps.expert())
                            pe.wait_ge(sem("y_added"), e + g0 + 1)
                            for i in range(NT):
                                ins = nc.tensor.transpose(PS[:, 6, i * P:(i + 1) * P], comb[:, i, :], ident)
                            ins.then_inc(sem("comb_turned"), 1)
                        if q == 48:
                            pe.wait_ge(sem("disp_ready"), e + g0 + 2)
                            gather()
                        hidden_quarter(ps, q)
                    pe.wait_ge(sem("ye_ready"), ps.expert())
                    pe.wait_ge(sem("combT_ready"), ps.expert())
                    pe.wait_ge(sem("xg_ready"), e + g0 + 2)
                    scatter()

            moe_round(0)
            pe.wait_ge(sem("flag_ready"), 1)
            over = pe.value_load(flag[0:1, 0:1], min_val=0, max_val=1)
            with pe.If(over > 0):
                moe_round(1)
            pe.wait_ge(sem("y_complete"), 1)


_INS = ["x", "c", "rel_bias", "ada_w", "ada_b", "norm_g", "w_in", "gate_b", "conv_w", "conv_b", "lam_vec",
        "attn_norm_g", "mlstm_norm_g", "w_out", "ffn_w1", "ffn_w3", "ffn_w2", "router_w", "moe_w1", "moe_w3", "moe_w2"]


def kernel(**inputs):
    import concourse.bacc as bacc
    from concourse.bass_utils import run_bass_kernel_spmd

    nc = bacc.Bacc("TRN2", target_bir_lowering=False, num_devices=1)
    arrays, args = {}, []
    for name in _INS + ["tables"]:
        a = shape_constants() if name == "tables" else np.ascontiguousarray(inputs[name])
        arrays[f"in_{name}"] = a
        args.append(nc.dram_tensor(f"in_{name}", a.shape, mybir.dt.from_np(a.dtype), kind="ExternalInput").ap())
    args.append(nc.dram_tensor("out_0", (1, S, D), F32, kind="ExternalOutput").ap())
    trunk(nc, *args)
    r = run_bass_kernel_spmd(nc, [arrays], core_ids=[0])
    return r.results[0]["out_0"]
```

```python
import math
from contextlib import ExitStack

import numpy as np
import concourse.bass as bass
from concourse import mybir

F32 = mybir.dt.float32
F32R = mybir.dt.float32r
I32 = mybir.dt.int32
U32 = mybir.dt.uint32
ACT = mybir.ActivationFunctionType
ALU = mybir.AluOpType
AX = mybir.AxisListType.X

P = 128
S = 256
NT = S // P
D = 1024
KT = D // P
L = 2
H = 4
DH = 64
DFF = 3584
NE = 8
NC = 512
NCH = DFF // NC
N_BUCKETS, MAX_DIST = 32, 128
EPS = 1e-6
NEG = -1e30

RAW = 14
MOE_RAW = 21
SPLIT = 4
QW = 1024

GROUPS = [("gate", 0), ("up", 0)]
for _c in range(1, NCH):
    GROUPS += [("gate", _c), ("up", _c), ("down", _c - 1)]
GROUPS += [("down", NCH - 1)]
PASS_Q = 4 * len(GROUPS)
LAST_Q = {g: 4 * i + 3 for i, g in enumerate(GROUPS)}
assert PASS_Q % MOE_RAW == 0 and PASS_Q % SPLIT == 0


def turn_after(c):
    return LAST_Q[("gate", 1)] if c == 0 else LAST_Q[("down", c - 1)]


W_IN = [("mq", 1536), ("mk", 2048), ("mv", 2560), ("mo", 3072), ("aq", 0), ("ak", 512), ("av", 1024)]
GATE_COL = 3584
FEATURE_MAJOR = ("mq", "mk", "aq", "ak")

AHEAD = SPLIT - 1

DECAY_AT = (1, 3, 5, 7)

ADA_BESIDE = {1: 4, 4: 5, 5: 6}
POOL_ADA = (7, 8, 9)
ADA_ORDER = [0, 1, 2, 3, 4, 7, 8, 9, 6, 5]
ADA_EARLY = 5
LATE_ADA = [(0, 10), (0, 11)] + [(1, n) for n in range(12)]
LATE_POOL = LATE_ADA[8:]
LATE_AFTER = (0, 2, 5, 7, 10, 12, 15, 17)
TURNS = 4 * 6


def plan():
    late = iter(LATE_ADA)
    for n in range(4):
        for q in range(4):
            yield ("ada", 0, n), q
    for l in range(L):
        for n in range(len(W_IN)):
            for q in range(4):
                if l == 0 and n in ADA_BESIDE:
                    yield ("ada", 0, ADA_BESIDE[n]), q
                yield ("in", l, n), q
        for n in range(2):
            for q in range(4):
                yield ("out", l, n), q
        if l == 0:
            for i in range(len(GROUPS)):
                for q in range(4):
                    yield ("ffn", 0, i), q
                if i in LATE_AFTER:
                    p = ("ada", *next(late))
                    for q in range(4):
                        yield p, q


PLAN = list(plan())
RAW_AT, SPLIT_AT = {}, {}
for _p, _q in PLAN:
    RAW_AT[_p, _q] = len(RAW_AT)
    if _p[0] != "ada":
        SPLIT_AT[_p, _q] = len(SPLIT_AT)
RAW_MOE, SPLIT_MOE = len(RAW_AT), len(SPLIT_AT)


def shape_constants():
    k = np.zeros((P, 1536), np.float32)
    p = np.arange(P)
    k[:, 0:128] = np.eye(P)
    k[:, 128:256] = np.where(p[:, None] > p[None, :], NEG, 0.0)
    k[:, 256:384] = (p[:, None] < p[None, :])
    k[:, 384:512] = p[None, :]
    k[:, 512:640] = 1.0
    dist = 255 - np.arange(384)
    n = np.maximum(dist, 0)
    exact = N_BUCKETS // 2
    nf = np.maximum(n, 1).astype(np.float32)
    large = exact + (np.log(nf / np.float32(exact)) / np.float32(math.log(MAX_DIST / exact))
                     * np.float32(N_BUCKETS - exact)).astype(np.int32)
    bucket = np.where(n < exact, n, np.minimum(large, N_BUCKETS - 1))
    for j in range(384):
        if dist[j] >= 0:
            k[bucket[j], 640 + j] = 1.0
        else:
            k[N_BUCKETS, 640 + j] = NEG
    for h in range(H):
        k[h, 1024 + h * P:1024 + (h + 1) * P] = 1.0
    return k


def trunk(nc, x, c, rel_bias, ada_w, ada_b, norm_g, w_in, gate_b, conv_w, conv_b, lam_vec, attn_norm_g,
          mlstm_norm_g, w_out, ffn_w1, ffn_w3, ffn_w2, router_w, moe_w1, moe_w3, moe_w2, tables, out):
    with ExitStack() as ctx:
        def sb(name, shape, dt=F32):
            return ctx.enter_context(nc.sbuf_tensor(name, shape, dt))

        sems = {}

        def sem(name):
            if name not in sems:
                sems[name] = ctx.enter_context(nc.semaphore(name))
            return sems[name]

        raw = sb("raw", [P, RAW, QW])
        w_hi = sb("w_hi", [P, SPLIT, QW], F32R)
        w_lo = sb("w_lo", [P, SPLIT, QW], F32R)
        hT_hi = sb("hT_hi", [P, KT, S], F32R)
        hT_lo = sb("hT_lo", [P, KT, S], F32R)
        sT_hi = sb("sT_hi", [P, 4, S], F32R)
        sT_lo = sb("sT_lo", [P, 4, S], F32R)
        xs = sb("xs", [P, NT, D])
        xn = sb("xn", [P, NT, D])
        K = sb("K", [P, 1536])
        grow = sb("grow", [P, 3, D])
        biasT = sb("biasT", [P, H, S])
        colT = sb("colT", [P, 3, P])
        cact = sb("cact", [P, KT])
        cT = sb("cT", [P, KT])
        modcol = sb("modcol", [P, 48])
        modA = sb("modA", [P, 2, KT])
        mixA = sb("mixA", [P, KT])
        gw = sb("gw", [P, KT, 8])
        gw_hi = sb("gw_hi", [P, KT, 8], F32R)
        gw_lo = sb("gw_lo", [P, KT, 8], F32R)
        gbias = sb("gbias", [H, 4])
        lamc = sb("lamc", [P, 8])
        eps = sb("eps", [P, 1])
        small = sb("small", [P, 64])
        att = sb("att", [P, H, 8])
        area = sb("area", [P, 13568])

        ident, negm, before, iota, ones = (K[:, i * P:(i + 1) * P] for i in range(5))
        onehot = K[0:N_BUCKETS + 1, 640:1024]
        headsel = K[0:H, 1024:1536]

        def part(at, *shape):
            n = int(np.prod(shape))
            v = area[:, at:at + n]
            if len(shape) == 2:
                v = v.rearrange("p (a b) -> p a b", a=shape[0])
            if len(shape) == 3:
                v = v.rearrange("p (a b c) -> p a b c", a=shape[0], b=shape[1])
            return v

        qk = part(0, 2 * H, S)
        aqT, akT = part(2048, H, S), part(3072, H, S)
        av, mv, so = part(4096, NT, NC), part(5120, NT, NC), part(6144, NT, NC)
        E = part(7168, 384)
        Sw = part(7552, 384)
        sq = part(7168, NC)
        sqh = part(7680, P)
        pr = part(8960, 2, 2, 384)
        aT = part(10496, 2, 384)
        grows = area[0:H, 8960:8960 + 8 * S].rearrange("p (a b) -> p a b", a=8)
        hidden = part(7168, NT, NC)
        htmp = part(5120, 2, NC)
        acc0 = part(4096, 2, NC)
        acc56 = grow[:, 1, :].rearrange("p (a b) -> p a b", a=2)
        accp = [grow[:, 2, 0:NC], grow[:, 2, NC:D], part(7936, NC)]
        acc1 = part(0, len(LATE_ADA), NC)
        pool_w = part(11264, 2, NC)
        ytmp0 = part(6144, D)
        ytmp1 = part(8192, D)
        ngb = part(9216, 4, D)
        tabs = part(9216, 3, P)
        lamrow = part(9728, 8, DH)
        brows = part(0, H, 384)
        relb = area[0:N_BUCKETS + 1, 2048:2560].rearrange("p (a b) -> p a b", a=H)
        lamp = part(2560, 4, DH)
        y_sb = part(0, NT, D)
        ye_sb = part(2048, D)
        xg = part(3072, D)
        disp = part(4096, NT, P)
        comb = part(4352, NT, P)
        combT = part(4608, S)
        lgT = area[0:NE, 4096:4096 + S]
        routing = sb("routing", [P, 160])
        midx = sb("midx", [P, NT, 8], U32)
        flag = sb("flag", [P, 1], I32)
        ranks = routing[:, 0:18].rearrange("p (a b) -> p a b", a=NT)
        sel = routing[:, 18:36].rearrange("p (a b) -> p a b", a=NT)
        gates = routing[:, 36:54].rearrange("p (a b) -> p a b", a=NT)
        lg = routing[:, 54:70].rearrange("p (a b) -> p a b", a=NT)
        top = routing[:, 70:86].rearrange("p (a b) -> p a b", a=NT)
        topi = routing[:, 86:102].rearrange("p (a b) -> p a b", a=NT)
        pick = routing[:, 102:134].rearrange("p (n a b) -> p n a b", n=2, a=NT)
        tw = routing[:, 134:150]
        acol = sb("acol", [P, NT, 8])
        mstat = sb("mstat", [P, 24])
        dn, msq, mroot = mstat[:, 0:8], mstat[:, 8:16], mstat[:, 16:24]

        PS = ctx.enter_context(nc.psum_tensor("PS", [P, 8, 512], F32))
        scratch = nc.dram_tensor("bias_rows_dram", [H, P, 384], F32)

        def source(p, q):
            kind, l, n = p
            if kind == "ada":
                return ada_w[l].rearrange("(k p) n -> p k n", p=P)[:, 2 * q:2 * q + 2, n * NC:(n + 1) * NC]
            if kind == "in":
                at = W_IN[n][1]
                return w_in[l].rearrange("(k p) n -> p k n", p=P)[:, 2 * q:2 * q + 2, at:at + NC]
            if kind == "out":
                return w_out[l].rearrange("(k p) n -> p k n", p=P)[:, 2 * q:2 * q + 2, n * NC:(n + 1) * NC]
            return hidden_source(ffn_w1[0], ffn_w3[0], ffn_w2[0], n, q)

        def hidden_source(w1, w3, w2, n, q):
            what, ch = GROUPS[n]
            if what == "down":
                return w2[ch * NC + q * P:ch * NC + (q + 1) * P, :]
            w = w1 if what == "gate" else w3
            return w.rearrange("(k p) n -> p k n", p=P)[:, 2 * q:2 * q + 2, ch * NC:(ch + 1) * NC]

        def raw_slot(i, wide):
            v = raw[:, i % RAW, :]
            return v if wide else v.rearrange("p (k n) -> p k n", k=2)

        moe_extra = [part(at, QW) for at in (4864, 5888, 7680, 8704, 9728, 10752, 11776)]

        def moe_slot(q):
            s = q % MOE_RAW
            return raw[:, s, :] if s < RAW else moe_extra[s - RAW]

        def score_bank(h):
            return 6 * (h % 2)

        class Pass:

            def __init__(self, blocks, chunks_before, e=None, round_=0):
                self.blocks, self.e, self.round = blocks, e, round_
                self.chunks_before = chunks_before

            def _v(self, base, per):
                base += per * NE * self.round
                return base if self.e is None else self.e * per + base

            def raw(self, q):
                if self.e is None:
                    return RAW_AT[("ffn", 0, q // 4), q % 4] + 1
                return self._v(RAW_MOE + q + 1, PASS_Q)

            def moe_loaded(self, q):
                return self._v(16 * (q // MOE_RAW + 1), 16 * PASS_Q // MOE_RAW)

            def split(self, q):
                if self.e is None:
                    return SPLIT_AT[("ffn", 0, q // 4), q % 4] + 1
                return self._v(SPLIT_MOE + q + 1, PASS_Q)

            def split_static(self, q):
                return (SPLIT_AT[("ffn", 0, 0), 0] if self.e is None else SPLIT_MOE) + q

            def chunk(self, ch):
                return self._v(self.chunks_before + ch + 1, NCH)

            def expert(self, n=1):
                return self._v(n, 1)

            def gate_bank(self, b):
                return b if self.blocks == 2 else 0

            def up_bank(self, b):
                return 2 + b if self.blocks == 2 else 1

        dense = Pass(NT, 0)

        def moe_pass(e, r):
            return Pass(1, NCH, e, r)

        def gw_load(eng, n):
            w = w_in[n].rearrange("(k p) n -> p k n", p=P)[:, :, GATE_COL:GATE_COL + 8] if n < L else \
                router_w[0].rearrange("(k p) n -> p k n", p=P)
            eng.dma_start(gw[:], w).then_inc(sem("gw_loaded"), 16)

        block = ctx.enter_context(nc.Block())

        @block.sync
        def _(sync):
            for r, (p, q) in enumerate(PLAN):
                if r >= RAW:
                    sync.wait_ge(sem("raw_used"), r - RAW + 1)
                wide = p[0] == "ffn" and GROUPS[p[2]][0] == "down"
                sync.dma_start(raw_slot(r, wide), source(p, q)).then_inc(sem(f"raw_loaded{r % RAW}"), 16)

            def expert_load(e, q, free):
                w1, w3, w2 = (w[0, bass.ds(e, 1)].rearrange("o a b -> (o a) b") for w in (moe_w1, moe_w3, moe_w2))
                what = GROUPS[q // 4][0]
                dst = moe_slot(q) if what == "down" else moe_slot(q).rearrange("p (k n) -> p k n", k=2)
                sync.wait_ge(sem("raw_used"), free)
                sync.dma_start(dst, hidden_source(w1, w3, w2, q // 4, q % 4)
                               ).then_inc(sem(f"moe_loaded{q % MOE_RAW}"), 16)

            def moe_round(r):
                base = RAW_MOE + r * NE * PASS_Q
                for q in range(MOE_RAW):
                    if r == 0 and q < RAW:
                        free = RAW_MOE - (RAW_MOE - 1 - q) % RAW
                    elif r == 0:
                        if q == RAW:
                            sync.wait_ge(sem("hT_lo_done"), TURNS)
                        free = RAW_MOE
                    else:
                        free = base + q - MOE_RAW + 1
                    expert_load(0, q, free)
                with sync.Fori(0, NE - 1) as e:
                    for q in range(MOE_RAW, PASS_Q):
                        expert_load(e, q, e * PASS_Q + (base + q - MOE_RAW + 1))
                    for q in range(MOE_RAW):
                        expert_load(e + 1, q, e * PASS_Q + (base + PASS_Q + q - MOE_RAW + 1))
                for q in range(MOE_RAW, PASS_Q):
                    expert_load(NE - 1, q, base + (NE - 1) * PASS_Q + q - MOE_RAW + 1)

            moe_round(0)
            sync.wait_ge(sem("flag_ready"), 1)
            over = sync.value_load(flag[0:1, 0:1], min_val=0, max_val=1)
            with sync.If(over > 0):
                moe_round(1)
            for i in range(NT):
                sync.wait_ge(sem("x_final"), i + 1)
                sync.dma_start(out[0, i * P:(i + 1) * P, :], xs[:, i, :]).then_inc(sem("out_stored"), 16)
            sync.wait_ge(sem("out_stored"), 16 * NT)

        @block.gpsimd
        def _(pool):
            pool.dma_start(lamc[0:N_BUCKETS, 4:4 + H], rel_bias).then_inc(sem("rel_loaded"), 16)
            gw_load(pool, 0)
            pool.dma_start(lamrow, lam_vec.rearrange("l f d -> (l f) d").partition_broadcast(P)
                           ).then_inc(sem("lam_loaded"), 16)
            pool.dma_start(gbias[:], gate_b.rearrange("l t h -> h (l t)"), allow_slow_non_contiguous=True
                           ).then_inc(sem("gbias_loaded"), 16)

            def gate_row_loads(l, sub, g, n):
                at = (2 + 3 * sub) * D
                pool.dma_start(grow[:, g, :], ada_b[l, at:at + D].partition_broadcast(P)
                               ).then_inc(sem(f"grow_loaded{2 * l + sub}"), 16)
                pool.dma_start(ngb[:, n, :], norm_g[l, 1 + 2 * sub, :].partition_broadcast(P)
                               ).then_inc(sem(f"grow_loaded{2 * l + sub}"), 16)

            pieces = [(0, n, accp[m]) for m, n in enumerate(POOL_ADA)]
            pieces += [(l, n, acc1[:, LATE_ADA.index((l, n)), :]) for l, n in LATE_POOL]

            def ada_row(i):
                (l, n, _), k = pieces[i // KT], i % KT
                pool.dma_start(pool_w[:, i % 2, :], ada_w[l, k * P:(k + 1) * P, n * NC:(n + 1) * NC]
                               ).then_inc(sem(f"pool_loaded{i % 2}"), 16)

            def ada_sums(first, last):
                for i in range(first * KT, last * KT):
                    m, k = i // KT, i % KT
                    row, acc = pool_w[:, i % 2, :], pieces[m][2]
                    pool.wait_ge(sem(f"pool_loaded{i % 2}"), 16 * (i // 2 + 1))
                    if k == 0:
                        nc.gpsimd.tensor_scalar(acc, row, cact[:, k:k + 1], None, ALU.mult).then_inc(sem("pool_scaled"), 1)
                        pool.wait_ge(sem("pool_scaled"), i + 1)
                    else:
                        nc.gpsimd.tensor_scalar(row, row, cact[:, k:k + 1], None, ALU.mult).then_inc(sem("pool_scaled"), 1)
                        pool.wait_ge(sem("pool_scaled"), i + 1)
                        nc.gpsimd.tensor_tensor(acc, acc, row, ALU.add).then_inc(sem("pool_added"), 1)
                        pool.wait_ge(sem("pool_added"), i - m)
                    if i + 2 < KT * len(pieces):
                        ada_row(i + 2)

            pool.wait_ge(sem("cact_ready"), 1)
            for i in range(2):
                ada_row(i)
            gate_row_loads(0, 0, 0, 3)
            pool.wait_ge(sem("bias_rows_copied"), 1)
            pool.dma_start(scratch[:, :, :].rearrange("h p n -> p h n"), brows).then_inc(sem("bias_stored"), 16)
            pool.wait_ge(sem("bias_stored"), 16)
            for h in range(H):
                skew = bass.AP(scratch, h * P * 384 + P - 1, [[383, P], [1, S]])
                pool.dma_start(biasT[:, h, :], skew).then_inc(sem("bias_loaded"), 16)
            ada_sums(0, len(POOL_ADA))
            pool.wait_ge(sem("gw_split"), 1)
            gw_load(pool, 1)
            pool.wait_ge(sem("x_added"), 2)
            gate_row_loads(0, 1, 1, 0)
            gate_row_loads(1, 0, 0, 1)
            gate_row_loads(1, 1, 2, 3)
            pool.wait_ge(sem("hT_lo_done"), 12)
            ada_sums(len(POOL_ADA), len(pieces))
            pool.wait_ge(sem("gw_split"), 2)
            gw_load(pool, 2)

        @block.scalar
        def _(act):
            act.dma_start(cT[:], c.rearrange("b (n p) -> p (b n)", p=P), allow_slow_non_contiguous=True
                          ).then_inc(sem("c_loaded"), 16)
            act.dma_start(K[:], tables).then_inc(sem("tables_loaded"), 16)
            for src, t, at in (
                (attn_norm_g, 2, 0),
                (mlstm_norm_g.rearrange("l (n p) -> (l n) p", p=P), 2, 2),
                (norm_g.rearrange("l f (n p) -> (l f n) p", p=P), 0, 0),
                (ada_b.rearrange("l (n p) -> (l n) p", p=P), 1, 0),
                (conv_w.rearrange("l f (n p) -> (l f n) p", p=P), 0, 64),
                (conv_b.rearrange("l (n p) -> (l n) p", p=P), 1, 96),
            ):
                n = src.shape[0]
                act.dma_start(tabs[at:at + n, t, :], src).then_inc(sem("rows_loaded"), 16)
            for i in range(NT):
                act.dma_start(xs[:, i, :], x[0, i * P:(i + 1) * P, :]).then_inc(sem(f"x_loaded{i}"), 16)
            done = [0]

            def after(ins):
                done[0] += 1
                ins.then_inc(sem("act_step"), 1)
                act.wait_ge(sem("act_step"), done[0])

            def hi_quarter(src, w, w_free):
                if w_free is not None:
                    act.wait_ge(sem("w_used"), w_free)
                nc.scalar.activation(w_hi[:, w % SPLIT, :], src, ACT.Copy).then_inc(sem("hi_ready"), 1)

            def plan_quarter(p, q):
                w = SPLIT_AT[p, q]
                r = RAW_AT[p, q]
                act.wait_ge(sem(f"raw_loaded{r % RAW}"), 16 * (r // RAW + 1))
                hi_quarter(raw[:, r % RAW, :], w, w - SPLIT + 1 if w >= SPLIT else None)

            def ahead(p):
                for q in range(AHEAD):
                    plan_quarter(p, q)

            def root(dst, src, n, scale):
                nc.scalar.activation(dst, src, ACT.Sqrt, bias=eps[:, 0:1], scale=scale).then_inc(sem("root_done"), 1)

            roots = [0]

            def norm_tokens(src, junk, what, n):
                for i in range(NT):
                    if what is not None:
                        act.wait_ge(sem(what[i]), n[i])
                    after(nc.scalar.activation(junk(i), src(i), ACT.Square, accum_out=small[:, i:i + 1]))
                    roots[0] += 1
                    root(small[:, 2 + i:3 + i], small[:, i:i + 1], roots[0], 1.0 / D)

            turns = [0]

            def split_turned(scale, bias, taken=None):
                if taken is not None:
                    act.wait_ge(sem(taken[0]), taken[1])
                for b in range(4):
                    turns[0] += 1
                    t = turns[0]
                    act.wait_ge(sem("turned"), t)
                    if t > 2:
                        act.wait_ge(sem("hT_lo_done"), t - 2)
                    for j in range(2):
                        k = 2 * b + j
                        ins = nc.scalar.activation(htmp[:, b % 2, j * S:(j + 1) * S], PS[:, b, j * S:(j + 1) * S],
                                                   ACT.Identity, bias=bias(k), scale=scale(k))
                    after(ins)
                    nc.scalar.activation(hT_hi[:, 2 * b:2 * b + 2, :], htmp[:, b % 2, :].rearrange("p (k n) -> p k n", k=2),
                                         ACT.Copy).then_inc(sem("hT_hi_done"), 1)

            act.wait_ge(sem("c_loaded"), 16)
            nc.scalar.activation(cact[:], cT[:], ACT.Silu).then_inc(sem("cact_ready"), 1)
            act.wait_ge(sem("eps_ready"), 1)
            norm_tokens(lambda i: xs[:, i, :], lambda i: xn[:, i, :], ("x_loaded0", "x_loaded1"), (16, 16))
            act.wait_ge(sem("cols_turned"), 1)
            after(nc.scalar.activation(colT[:].rearrange("p a b -> p (a b)")[:, 0:240], PS[:, 4, 0:240], ACT.Copy))
            nc.scalar.activation(colT[:, 2, 0:10], PS[:, 4, 2 * P:2 * P + 10], ACT.Copy).then_inc(sem("cols_ready"), 1)
            act.wait_ge(sem("bias_rows"), 1)
            nc.scalar.activation(brows, PS[:, 0:4, 0:384], ACT.Copy).then_inc(sem("bias_rows_copied"), 1)
            act.wait_ge(sem("lam_sums"), 1)
            nc.scalar.activation(lamc[:, 0:4], small[:, 8:12], ACT.Exp).then_inc(sem("lam_exp"), 1)

            def evacuate(l, n):
                name = W_IN[n][0]
                b = 2 * (n % 2)
                act.wait_ge(sem("w_used"), SPLIT_AT[("in", l, n), 3] + 1)
                two = PS[:, b:b + 2, :]
                if name == "aq":
                    ins = nc.scalar.activation(aqT.rearrange("p a b -> p (a b)").rearrange("p (a b) -> p a b", a=2),
                                               two, ACT.Copy, scale=float(DH) ** -0.5)
                elif name == "ak":
                    ins = nc.scalar.activation(akT.rearrange("p a b -> p (a b)").rearrange("p (a b) -> p a b", a=2),
                                               two, ACT.Copy)
                else:
                    dst = {"av": av, "mv": mv, "mo": so}[name]
                    ins = nc.scalar.activation(dst, two, ACT.Sigmoid if name == "mo" else ACT.Copy)
                ins.then_inc(sem("in_out"), 1)

            def silu_conv(l, half):
                act.wait_ge(sem("conv_done"), 2 * l + half + 1)
                v = qk[:, 4 * half:4 * half + 4, :]
                nc.scalar.activation(v, v, ACT.Silu).then_inc(sem("qk_ready"), 1)

            def log_forget(l):
                z, t = grows[:, 1, :], grows[:, 2, :]
                act.wait_ge(sem("gate_pre"), l + 1)
                after(nc.scalar.activation(t, z, ACT.Abs))
                after(nc.scalar.activation(t, t, ACT.Exp, scale=-1.0))
                nc.scalar.activation(t, t, ACT.Ln, bias=1.0).then_inc(sem("log_done"), 1)

            def decay(l, h):
                n = H * l + h
                act.wait_ge(sem("decay_logits"), n + 1)
                if n == H * l:
                    act.wait_ge(sem("gate_cols_copied"), l + 1)
                nc.scalar.activation(E[:, 0:S], PS[:, 4, 0:S], ACT.Exp, bias=acol[:, 0, h:h + 1])
                nc.scalar.activation(E[:, S:384], PS[:, 4, S:384], ACT.Exp,
                                     bias=acol[:, 1, h:h + 1]).then_inc(sem("decay_done"), 1)

            def mixer(l):
                for n in range(len(W_IN)):
                    for q in range(4):
                        if q == 3 and n > 2:
                            evacuate(l, n - 1)
                        if q == 0 and n in (3, 4):
                            silu_conv(l, n - 3)
                        if q == 1 and n == 2:
                            log_forget(l)
                        for h in range(H):
                            if 4 * (n - 4) + q == DECAY_AT[h] + 3:
                                decay(l, h)
                        if n or q >= AHEAD:
                            plan_quarter(("in", l, n), q)
                ahead(("out", l, 0))
                evacuate(l, len(W_IN) - 1)
                nc.scalar.activation(acol[:, :, 4:8], acol[:, :, 4:8], ACT.Exp, scale=-1.0).then_inc(sem("floor_ready"), 1)
                for h in range(H + 2):
                    if h < H:
                        n = H * l + h
                        act.wait_ge(sem("scores_max"), n + 1)
                        if n >= 2:
                            act.wait_ge(sem("probs_turned"), n - 1)
                        for cc in range(2):
                            for i in range(NT):
                                o, w = (0, P) if i == 0 else (P, S)
                                at = 2 * cc + i
                                ins = nc.scalar.activation(
                                    pr[:, h % 2, cc, o:o + w], PS[:, score_bank(h) + cc, o:o + w], ACT.Exp,
                                    bias=att[:, h, at:at + 1], accum_out=att[:, h, 4 + at:5 + at])
                        ins.then_inc(sem("exp_done"), 1)
                    if 1 <= h <= H:
                        n = H * l + h - 1
                        act.wait_ge(sem("probs_turned"), n + 1)
                        if n >= 1:
                            act.wait_ge(sem("attn_out"), n)
                        nc.scalar.activation(aT, PS[:, 2:4, 0:384], ACT.Copy).then_inc(sem("aT_ready"), 1)
                    if h >= 2:
                        g = h - 2
                        act.wait_ge(sem("head_mixed"), H * l + g + 1)
                        for i in range(NT):
                            after(nc.scalar.activation(sqh, xn[:, i, g * P:(g + 1) * P], ACT.Square,
                                                       accum_out=small[:, 16 + 4 * i + g:17 + 4 * i + g]))
                roots[0] += 1
                root(small[:, 24:32], small[:, 16:24], roots[0], 1.0 / P)
                act.wait_ge(sem("head_squares"), l + 1)
                roots[0] += 1
                root(mroot, msq, roots[0], 1.0 / P)
                split_turned(lambda k: mixA[:, k:k + 1], lambda k: 0.0)
                for n in range(2):
                    for q in range(0 if n else AHEAD, 4):
                        plan_quarter(("out", l, n), q)
                if l == 0:
                    ahead(("ffn", 0, 0))
                act.wait_ge(sem("w_used"), SPLIT_AT[("out", l, 1), 3] + 1)
                norm_tokens(lambda i: PS[:, 4 + 2 * i:6 + 2 * i, :], lambda i: xn[:, i, :].rearrange("p (a b) -> p a b", a=2),
                            None, None)
                norm_tokens(lambda i: xs[:, i, :], lambda i: xn[:, i, :], ("x_added",) * 2, (4 * l + 1, 4 * l + 2))
                split_turned(lambda k: modA[:, 1, k:k + 1], lambda k: modcol[:, 24 + k:25 + k],
                             ("late_cols_taken", 1) if l else ("ada_taken", 10))

            def extras(ps, q):
                for ch in range(NCH):
                    if q == LAST_Q[("gate", ch)] + SPLIT:
                        act.wait_ge(sem("w_used"), ps.split(LAST_Q[("gate", ch)]))
                        for b in range(ps.blocks):
                            ins = nc.scalar.activation(hidden[:, b, :], PS[:, ps.gate_bank(b), :], ACT.Silu)
                        ins.then_inc(sem("silu_done"), 1)
                    if q == turn_after(ch) + SPLIT:
                        act.wait_ge(sem("hidden_turned"), ps.chunk(ch))
                        for b in range(ps.blocks):
                            ins = nc.scalar.activation(sT_hi[:, :, b * P:(b + 1) * P],
                                                       PS[:, ps.up_bank(b), :].rearrange("p (a b) -> p a b", a=4), ACT.Copy)
                        ins.then_inc(sem("sT_hi_done"), 1)

            ahead(("in", 0, 0))
            split_turned(lambda k: modA[:, 0, k:k + 1], lambda k: modcol[:, k:k + 1], ("ada_taken", 4))
            mixer(0)
            for q in range(PASS_Q):
                extras(dense, q)
                if q >= AHEAD:
                    plan_quarter(("ffn", 0, q // 4), q % 4)
            ahead(("in", 1, 0))
            act.wait_ge(sem("w_used"), dense.split(PASS_Q - 1))
            norm_tokens(lambda i: PS[:, 4 + 2 * i:6 + 2 * i, :], lambda i: xn[:, i, :].rearrange("p (a b) -> p a b", a=2),
                        None, None)
            norm_tokens(lambda i: xs[:, i, :], lambda i: xn[:, i, :], ("x_added",) * 2, (3, 4))
            split_turned(lambda k: modA[:, 0, k:k + 1], lambda k: modcol[:, k:k + 1], ("late_cols_taken", 1))
            mixer(1)
            act.wait_ge(sem("top_gap"), 1)
            nc.scalar.activation(tw[:, 2:4], tw[:, 0:2], ACT.Exp).then_inc(sem("top_exp"), 1)

            def modulate(k, n):
                if k == 0:
                    act.wait_ge(sem("gathered"), n)
                ins = nc.scalar.activation(xg[:, k * P:(k + 1) * P], PS[:, 2 + k // 4, (k % 4) * P:(k % 4 + 1) * P],
                                           ACT.Identity, bias=modcol[:, 24 + k:25 + k], scale=modA[:, 1, k:k + 1])
                if k == KT - 1:
                    ins.then_inc(sem("xg_ready"), 1)

            def expert_hi(n):
                act.wait_ge(sem("xg_ready"), n)
                nc.scalar.activation(hT_hi[:, :, 0:P], xg.rearrange("p (a b) -> p a b", a=KT), ACT.Copy
                                     ).then_inc(sem("xT_hi_done"), 1)

            def moe_round(r):
                g0 = (NE + 1) * r
                for k in range(KT):
                    modulate(k, g0 + 1)
                expert_hi(g0 + 1)
                with act.Fori(0, NE) as e:
                    ps = moe_pass(e, r)
                    for q in range(PASS_Q):
                        extras(ps, q)
                        if q == 4:
                            act.wait_ge(sem("w_used"), ps.split(0))
                            nc.scalar.activation(ye_sb.rearrange("p (a b) -> p a b", a=2), PS[:, 4:6, :], ACT.Copy
                                                 ).then_inc(sem("ye_ready"), 1)
                        if q == 28:
                            act.wait_ge(sem("comb_turned"), ps.expert())
                            nc.scalar.activation(combT, PS[:, 6, 0:S], ACT.Copy)
                        if 52 <= q < 52 + KT:
                            modulate(q - 52, e + g0 + 2)
                        if q == LAST_Q[("up", NCH - 1)] + SPLIT:
                            act.wait_ge(sem("w_used"), ps.split(LAST_Q[("up", NCH - 1)]))
                            expert_hi(e + g0 + 2)
                        act.wait_ge(sem(f"moe_loaded{q % MOE_RAW}"), ps.moe_loaded(q))
                        hi_quarter(moe_slot(q), ps.split_static(q), ps.split(q) - SPLIT)
                act.wait_ge(sem("w_used"), SPLIT_MOE + (r + 1) * NE * PASS_Q)
                nc.scalar.activation(ye_sb.rearrange("p (a b) -> p a b", a=2), PS[:, 4:6, :], ACT.Copy
                                     ).then_inc(sem("ye_ready"), 1)

            moe_round(0)
            act.wait_ge(sem("flag_ready"), 1)
            over = act.value_load(flag[0:1, 0:1], min_val=0, max_val=1)
            with act.If(over > 0):
                moe_round(1)
            norm_tokens(lambda i: y_sb[:, i, :], lambda i: ye_sb, ("y_complete",) * 2, (1, 1))

        @block.vector
        def _(dve):
            done = [0]

            def after(ins):
                done[0] += 1
                ins.then_inc(sem("dve_step"), 1)
                dve.wait_ge(sem("dve_step"), done[0])

            def lo_quarter(src, w, hi):
                dve.wait_ge(sem("hi_ready"), hi)
                nc.vector.tensor_tensor(w_lo[:, w % SPLIT, :], src, w_hi[:, w % SPLIT, :],
                                        ALU.subtract).then_inc(sem("raw_used"), 1)

            def plan_quarter(p, q):
                lo_quarter(raw[:, RAW_AT[p, q] % RAW, :], SPLIT_AT[p, q], SPLIT_AT[p, q] + 1)

            roots = [0]

            def ahead(p):
                for q in range(AHEAD):
                    plan_quarter(p, q)

            def invert_root(dst, src):
                roots[0] += 1
                dve.wait_ge(sem("root_done"), roots[0])
                after(nc.vector.reciprocal(dst, src))

            def normalise():
                for i in range(NT):
                    invert_root(small[:, 4 + i:5 + i], small[:, 2 + i:3 + i])
                    nc.vector.tensor_scalar(xn[:, i, :], xs[:, i, :], small[:, 4 + i:5 + i], None,
                                            ALU.mult).then_inc(sem("xn_ready"), 1)

            turns = [0]

            def split_turned():
                for b in range(4):
                    turns[0] += 1
                    dve.wait_ge(sem("hT_hi_done"), turns[0])
                    nc.vector.tensor_tensor(hT_lo[:, 2 * b:2 * b + 2, :], htmp[:, b % 2, :].rearrange("p (k n) -> p k n", k=2),
                                            hT_hi[:, 2 * b:2 * b + 2, :], ALU.subtract).then_inc(sem("hT_lo_done"), 1)

            def ada_acc(l, n):
                if (l, n) in LATE_ADA:
                    return acc1[:, LATE_ADA.index((l, n)), :]
                return acc0[:, n % 2, :] if n < 5 else acc56[:, n - 5, :]

            def ada_sum(l, n, q):
                acc = ada_acc(l, n)
                if l == 0 and q == 0 and 2 <= n < 5:
                    dve.wait_ge(sem("ada_summed"), n - 1)
                r = RAW_AT[("ada", l, n), q]
                dve.wait_ge(sem(f"raw_loaded{r % RAW}"), 16 * (r // RAW + 1))
                v = raw_slot(r, False)
                for j in range(2):
                    k = 2 * q + j
                    if k == 0:
                        ins = nc.vector.tensor_scalar(acc, v[:, j, :], cact[:, k:k + 1], None, ALU.mult)
                    else:
                        ins = nc.vector.scalar_tensor_tensor(acc, v[:, j, :], cact[:, k:k + 1], acc, ALU.mult, ALU.add)
                    if j == 0:
                        after(ins)
                ins.then_inc(sem("raw_used"), 1)
                dve.wait_ge(sem("raw_used"), r + 1)

            def gate_row(l, n, bank, g, gain):
                sub, half = (0 if n // 2 == 2 else 1), slice((n % 2) * NC, (n % 2 + 1) * NC)
                dve.wait_ge(sem(f"grow_loaded{2 * l + sub}"), 32)
                after(nc.vector.tensor_tensor(grow[:, g, half], PS[:, bank, :], grow[:, g, half], ALU.add))
                return nc.vector.tensor_tensor(grow[:, g, half], grow[:, g, half], ngb[:, gain, half], ALU.mult)

            def mod_columns(l, n, count, bank):
                c = slice(4 * n, 4 * (n + count))
                after(nc.vector.tensor_tensor(modcol[:, c], PS[:, bank, c],
                                              colT[:, 1, 48 * l + c.start:48 * l + c.stop], ALU.add))

            def mod_scale(l, sub):
                at, s = 8 * (4 * l + 2 * sub), 8 * (1 + 3 * sub)
                return nc.vector.scalar_tensor_tensor(modA[:, sub, :], modcol[:, s:s + 8], 1.0, colT[:, 0, at:at + 8],
                                                      ALU.add, ALU.mult)

            def ada_take(n):
                i = ADA_ORDER.index(n)
                dve.wait_ge(sem("ada_summed"), i + 1 if i < ADA_EARLY else len(ADA_ORDER))
                if n // 2 == 2:
                    ins = gate_row(0, n, 5 if n == 4 else 1, 0, 3)
                else:
                    c = slice(4 * n, 4 * n + 4)
                    ins = nc.vector.tensor_tensor(modcol[:, c], PS[:, 0 if n >= 6 else 4, c],
                                                  colT[:, 1, c], ALU.add)
                    if n in (3, 6):
                        after(ins)
                        ins = mod_scale(0, 0 if n == 3 else 1)
                ins.then_inc(sem("ada_taken"), 1)

            def late_row(m, l, n, bank, g, gain):
                dve.wait_ge(sem("late_rows_summed"), m)
                gate_row(l, n, bank, g, gain).then_inc(sem("late_rows_taken"), 1)
                dve.wait_ge(sem("late_rows_taken"), m)

            def conv(l, half, tap):
                if tap == 0:
                    dve.wait_ge(sem("w_used"), SPLIT_AT[("in", l, half), 3] + 1)
                    if l == 0:
                        dve.wait_ge(sem("bias_stored"), 16)
                else:
                    dve.wait_ge(sem("tap_done"), 3 * (2 * l + half) + tap)
                for j in range(4):
                    n = 4 * half + j
                    psv = PS[:, 2 * half + j // 2, (j % 2) * S:(j % 2 + 1) * S]
                    wt = colT[:, 0, 64 + (4 * l + 3 - tap) * 8 + n:65 + (4 * l + 3 - tap) * 8 + n]
                    if tap == 0:
                        ins = nc.vector.tensor_scalar(qk[:, n, :], psv, wt, colT[:, 1, 96 + 8 * l + n:97 + 8 * l + n],
                                                      ALU.mult, ALU.add)
                    else:
                        ins = nc.vector.scalar_tensor_tensor(qk[:, n, tap:S], psv[:, 0:S - tap], wt, qk[:, n, tap:S],
                                                             ALU.mult, ALU.add)
                ins.then_inc(sem("tap_done" if tap < 3 else "conv_done"), 1)

            def split_gates(n, l):
                dve.wait_ge(sem("gw_loaded"), 16 * (n + 1))
                if n:
                    dve.wait_ge(sem("gates_done"), n)
                after(nc.vector.tensor_copy(gw_hi[:], gw[:]))
                nc.vector.tensor_tensor(gw_lo[:], gw[:], gw_hi[:], ALU.subtract).then_inc(sem("gw_split"), 1)

            zi, zf, lnf, cum, a_row, run_max, stab = (grows[:, i, :] for i in (0, 1, 2, 3, 4, 5, 6))

            def gate_rows_in(l):
                dve.wait_ge(sem("gates_done"), l + 1)
                after(nc.vector.memset(grows[:, 7, :], 1.0))
                nc.vector.tensor_scalar(zi, PS[0:H, 7, 0:S], gbias[:, 2 * l:2 * l + 1], None, ALU.add)
                nc.vector.tensor_scalar(zf, PS[0:H, 7, S:2 * S], gbias[:, 2 * l + 1:2 * l + 2], None, ALU.add
                                        ).then_inc(sem("gate_pre"), 1)

            def gate_chain(l):
                dve.wait_ge(sem("log_done"), l + 1)
                after(nc.vector.scalar_tensor_tensor(lnf, zf, 0.0, lnf, ALU.min, ALU.subtract))
                after(nc.vector.tensor_tensor_scan(cum, grows[:, 7, :], lnf, 0.0, ALU.mult, ALU.add))
                after(nc.vector.tensor_tensor(a_row, zi, cum, ALU.subtract))
                after(nc.vector.tensor_tensor_scan(run_max, a_row, a_row, 0.0, ALU.max, ALU.max))
                after(nc.vector.tensor_scalar(zi, run_max, -1.0, None, ALU.mult))
                nc.vector.tensor_tensor(stab, cum, run_max, ALU.add).then_inc(sem("gate_ready"), 1)

            def post(l, sub, y, n):
                ytmp = ytmp0 if n == 0 else ytmp1
                for i in range(NT):
                    invert_root(small[:, 4 + i:5 + i], small[:, 2 + i:3 + i])
                    after(nc.vector.scalar_tensor_tensor(ytmp.rearrange("p (a b) -> p a b", a=2), y(i), small[:, 4 + i:5 + i],
                                                         grow[:, (sub, 2 * sub)[l], :].rearrange("p (a b) -> p a b", a=2),
                                                         ALU.mult, ALU.mult))
                    nc.vector.tensor_tensor(xs[:, i, :], xs[:, i, :], ytmp, ALU.add).then_inc(
                        sem("x_final" if n == 3 else "x_added"), 1)
                    if n < 3:
                        dve.wait_ge(sem("x_added"), NT * n + i + 1)

            def heads(v):
                return v.rearrange("p (h d) -> p h d", h=H)

            def wide(v):
                return v.unsqueeze(2).to_broadcast([P, H, P])

            def mlstm_weights(l, h):
                n = H * l + h
                dve.wait_ge(sem("decay_done"), n + 1)
                dve.wait_ge(sem("mqk_done"), n + 1)
                nc.vector.scalar_tensor_tensor(Sw, PS[:, 5, 0:384], float(P) ** -0.5, E, ALU.mult, ALU.mult
                                               ).then_inc(sem("sw_done"), 1)

            def mlstm_out(l):
                dve.wait_ge(sem("mlstm_sums"), H * (l + 1))
                dve.wait_ge(sem("floor_ready"), l + 1)
                after(nc.vector.tensor_copy(dn, PS[:, 5, 384:392]))
                after(nc.vector.scalar_tensor_tensor(dn, dn, -1.0, dn, ALU.mult, ALU.max))
                dn3 = dn.rearrange("p (i h) -> p i h", i=NT)
                after(nc.vector.tensor_tensor(dn3, dn3, acol[:, :, 4:8], ALU.max))
                after(nc.vector.reciprocal(dn, dn))
                for i in range(NT):
                    nc.vector.tensor_tensor(heads(xn[:, i, NC:D]), heads(PS[:, 6 + i, :]), wide(dn[:, 4 * i:4 * i + 4]),
                                            ALU.mult).then_inc(sem("num_taken"), 1)
                    dve.wait_ge(sem("num_taken"), NT * l + i + 1)

            def mlstm_gate(l, i):
                v = xn[:, i, NC:D]
                after(nc.vector.tensor_tensor(v, v, so[:, i, :], ALU.mult))
                after(nc.vector.tensor_tensor(sq, v, v, ALU.mult))
                ins = nc.vector.tensor_reduce(msq[:, 4 * i:4 * i + 4], heads(sq), AX, ALU.add)
                if i == NT - 1:
                    ins.then_inc(sem("head_squares"), 1)
                else:
                    after(ins)

            def scores_max(l, h):
                dve.wait_ge(sem("scores_done"), H * l + h + 1)
                mx = att[:, h, 0:4].rearrange("p (c i) -> p c i", c=2)
                nc.vector.tensor_reduce(mx[:, :, 0], PS[:, score_bank(h):score_bank(h) + 2, 0:P], AX, ALU.max)
                after(nc.vector.tensor_reduce(mx[:, :, 1], PS[:, score_bank(h):score_bank(h) + 2, P:384], AX, ALU.max))
                nc.vector.tensor_scalar(att[:, h, 0:4], att[:, h, 0:4], -1.0, None, ALU.mult
                                        ).then_inc(sem("scores_max"), 1)

            def combine(l, h):
                n = H * l + h
                r = att[:, h, 4:8]
                dve.wait_ge(sem("exp_done"), n + 1)
                after(nc.vector.reciprocal(r, r))
                after(nc.vector.tensor_scalar(r[:, 2:4], r[:, 2:4], lamc[:, l:l + 1], None, ALU.mult))
                dve.wait_ge(sem("attn_out"), n + 1)
                o = slice(h * P, (h + 1) * P)
                for i in range(NT):
                    ins = nc.vector.tensor_scalar(xn[:, i, o], PS[:, 4 + h % 2, S + i * P:S + (i + 1) * P], r[:, 2 + i:3 + i], None, ALU.mult)
                after(ins)
                for i in range(NT):
                    ins = nc.vector.scalar_tensor_tensor(xn[:, i, o], PS[:, 4 + h % 2, i * P:(i + 1) * P], r[:, i:i + 1], xn[:, i, o],
                                                         ALU.mult, ALU.subtract)
                ins.then_inc(sem("head_mixed"), 1)

            def mixer(l):
                split_gates(l, l)
                for n in range(len(W_IN)):
                    for q in range(4):
                        for half in range(2):
                            if 0 <= 4 * (n - half - 1) + q - 3 < 4:
                                conv(l, half, 4 * (n - half - 1) + q - 3)
                        if q == 0 and n == 2:
                            gate_rows_in(l)
                        if q == 3 and n == 3:
                            gate_chain(l)
                        if l == 0 and n == 3 and q == 3:
                            ada_take(4)
                        if l == 0 and n in ADA_BESIDE:
                            ada_sum(0, ADA_BESIDE[n], q)
                        if q == 2 and n == 4:
                            dve.wait_ge(sem("gate_cols"), l + 1)
                            nc.vector.tensor_copy(acol[:], PS[:, 7, 0:16].rearrange("p (a b) -> p a b", a=NT)
                                                  ).then_inc(sem("gate_cols_copied"), 1)
                        for h in range(H):
                            if 4 * (n - 4) + q == DECAY_AT[h] + 3:
                                mlstm_weights(l, h)
                        if n or q >= AHEAD:
                            plan_quarter(("in", l, n), q)
                ahead(("out", l, 0))
                nc.vector.tensor_scalar(mixA[:, 0:H], colT[:, 2, l:l + 1].to_broadcast([P, H]),
                                        float(1.0 - (0.8 - 0.6 * math.exp(-0.3 * l))), None, ALU.mult)
                after(nc.vector.tensor_copy(mixA[:, H:2 * H], colT[:, 2, 2 + 4 * l:6 + 4 * l]))
                mlstm_out(l)
                for h in range(H + 2):
                    if h < H:
                        scores_max(l, h)
                    if h < NT:
                        mlstm_gate(l, h)
                    if h >= 2:
                        combine(l, h - 2)
                invert_root(small[:, 24:32], small[:, 24:32])
                roots[0] += 1
                dve.wait_ge(sem("root_done"), roots[0])
                after(nc.vector.reciprocal(mroot, mroot))
                for i in range(NT):
                    nc.vector.tensor_tensor(heads(xn[:, i, 0:NC]), heads(xn[:, i, 0:NC]),
                                            wide(small[:, 24 + 4 * i:28 + 4 * i]), ALU.mult)
                    nc.vector.tensor_tensor(heads(xn[:, i, NC:D]), heads(xn[:, i, NC:D]),
                                            wide(mroot[:, 4 * i:4 * i + 4]), ALU.mult).then_inc(sem("mixed_ready"), 1)
                split_turned()
                for n in range(2):
                    for q in range(0 if n else AHEAD, 4):
                        plan_quarter(("out", l, n), q)
                if l == 0:
                    ahead(("ffn", 0, 0))
                    for m in ADA_ORDER[ADA_EARLY:]:
                        ada_take(m)
                post(l, 0, lambda i: PS[:, 4 + 2 * i:6 + 2 * i, :], 2 * l)
                normalise()
                split_turned()

            def extras(ps, q):
                for ch in range(NCH):
                    if q == LAST_Q[("up", ch)] + SPLIT:
                        dve.wait_ge(sem("w_used"), ps.split(LAST_Q[("up", ch)]))
                        dve.wait_ge(sem("silu_done"), ps.chunk(ch))
                        for b in range(ps.blocks):
                            ins = nc.vector.tensor_tensor(hidden[:, b, :], PS[:, ps.up_bank(b), :], hidden[:, b, :], ALU.mult)
                        ins.then_inc(sem("hidden_ready"), 1)
                    if q == turn_after(ch) + SPLIT:
                        dve.wait_ge(sem("sT_hi_done"), ps.chunk(ch))
                        for b in range(ps.blocks):
                            ins = nc.vector.tensor_tensor(sT_lo[:, :, b * P:(b + 1) * P],
                                                          PS[:, ps.up_bank(b), :].rearrange("p (a b) -> p a b", a=4),
                                                          sT_hi[:, :, b * P:(b + 1) * P], ALU.subtract)
                        ins.then_inc(sem("sT_lo_done"), 1)

            def relative_bias():
                nc.vector.memset(relb[32:33, :, :], 1.0)
                dve.wait_ge(sem("rel_loaded"), 16)
                nc.vector.tensor_copy(relb[0:N_BUCKETS, :, :],
                                      lamc[0:N_BUCKETS, 4:4 + H].unsqueeze(2).to_broadcast([N_BUCKETS, H, P])
                                      ).then_inc(sem("relb_ready"), 1)

            def lambda_sums():
                dve.wait_ge(sem("lam_loaded"), 16)
                lv = lamrow.rearrange("p (a b) d -> p a b d", b=2)
                after(nc.vector.tensor_tensor(lamp, lv[:, :, 0, :], lv[:, :, 1, :], ALU.mult))
                nc.vector.tensor_reduce(small[:, 8:12], lamp, AX, ALU.add).then_inc(sem("lam_sums"), 1)

            nc.vector.memset(eps[:], EPS).then_inc(sem("eps_ready"), 1)
            dve.wait_ge(sem("cact_ready"), 1)
            for n in range(4):
                for q in range(4):
                    ada_sum(0, n, q)
                if n == 0:
                    relative_bias()
                    lambda_sums()
                    normalise()
                    dve.wait_ge(sem("cols_ready"), 1)
                else:
                    ada_take(n - 1)
            ada_take(3)
            ahead(("in", 0, 0))
            split_turned()
            dve.wait_ge(sem("lam_exp"), 1)
            for l in range(L):
                lam_init = 0.8 - 0.6 * math.exp(-0.3 * l)
                after(nc.vector.scalar_tensor_tensor(lamc[:, 4 + l:5 + l], lamc[:, 2 * l:2 * l + 1], float(lam_init),
                                                     lamc[:, 2 * l + 1:2 * l + 2], ALU.add, ALU.subtract))
            after(nc.vector.tensor_copy(lamc[:, 0:2], lamc[:, 4:6]))
            dve.wait_ge(sem("gbias_loaded"), 16)
            mixer(0)
            nxt = 0
            for g in range(len(GROUPS)):
                for q in range(4):
                    extras(dense, 4 * g + q)
                    if g or q >= AHEAD:
                        plan_quarter(("ffn", 0, g), q)
                if g in LATE_AFTER:
                    for q in range(4):
                        ada_sum(*LATE_ADA[nxt], q)
                    nxt += 1
            ahead(("in", 1, 0))
            late_row(1, 0, 10, 1, 1, 0)
            late_row(2, 0, 11, 2, 1, 0)
            dve.wait_ge(sem("late_cols_summed"), 1)
            mod_columns(1, 0, 4, 0)
            mod_columns(1, 6, 4, 0)
            mod_scale(1, 0)
            mod_scale(1, 1).then_inc(sem("late_cols_taken"), 1)
            late_row(3, 1, 4, 3, 0, 1)
            post(0, 1, lambda i: PS[:, 4 + 2 * i:6 + 2 * i, :], 1)
            normalise()
            split_turned()
            late_row(4, 1, 5, 4, 0, 1)
            late_row(5, 1, 10, 5, 2, 3)
            late_row(6, 1, 11, 7, 2, 3)
            mixer(1)

            split_gates(2, None)
            dve.wait_ge(sem("gates_done"), 3)
            nc.vector.tensor_copy(lgT, PS[0:NE, 6, 0:S]).then_inc(sem("logit_rows"), 1)
            nc.vector.memset(routing[:, 0:54], 0.0)
            dve.wait_ge(sem("logits_turned"), 1)
            after(nc.vector.tensor_copy(lg, PS[:, 7, 0:16].rearrange("p (a b) -> p a b", a=NT)))
            for i in range(NT):
                after(nc.vector.max(top[:, i, :], lg[:, i, :]))
                after(nc.vector.max_index(midx[:, i, :], top[:, i, :], lg[:, i, :]))
            after(nc.vector.tensor_copy(topi, midx[:]))
            nc.vector.tensor_tensor(tw[:, 0:2], top[:, :, 1], top[:, :, 0], ALU.subtract).then_inc(sem("top_gap"), 1)
            for n in range(2):
                for i in range(NT):
                    ins = nc.vector.tensor_scalar(pick[:, n, i, :], iota[:, 0:NE], topi[:, i, n:n + 1], None, ALU.is_equal)
            after(ins)
            nc.vector.tensor_tensor(sel[:, :, 0:NE], pick[:, 0], pick[:, 1], ALU.add).then_inc(sem("sel_ready"), 1)
            dve.wait_ge(sem("top_exp"), 1)
            after(nc.vector.tensor_scalar(tw[:, 4:6], tw[:, 2:4], 1.0, None, ALU.add))
            after(nc.vector.reciprocal(tw[:, 6:8], tw[:, 4:6]))
            after(nc.vector.tensor_tensor(tw[:, 8:10], tw[:, 6:8], tw[:, 2:4], ALU.mult))
            for i in range(NT):
                after(nc.vector.tensor_scalar(gates[:, i, 0:NE], pick[:, 1, i, :], tw[:, 8 + i:9 + i], None, ALU.mult))
                after(nc.vector.scalar_tensor_tensor(gates[:, i, 0:NE], pick[:, 0, i, :], tw[:, 6 + i:7 + i],
                                                     gates[:, i, 0:NE], ALU.mult, ALU.add))
            dve.wait_ge(sem("ranks_done"), 1)
            after(nc.vector.tensor_copy(ranks[:, :, 0:NE], PS[:, 6, 16:32].rearrange("p (a b) -> p a b", a=NT)))
            after(nc.vector.tensor_reduce(tw[:, 10:11], PS[:, 6, 32:40], AX, ALU.max))
            after(nc.vector.tensor_scalar(tw[:, 11:12], tw[:, 10:11], float(P), None, ALU.is_gt))
            nc.vector.tensor_copy(flag[:], tw[:, 11:12]).then_inc(sem("flag_ready"), 1)
            after(nc.vector.memset(y_sb, 0.0))

            def onehots(dst, weight, col):
                for i in range(NT):
                    ins = nc.vector.tensor_scalar(dst[:, i, :], iota, ranks[:, i, col], weight[:, i, col],
                                                  ALU.is_equal, ALU.mult)
                return ins

            def expert_lo(n):
                dve.wait_ge(sem("xT_hi_done"), n)
                nc.vector.tensor_tensor(hT_lo[:, :, 0:P], xg.rearrange("p (a b) -> p a b", a=KT), hT_hi[:, :, 0:P],
                                        ALU.subtract).then_inc(sem("xT_ready"), 1)

            def add_scattered(n, m):
                dve.wait_ge(sem("scattered"), n)
                nc.vector.tensor_tensor(y_sb[:, 0, :].rearrange("p (a b) -> p a b", a=2), PS[:, 6:8, :],
                                        y_sb[:, 0, :].rearrange("p (a b) -> p a b", a=2), ALU.add)
                nc.vector.tensor_tensor(y_sb[:, 1, :].rearrange("p (a b) -> p a b", a=2), PS[:, 2:4, :],
                                        y_sb[:, 1, :].rearrange("p (a b) -> p a b", a=2), ALU.add).then_inc(sem("y_added"), 1)
                dve.wait_ge(sem("y_added"), m)

            def moe_round(r):
                g0 = (NE + 1) * r
                if r:
                    nc.vector.tensor_scalar(ranks, ranks, -float(P), None, ALU.add).then_inc(sem("ranks_moved"), 1)
                    dve.wait_ge(sem("ranks_moved"), 1)
                nc.vector.memset(combT, 0.0).then_inc(sem("zeros_ready"), 1)
                onehots(disp, sel, slice(0, 1)).then_inc(sem("disp_ready"), 1)
                expert_lo(g0 + 1)
                with dve.Fori(0, NE) as e:
                    ps = moe_pass(e, r)
                    for q in range(PASS_Q):
                        extras(ps, q)
                        if q == 10:
                            add_scattered(e + g0 + 1, e + g0 + 1)
                        if q == 4:
                            onehots(comb, gates, bass.ds(e, 1)).then_inc(sem("comb_ready"), 1)
                        if q == 36:
                            onehots(disp, sel, bass.ds(e + 1, 1)).then_inc(sem("disp_ready"), 1)
                        if q == LAST_Q[("up", NCH - 1)] + SPLIT:
                            expert_lo(e + g0 + 2)
                        lo_quarter(moe_slot(q), ps.split_static(q), ps.split(q))
                add_scattered(g0 + NE + 1, g0 + NE + 1)

            moe_round(0)
            over = dve.value_load(flag[0:1, 0:1], min_val=0, max_val=1)
            with dve.If(over > 0):
                moe_round(1)
            nc.vector.memset(small[:, 58:59], 0.0).then_inc(sem("y_complete"), 1)
            post(1, 1, lambda i: y_sb[:, i, :].rearrange("p (a b) -> p a b", a=2), 3)

        @block.tensor
        def _(pe):
            def three(dst, a_hi, a_lo, b_hi, b_lo, start, stop):
                nc.tensor.matmul(dst, a_hi, b_hi, start=start, stop=False, skip_group_check=True)
                nc.tensor.matmul(dst, a_hi, b_lo, start=False, stop=False, skip_group_check=True)
                return nc.tensor.matmul(dst, a_lo, b_hi, start=False, stop=stop, skip_group_check=True)

            def mm(dst, a, b, start=True, stop=True):
                return nc.tensor.matmul(dst, a, b, start=start, stop=stop, skip_group_check=True)

            def split_view(w):
                return (w_hi[:, w % SPLIT, :].rearrange("p (k n) -> p k n", k=2),
                        w_lo[:, w % SPLIT, :].rearrange("p (k n) -> p k n", k=2))

            turned = [0]

            def turn(src_sem, counts):
                for i in range(NT):
                    pe.wait_ge(sem(src_sem), counts[i])
                if turned[0]:
                    pe.wait_ge(sem("hT_lo_done"), turned[0])
                if turned[0] == 8:
                    pe.wait_ge(sem("ada_taken"), 10)
                if turned[0] == 12:
                    pe.wait_ge(sem("late_rows_taken"), 3)
                for b in range(4):
                    for j in range(2):
                        for i in range(NT):
                            k = 2 * b + j
                            ins = nc.tensor.transpose(PS[:, b, j * S + i * P:j * S + (i + 1) * P],
                                                      xn[:, i, k * P:(k + 1) * P], ident)
                    ins.then_inc(sem("turned"), 1)
                    turned[0] += 1

            def split_ready(q=3):
                pe.wait_ge(sem("hT_lo_done"), turned[0] - 3 + max(q, 1))

            def ada_reduce(n):
                if n in POOL_ADA:
                    m = POOL_ADA.index(n)
                    pe.wait_ge(sem("pool_added"), (KT - 1) * (m + 1))
                    acc = accp[m]
                else:
                    pe.wait_ge(sem("raw_used"), RAW_AT[("ada", 0, n), 3] + 1)
                    acc = acc0[:, n % 2, :] if n < 5 else acc56[:, n - 5, :]
                if n:
                    pe.wait_ge(sem("ada_taken"), min(ADA_ORDER.index(n), ADA_EARLY))
                if n // 2 == 2:
                    mm(PS[:, 5 if n == 4 else 1, :], ones, acc).then_inc(sem("ada_summed"), 1)
                else:
                    columns(acc, n, 0 if n >= 6 else 4).then_inc(sem("ada_summed"), 1)

            def columns(acc, n, bank):
                for j in range(4):
                    ins = mm(PS[:, bank, 4 * n + j:4 * n + j + 1], acc[:, j * P:(j + 1) * P], ones[:, 0:1])
                return ins

            def late_rows(first, rows):
                for m, (l, n, bank) in enumerate(rows):
                    mm(PS[:, bank, :], ones, acc1[:, LATE_ADA.index((l, n)), :]).then_inc(sem("late_rows_summed"), 1)

            def small_rows(l, dsts):
                pe.wait_ge(sem("gw_split"), l + 1)
                n = 8 // len(dsts)
                for i, dst in enumerate(dsts):
                    c = slice(i * n, (i + 1) * n)
                    for k in range(KT):
                        ins = three(dst, gw_hi[:, k, c], gw_lo[:, k, c], hT_hi[:, k, :], hT_lo[:, k, :], k == 0, k == KT - 1)
                ins.then_inc(sem("gates_done"), 1)

            def token_quarter(w, q, banks):
                hi, lo = split_view(w)
                for i in range(NT):
                    for j in range(2):
                        k = 2 * q + j
                        ins = three(PS[:, banks[i], :], hT_hi[:, k, i * P:(i + 1) * P], hT_lo[:, k, i * P:(i + 1) * P],
                                    hi[:, j, :], lo[:, j, :], k == 0, k == KT - 1)
                return ins

            def feature_quarter(w, q, b):
                hi, lo = split_view(w)
                for j in range(2):
                    k = 2 * q + j
                    for f in range(4):
                        ins = three(PS[:, b + f // 2, (f % 2) * S:(f % 2 + 1) * S], hi[:, j, f * P:(f + 1) * P],
                                    lo[:, j, f * P:(f + 1) * P], hT_hi[:, k, :], hT_lo[:, k, :],
                                    k == 0 and f % 2 == 0, k == KT - 1)
                return ins

            def piece_free(l, n):
                if n < 2:
                    return
                m = n - 2
                if m < 2:
                    pe.wait_ge(sem("conv_done"), 2 * l + m + 1)
                else:
                    pe.wait_ge(sem("in_out"), 5 * l + m - 1)

            def mlstm_logits(l, h):
                n = H * l + h
                if h >= 1:
                    pe.wait_ge(sem("sw_done"), n)
                else:
                    pe.wait_ge(sem("qk_ready"), 2 * (l + 1))
                    if l == 0:
                        pe.wait_ge(sem("ada_taken"), ADA_EARLY)
                    else:
                        pe.wait_ge(sem("late_rows_taken"), 6)
                nm = grows[:, 0, :]
                hs = headsel[:, h * P:(h + 1) * P]
                mm(PS[:, 4, 0:S], hs, nm, True, False)
                mm(PS[:, 4, 0:P], ident, negm, False, True)
                mm(PS[:, 4, S:384], hs, nm[:, P:S], False, False)
                mm(PS[:, 4, S:384], ident, negm, False, True).then_inc(sem("decay_logits"), 1)
                mm(PS[:, 5, 0:S], qk[:, H + h, 0:P], qk[:, h, :])
                mm(PS[:, 5, S:384], qk[:, H + h, P:S], qk[:, h, P:S]).then_inc(sem("mqk_done"), 1)

            def mlstm_sums(l, h):
                pe.wait_ge(sem("sw_done"), H * l + h + 1)
                if h == 0:
                    pe.wait_ge(sem("gate_cols_copied"), l + 1)
                    pe.wait_ge(sem("in_out"), 5 * l + 1)
                vh = lambda i: mv[:, i, h * P:(h + 1) * P]
                for i in range(NT):
                    for dst, rhs in ((PS[:, 6 + i, h * P:(h + 1) * P], vh),
                                     (PS[:, 5, 384 + 4 * i + h:385 + 4 * i + h], lambda _: ones[:, 0:1])):
                        if i == 0:
                            ins = mm(dst, Sw[:, 0:P], rhs(0))
                        else:
                            mm(dst, Sw[:, P:S], rhs(0), True, False)
                            ins = mm(dst, Sw[:, S:384], rhs(1), False, True)
                ins.then_inc(sem("mlstm_sums"), 1)

            def scores(l, h):
                if h >= 2:
                    pe.wait_ge(sem("exp_done"), H * l + h - 1)
                elif h == 1:
                    pe.wait_ge(sem("num_taken"), NT * (l + 1))
                elif l == 0:
                    pe.wait_ge(sem("bias_loaded"), 16 * H)
                for cc in range(2):
                    a, b = slice(cc * DH, (cc + 1) * DH), score_bank(h) + cc
                    mm(PS[:, b, 0:P], ident, biasT[:, h, P:S], True, False)
                    mm(PS[:, b, P:384], ident, biasT[:, h, :], False, False)
                    mm(PS[:, b, 0:P], aqT[a, h, 0:P], akT[a, h, 0:P], False, True)
                    ins = mm(PS[:, b, P:384], aqT[a, h, P:S], akT[a, h, :], False, True)
                ins.then_inc(sem("scores_done"), 1)

            def turn_probs(l, h):
                pe.wait_ge(sem("exp_done"), H * l + h + 1)
                for cc in range(2):
                    for j in range(3):
                        ins = nc.tensor.transpose(PS[:, 2 + cc, j * P:(j + 1) * P],
                                                  pr[:, h % 2, cc, j * P:(j + 1) * P], ident)
                ins.then_inc(sem("probs_turned"), 1)

            def attn_sums(l, h):
                pe.wait_ge(sem("aT_ready"), H * l + h + 1)
                if h >= 2:
                    pe.wait_ge(sem("head_mixed"), H * l + h - 1)
                vh = lambda i: av[:, i, h * P:(h + 1) * P]
                for cc in range(2):
                    o = PS[:, 4 + h % 2, 2 * cc * P:2 * (cc + 1) * P]
                    mm(o[:, 0:P], aT[:, cc, 0:P], vh(0))
                    mm(o[:, P:S], aT[:, cc, P:S], vh(0), True, False)
                    ins = mm(o[:, P:S], aT[:, cc, S:384], vh(1), False, True)
                ins.then_inc(sem("attn_out"), 1)

            def mixer(l):
                for n, (name, _) in enumerate(W_IN):
                    piece_free(l, n)
                    b = 2 * (n % 2)
                    for q in range(4):
                        for h in range(H):
                            if 4 * (n - 4) + q == DECAY_AT[h]:
                                mlstm_logits(l, h)
                            if 4 * (n - 4) + q == DECAY_AT[h] + 1:
                                mlstm_sums(l, h)
                        w = SPLIT_AT[("in", l, n), q]
                        pe.wait_ge(sem("raw_used"), RAW_AT[("in", l, n), q] + 1)
                        if n == 0:
                            split_ready(q)
                        if name in FEATURE_MAJOR:
                            ins = feature_quarter(w, q, b)
                        else:
                            ins = token_quarter(w, q, (b, b + 1))
                        ins.then_inc(sem("w_used"), 1)
                    if n == 0:
                        small_rows(l, [PS[0:H, 7, 0:S], PS[0:H, 7, S:2 * S]])
                    if l == 0 and n == 2:
                        ada_reduce(4)
                    if n == 3:
                        pe.wait_ge(sem("gate_ready"), l + 1)
                        for i in range(NT):
                            mm(PS[:, 7, 8 * i:8 * i + 4], grows[:, 4, i * P:(i + 1) * P], ident[0:H, 0:H])
                            ins = mm(PS[:, 7, 8 * i + 4:8 * i + 8], grows[:, 6, i * P:(i + 1) * P], ident[0:H, 0:H])
                        ins.then_inc(sem("gate_cols"), 1)
                pe.wait_ge(sem("in_out"), 5 * (l + 1))
                scores(l, 0)
                scores(l, 1)
                for h in range(H):
                    turn_probs(l, h)
                    if h + 2 < H:
                        scores(l, h + 2)
                    attn_sums(l, h)
                turn("mixed_ready", (NT * l + 1, NT * l + 2))
                for n in range(2):
                    for q in range(4):
                        w = SPLIT_AT[("out", l, n), q]
                        pe.wait_ge(sem("raw_used"), RAW_AT[("out", l, n), q] + 1)
                        if n == 0:
                            split_ready(q)
                        token_quarter(w, q, (4 + n, 6 + n)).then_inc(sem("w_used"), 1)
                    if l == 0 and n == 0:
                        for m in ADA_ORDER[ADA_EARLY:]:
                            ada_reduce(m)
                turn("xn_ready", (4 * l + 3, 4 * l + 4))

            def hidden_quarter(ps, q):
                what, ch = GROUPS[q // 4]
                qq = q % 4
                w = ps.split_static(q)
                pe.wait_ge(sem("raw_used"), ps.raw(q))
                if ps.e is None and q < 4:
                    split_ready(q)
                if qq == 0 and what == "gate" and ch == 1:
                    pe.wait_ge(sem("silu_done"), ps.chunk(0))
                if qq == 0 and what == "up" and ch > 0:
                    pe.wait_ge(sem("sT_lo_done"), ps.chunk(ch - 1))
                if qq == 0 and what == "down" and ch == NCH - 1:
                    pe.wait_ge(sem("sT_lo_done"), ps.chunk(ch))
                if what == "down":
                    for b in range(ps.blocks):
                        for n in range(2):
                            ins = three(PS[:, 4 + 2 * b + n, :], sT_hi[:, qq, b * P:(b + 1) * P], sT_lo[:, qq, b * P:(b + 1) * P],
                                        w_hi[:, w % SPLIT, n * NC:(n + 1) * NC], w_lo[:, w % SPLIT, n * NC:(n + 1) * NC],
                                        ch == 0 and qq == 0, ch == NCH - 1 and qq == 3)
                else:
                    hi, lo = split_view(w)
                    for b in range(ps.blocks):
                        bank = ps.gate_bank(b) if what == "gate" else ps.up_bank(b)
                        for j in range(2):
                            k = 2 * qq + j
                            ins = three(PS[:, bank, :], hT_hi[:, k, b * P:(b + 1) * P], hT_lo[:, k, b * P:(b + 1) * P],
                                        hi[:, j, :], lo[:, j, :], k == 0, k == KT - 1)
                ins.then_inc(sem("w_used"), 1)
                for c2 in range(NCH):
                    if q == turn_after(c2):
                        pe.wait_ge(sem("hidden_ready"), ps.chunk(c2))
                        for b in range(ps.blocks):
                            for f in range(4):
                                ins = nc.tensor.transpose(PS[:, ps.up_bank(b), f * P:(f + 1) * P],
                                                          hidden[:, b, f * P:(f + 1) * P], ident)
                        ins.then_inc(sem("hidden_turned"), 1)

            pe.wait_ge(sem("tables_loaded"), 16)
            pe.wait_ge(sem("rows_loaded"), 16 * 6)
            for t, n in ((0, 128), (1, 112), (2, 10)):
                ins = nc.tensor.transpose(PS[:, 4, t * P:t * P + n], tabs[0:n, t, :], ident[0:n, 0:n])
            ins.then_inc(sem("cols_turned"), 1)
            pe.wait_ge(sem("relb_ready"), 1)
            for h in range(H):
                ins = mm(PS[:, h, 0:384], relb[:, h, :], onehot)
            ins.then_inc(sem("bias_rows"), 1)
            pe.wait_ge(sem("bias_rows_copied"), 1)
            turn("xn_ready", (1, 2))
            pe.wait_ge(sem("cols_ready"), 1)
            for n in range(4):
                ada_reduce(n)
            mixer(0)
            for q in range(PASS_Q):
                hidden_quarter(dense, q)
            pe.wait_ge(sem("raw_used"), RAW_AT[("in", 1, 0), 0])
            pe.wait_ge(sem("sT_lo_done"), NCH)
            late_rows(0, ((0, 10, 1), (0, 11, 2)))
            pe.wait_ge(sem("pool_added"), (KT - 1) * (len(POOL_ADA) + len(LATE_POOL)))
            for n in (0, 1, 2, 3, 6, 7, 8, 9):
                ins = columns(acc1[:, LATE_ADA.index((1, n)), :], n, 0)
            ins.then_inc(sem("late_cols_summed"), 1)
            late_rows(2, ((1, 4, 3),))
            pe.wait_ge(sem("x_added"), 4)
            late_rows(3, ((1, 5, 4), (1, 10, 5), (1, 11, 7)))
            turn("xn_ready", (5, 6))
            mixer(1)
            split_ready()
            small_rows(2, [PS[0:NE, 6, 0:S]])
            pe.wait_ge(sem("logit_rows"), 1)
            for i in range(NT):
                ins = nc.tensor.transpose(PS[:, 7, 8 * i:8 * i + 8], lgT[:, i * P:(i + 1) * P], ident[0:NE, 0:NE])
            ins.then_inc(sem("logits_turned"), 1)
            pe.wait_ge(sem("sel_ready"), 1)
            mm(PS[:, 6, 16:24], before, sel[:, 0, 0:NE])
            mm(PS[:, 6, 24:32], ones, sel[:, 0, 0:NE], True, False)
            mm(PS[:, 6, 24:32], before, sel[:, 1, 0:NE], False, True)
            mm(PS[:, 6, 32:40], ones, sel[:, 0, 0:NE], True, False)
            mm(PS[:, 6, 32:40], ones, sel[:, 1, 0:NE], False, True).then_inc(sem("ranks_done"), 1)

            def gather():
                for k in range(KT):
                    for i in range(NT):
                        ins = mm(PS[:, 2 + k // 4, (k % 4) * P:(k % 4 + 1) * P], xn[:, i, k * P:(k + 1) * P], disp[:, i, :],
                                 k % 4 == 0 and i == 0, i == NT - 1)
                ins.then_inc(sem("gathered"), 1)

            def scatter():
                for i in range(NT):
                    for n in range(2):
                        ins = mm(PS[:, (6 if i == 0 else 2) + n, :], combT[:, i * P:(i + 1) * P], ye_sb[:, n * NC:(n + 1) * NC])
                ins.then_inc(sem("scattered"), 1)

            def moe_round(r):
                g0 = (NE + 1) * r
                if r:
                    pe.wait_ge(sem("y_added"), g0)
                pe.wait_ge(sem("disp_ready"), g0 + 1)
                gather()
                pe.wait_ge(sem("zeros_ready"), r + 1)
                for n in range(2):
                    for j in range(2):
                        mm(PS[:, 4 + n, j * S:(j + 1) * S], combT[:, 0:P], combT)
                with pe.Fori(0, NE) as e:
                    ps = moe_pass(e, r)
                    pe.wait_ge(sem("xT_ready"), e + g0 + 1)
                    for q in range(PASS_Q):
                        if q == 5:
                            pe.wait_ge(sem("ye_ready"), e + g0 + 1)
                            scatter()
                        if q == 20:
                            pe.wait_ge(sem("comb_ready"), ps.expert())
                            pe.wait_ge(sem("y_added"), e + g0 + 1)
                            for i in range(NT):
                                ins = nc.tensor.transpose(PS[:, 6, i * P:(i + 1) * P], comb[:, i, :], ident)
                            ins.then_inc(sem("comb_turned"), 1)
                        if q == 48:
                            pe.wait_ge(sem("disp_ready"), e + g0 + 2)
                            gather()
                        hidden_quarter(ps, q)
                pe.wait_ge(sem("ye_ready"), g0 + NE + 1)
                scatter()

            moe_round(0)
            pe.wait_ge(sem("flag_ready"), 1)
            over = pe.value_load(flag[0:1, 0:1], min_val=0, max_val=1)
            with pe.If(over > 0):
                moe_round(1)
            pe.wait_ge(sem("y_complete"), 1)


_INS = ["x", "c", "rel_bias", "ada_w", "ada_b", "norm_g", "w_in", "gate_b", "conv_w", "conv_b", "lam_vec",
        "attn_norm_g", "mlstm_norm_g", "w_out", "ffn_w1", "ffn_w3", "ffn_w2", "router_w", "moe_w1", "moe_w3", "moe_w2"]


def kernel(**inputs):
    import concourse.bacc as bacc
    from concourse.bass_utils import run_bass_kernel_spmd

    nc = bacc.Bacc("TRN2", target_bir_lowering=False, num_devices=1)
    arrays, args = {}, []
    for name in _INS + ["tables"]:
        a = shape_constants() if name == "tables" else np.ascontiguousarray(inputs[name])
        arrays[f"in_{name}"] = a
        args.append(nc.dram_tensor(f"in_{name}", a.shape, mybir.dt.from_np(a.dtype), kind="ExternalInput").ap())
    args.append(nc.dram_tensor("out_0", (1, S, D), F32, kind="ExternalOutput").ap())
    trunk(nc, *args)
    r = run_bass_kernel_spmd(nc, [arrays], core_ids=[0])
    return r.results[0]["out_0"]
```

```python
import math
from contextlib import ExitStack

import numpy as np
import concourse.bass as bass
from concourse import mybir

F32 = mybir.dt.float32
F32R = mybir.dt.float32r
I32 = mybir.dt.int32
U32 = mybir.dt.uint32
ACT = mybir.ActivationFunctionType
ALU = mybir.AluOpType
AX = mybir.AxisListType.X

P = 128
S = 256
NT = S // P
D = 1024
KT = D // P
L = 2
H = 4
DH = 64
DFF = 3584
NE = 8
NC = 512
NCH = DFF // NC
N_BUCKETS, MAX_DIST = 32, 128
EPS = 1e-6
NEG = -1e30

RAW = 14
MOE_RAW = 21
SPLIT = 4
QW = 1024

GROUPS = [("gate", 0), ("up", 0)]
for _c in range(1, NCH):
    GROUPS += [("gate", _c), ("up", _c), ("down", _c - 1)]
GROUPS += [("down", NCH - 1)]
PASS_Q = 4 * len(GROUPS)
LAST_Q = {g: 4 * i + 3 for i, g in enumerate(GROUPS)}
assert PASS_Q % MOE_RAW == 0 and PASS_Q % SPLIT == 0


def turn_after(c, blocks):
    if c == 0:
        return LAST_Q[("gate", 1)]
    return LAST_Q[("down", c - 1)] - (2 if blocks == 1 else 0)


W_IN = [("mq", 1536), ("mk", 2048), ("mv", 2560), ("mo", 3072), ("aq", 0), ("ak", 512), ("av", 1024)]
GATE_COL = 3584
FEATURE_MAJOR = ("mq", "mk", "aq", "ak")

AHEAD = SPLIT - 1

DECAY_AT = (1, 3, 5, 7)

ADA_BESIDE = {1: 4, 4: 5, 5: 6, 6: 9}
POOL_ADA = (7, 8)
ADA_ORDER = [0, 1, 2, 3, 4, 7, 8, 9, 6, 5]
ADA_EARLY = 5
LATE_ADA = [(0, 10), (0, 11)] + [(1, n) for n in range(12)]
LATE_POOL = LATE_ADA[8:]
LATE_BESIDE = (1, 3, 6, 8, 11, 13, 15, 17)
TURNS = 4 * 6


LATE_ROWS_1 = [(4, 4, 0, 1, 3), (5, 5, 0, 1, 4), (10, 6, 2, 3, 5), (11, 6, 2, 3, 16)]


def plan():
    late = iter(LATE_ADA)
    for n in range(4):
        for q in range(4):
            yield ("ada", 0, n), q
    for l in range(L):
        for n in range(len(W_IN)):
            for q in range(4):
                if l == 0 and n in ADA_BESIDE:
                    yield ("ada", 0, ADA_BESIDE[n]), q
                yield ("in", l, n), q
        for n in range(2):
            for q in range(4):
                yield ("out", l, n), q
        if l == 0:
            for i in range(len(GROUPS)):
                p = ("ada", *next(late)) if i in LATE_BESIDE else None
                for q in range(4):
                    yield ("ffn", 0, i), q
                    if p is not None:
                        yield p, q


PLAN = list(plan())
RAW_AT, SPLIT_AT = {}, {}
for _p, _q in PLAN:
    RAW_AT[_p, _q] = len(RAW_AT)
    if _p[0] != "ada":
        SPLIT_AT[_p, _q] = len(SPLIT_AT)
RAW_MOE, SPLIT_MOE = len(RAW_AT), len(SPLIT_AT)


def shape_constants():
    k = np.zeros((P, 1536), np.float32)
    p = np.arange(P)
    k[:, 0:128] = np.eye(P)
    k[:, 128:256] = np.where(p[:, None] > p[None, :], NEG, 0.0)
    k[:, 256:384] = (p[:, None] < p[None, :])
    k[:, 384:512] = p[None, :]
    k[:, 512:640] = 1.0
    dist = 255 - np.arange(384)
    n = np.maximum(dist, 0)
    exact = N_BUCKETS // 2
    nf = np.maximum(n, 1).astype(np.float32)
    large = exact + (np.log(nf / np.float32(exact)) / np.float32(math.log(MAX_DIST / exact))
                     * np.float32(N_BUCKETS - exact)).astype(np.int32)
    bucket = np.where(n < exact, n, np.minimum(large, N_BUCKETS - 1))
    for j in range(384):
        if dist[j] >= 0:
            k[bucket[j], 640 + j] = 1.0
        else:
            k[N_BUCKETS, 640 + j] = NEG
    for h in range(H):
        k[h, 1024 + h * P:1024 + (h + 1) * P] = 1.0
    return k


def trunk(nc, x, c, rel_bias, ada_w, ada_b, norm_g, w_in, gate_b, conv_w, conv_b, lam_vec, attn_norm_g,
          mlstm_norm_g, w_out, ffn_w1, ffn_w3, ffn_w2, router_w, moe_w1, moe_w3, moe_w2, tables, out):
    with ExitStack() as ctx:
        def sb(name, shape, dt=F32):
            return ctx.enter_context(nc.sbuf_tensor(name, shape, dt))

        sems = {}

        def sem(name):
            if name not in sems:
                sems[name] = ctx.enter_context(nc.semaphore(name))
            return sems[name]

        raw = sb("raw", [P, RAW, QW])
        w_hi = sb("w_hi", [P, SPLIT, QW], F32R)
        w_lo = sb("w_lo", [P, SPLIT, QW], F32R)
        hT_hi = sb("hT_hi", [P, KT, S], F32R)
        hT_lo = sb("hT_lo", [P, KT, S], F32R)
        sT_hi = sb("sT_hi", [P, 4, S], F32R)
        sT_lo = sb("sT_lo", [P, 4, S], F32R)
        xs = sb("xs", [P, NT, D])
        xn = sb("xn", [P, NT, D])
        K = sb("K", [P, 1536])
        grow = sb("grow", [P, 3, D])
        biasT = sb("biasT", [P, H, S])
        colT = sb("colT", [P, 3, P])
        cact = sb("cact", [P, KT])
        cT = sb("cT", [P, KT])
        modcol = sb("modcol", [P, 48])
        modA = sb("modA", [P, 2, KT])
        mixA = sb("mixA", [P, KT])
        gw = sb("gw", [P, KT, 8])
        gw_hi = sb("gw_hi", [P, KT, 8], F32R)
        gw_lo = sb("gw_lo", [P, KT, 8], F32R)
        gbias = sb("gbias", [H, 4])
        lamc = sb("lamc", [P, 8])
        eps = sb("eps", [P, 1])
        small = sb("small", [P, 64])
        att = sb("att", [P, H, 8])
        area = sb("area", [P, 13312])
        combT = sb("combT", [P, S], F32R)

        ident, negm, before, iota, ones = (K[:, i * P:(i + 1) * P] for i in range(5))
        onehot = K[0:N_BUCKETS + 1, 640:1024]
        headsel = K[0:H, 1024:1536]

        def part(at, *shape):
            n = int(np.prod(shape))
            v = area[:, at:at + n]
            if len(shape) == 2:
                v = v.rearrange("p (a b) -> p a b", a=shape[0])
            if len(shape) == 3:
                v = v.rearrange("p (a b c) -> p a b c", a=shape[0], b=shape[1])
            return v

        qk = part(0, 2 * H, S)
        aqT, akT = part(2048, H, S), part(3072, H, S)
        av, mv, so = part(4096, NT, NC), part(5120, NT, NC), part(6144, NT, NC)
        E = part(7168, 384)
        Sw = part(7552, 384)
        sq = part(7168, NC)
        sqh = part(7680, P)
        pr = part(8960, 2, 2, 384)
        aT = part(10496, 2, 384)
        grows = area[0:H, 8960:8960 + 8 * S].rearrange("p (a b) -> p a b", a=8)
        hidden = part(7168, NT, NC)
        htmp = part(5120, 2, NC)
        acc0 = [part(at, NC) for at in (4096, 4608, 6144, 6656)]
        acc9 = part(7936, NC)
        acc56 = grow[:, 1, :].rearrange("p (a b) -> p a b", a=2)
        accp = grow[:, 2, :].rearrange("p (a b) -> p a b", a=2)
        acc1 = part(0, len(LATE_ADA), NC)
        pool_w = part(11264, 2, NC)
        pool_t = part(8448, NC)
        ytmp0 = part(6144, D)
        ytmp1 = part(8192, D)
        ngb = part(9216, 4, D)
        tabs = part(9216, 3, P)
        lamrow = part(9728, 8, DH)
        brows = part(0, H, 384)
        relb = area[0:N_BUCKETS + 1, 2048:2560].rearrange("p (a b) -> p a b", a=H)
        lamp = part(2560, 4, DH)
        y_sb = part(0, NT, D)
        junk = part(2048, D)
        xg = part(3072, D)
        disp = part(4096, NT, P)
        comb = part(4352, NT, P)
        ye_hi, ye_lo = hT_hi[:, :, P:S], hT_lo[:, :, P:S]
        lgT = area[0:NE, 4096:4096 + S]
        routing = sb("routing", [P, 160])
        midx = sb("midx", [P, NT, 8], U32)
        flag = sb("flag", [P, 1], I32)
        ranks = routing[:, 0:18].rearrange("p (a b) -> p a b", a=NT)
        sel = routing[:, 18:36].rearrange("p (a b) -> p a b", a=NT)
        gates = routing[:, 36:54].rearrange("p (a b) -> p a b", a=NT)
        lg = routing[:, 54:70].rearrange("p (a b) -> p a b", a=NT)
        top = routing[:, 70:86].rearrange("p (a b) -> p a b", a=NT)
        topi = routing[:, 86:102].rearrange("p (a b) -> p a b", a=NT)
        pick = routing[:, 102:134].rearrange("p (n a b) -> p n a b", n=2, a=NT)
        tw = routing[:, 134:150]
        acol = sb("acol", [P, NT, 8])
        gcur = sb("gcur", [P, 4])
        mstat = sb("mstat", [P, 24])
        dn, msq, mroot = mstat[:, 0:8], mstat[:, 8:16], mstat[:, 16:24]

        PS = ctx.enter_context(nc.psum_tensor("PS", [P, 8, 512], F32))
        scratch = nc.dram_tensor("bias_rows_dram", [H, P, 384], F32)

        def source(p, q):
            kind, l, n = p
            if kind == "ada":
                return ada_w[l].rearrange("(k p) n -> p k n", p=P)[:, 2 * q:2 * q + 2, n * NC:(n + 1) * NC]
            if kind == "in":
                at = W_IN[n][1]
                return w_in[l].rearrange("(k p) n -> p k n", p=P)[:, 2 * q:2 * q + 2, at:at + NC]
            if kind == "out":
                return w_out[l].rearrange("(k p) n -> p k n", p=P)[:, 2 * q:2 * q + 2, n * NC:(n + 1) * NC]
            return hidden_source(ffn_w1[0], ffn_w3[0], ffn_w2[0], n, q)

        def hidden_source(w1, w3, w2, n, q):
            what, ch = GROUPS[n]
            if what == "down":
                return w2[ch * NC + q * P:ch * NC + (q + 1) * P, :]
            w = w1 if what == "gate" else w3
            return w.rearrange("(k p) n -> p k n", p=P)[:, 2 * q:2 * q + 2, ch * NC:(ch + 1) * NC]

        def raw_slot(i, wide):
            v = raw[:, i % RAW, :]
            return v if wide else v.rearrange("p (k n) -> p k n", k=2)

        moe_extra = [part(at, QW) for at in (4864, 5888, 7680, 8704, 9728, 10752, 11776)]

        def moe_slot(q):
            s = q % MOE_RAW
            return raw[:, s, :] if s < RAW else moe_extra[s - RAW]

        def score_bank(h):
            return 6 * (h % 2)

        class Pass:

            def __init__(self, blocks, chunks_before, e=None, round_=0):
                self.blocks, self.e, self.round = blocks, e, round_
                self.chunks_before = chunks_before

            def _v(self, base, per):
                base += per * NE * self.round
                return base if self.e is None else self.e * per + base

            def raw(self, q):
                if self.e is None:
                    return RAW_AT[("ffn", 0, q // 4), q % 4] + 1
                return self._v(RAW_MOE + q + 1, PASS_Q)

            def moe_loaded(self, q):
                return self._v(16 * (q // MOE_RAW + 1), 16 * PASS_Q // MOE_RAW)

            def split(self, q):
                if self.e is None:
                    return SPLIT_AT[("ffn", 0, q // 4), q % 4] + 1
                return self._v(SPLIT_MOE + q + 1, PASS_Q)

            def split_static(self, q):
                return (SPLIT_AT[("ffn", 0, 0), 0] if self.e is None else SPLIT_MOE) + q

            def chunk(self, ch):
                return self._v(self.chunks_before + ch + 1, NCH)

            def expert(self, n=1):
                return self._v(n, 1)

            def blocks_of(self, tile):
                return range(self.blocks) if tile is None else [tile]

            def turned_cols(self, ch, b):
                at = (b if self.blocks == 2 else ch % 2) * P
                return slice(at, at + P)

            def gate_bank(self, b):
                return b if self.blocks == 2 else 0

            def up_bank(self, b):
                return 2 + b if self.blocks == 2 else 1

            def turn_bank(self, b):
                return 2 + b if self.blocks == 2 else 7

        dense = Pass(NT, 0)

        def moe_pass(e, r):
            return Pass(1, NCH, e, r)

        def gw_load(eng, n):
            w = w_in[n].rearrange("(k p) n -> p k n", p=P)[:, :, GATE_COL:GATE_COL + 8] if n < L else \
                router_w[0].rearrange("(k p) n -> p k n", p=P)
            eng.dma_start(gw[:], w).then_inc(sem("gw_loaded"), 16)

        block = ctx.enter_context(nc.Block())

        @block.sync
        def _(sync):
            for r, (p, q) in enumerate(PLAN):
                if r >= RAW:
                    sync.wait_ge(sem("raw_used"), r - RAW + 1)
                wide = p[0] == "ffn" and GROUPS[p[2]][0] == "down"
                sync.dma_start(raw_slot(r, wide), source(p, q)).then_inc(sem(f"raw_loaded{r % RAW}"), 16)

            def expert_load(e, q, free):
                w1, w3, w2 = (w[0, bass.ds(e, 1)].rearrange("o a b -> (o a) b") for w in (moe_w1, moe_w3, moe_w2))
                what = GROUPS[q // 4][0]
                dst = moe_slot(q) if what == "down" else moe_slot(q).rearrange("p (k n) -> p k n", k=2)
                sync.wait_ge(sem("raw_used"), free)
                sync.dma_start(dst, hidden_source(w1, w3, w2, q // 4, q % 4)
                               ).then_inc(sem(f"moe_loaded{q % MOE_RAW}"), 16)

            def moe_round(r):
                base = RAW_MOE + r * NE * PASS_Q
                for q in range(MOE_RAW):
                    if r == 0 and q < RAW:
                        free = RAW_MOE - (RAW_MOE - 1 - q) % RAW
                    elif r == 0:
                        if q == RAW:
                            sync.wait_ge(sem("hT_lo_done"), TURNS)
                        free = RAW_MOE
                    else:
                        free = base + q - MOE_RAW + 1
                    expert_load(0, q, free)
                with sync.Fori(0, NE - 1) as e:
                    for q in range(MOE_RAW, PASS_Q):
                        expert_load(e, q, e * PASS_Q + (base + q - MOE_RAW + 1))
                    for q in range(MOE_RAW):
                        expert_load(e + 1, q, e * PASS_Q + (base + PASS_Q + q - MOE_RAW + 1))
                for q in range(MOE_RAW, PASS_Q):
                    expert_load(NE - 1, q, base + (NE - 1) * PASS_Q + q - MOE_RAW + 1)

            moe_round(0)
            sync.wait_ge(sem("flag_ready"), 1)
            over = sync.value_load(flag[0:1, 0:1], min_val=0, max_val=1)
            with sync.If(over > 0):
                moe_round(1)
            for i in range(NT):
                sync.wait_ge(sem("x_final"), i + 1)
                sync.dma_start(out[0, i * P:(i + 1) * P, :], xs[:, i, :]).then_inc(sem("out_stored"), 16)
            sync.wait_ge(sem("out_stored"), 16 * NT)

        @block.gpsimd
        def _(pool):
            pool.dma_start(lamc[0:N_BUCKETS, 4:4 + H], rel_bias).then_inc(sem("rel_loaded"), 16)
            gw_load(pool, 0)
            pool.dma_start(lamrow, lam_vec.rearrange("l f d -> (l f) d").partition_broadcast(P)
                           ).then_inc(sem("lam_loaded"), 16)
            pool.dma_start(gbias[:], gate_b.rearrange("l t h -> h (l t)"), allow_slow_non_contiguous=True
                           ).then_inc(sem("gbias_loaded"), 16)

            def gate_row_loads(l, sub, g, n):
                at = (2 + 3 * sub) * D
                pool.dma_start(grow[:, g, :], ada_b[l, at:at + D].partition_broadcast(P)
                               ).then_inc(sem(f"grow_loaded{2 * l + sub}"), 16)
                pool.dma_start(ngb[:, n, :], norm_g[l, 1 + 2 * sub, :].partition_broadcast(P)
                               ).then_inc(sem(f"grow_loaded{2 * l + sub}"), 16)

            pieces = [(0, n, accp[:, m, :]) for m, n in enumerate(POOL_ADA)]
            pieces += [(l, n, acc1[:, LATE_ADA.index((l, n)), :]) for l, n in LATE_POOL]

            def ada_row(i):
                (l, n, _), k = pieces[i // KT], i % KT
                pool.dma_start(pool_w[:, i % 2, :], ada_w[l, k * P:(k + 1) * P, n * NC:(n + 1) * NC]
                               ).then_inc(sem(f"pool_loaded{i % 2}"), 16)

            def ada_sums(first, last):
                for i in range(first * KT, last * KT):
                    m, k = i // KT, i % KT
                    row, acc = pool_w[:, i % 2, :], pieces[m][2]
                    pool.wait_ge(sem(f"pool_loaded{i % 2}"), 16 * (i // 2 + 1))
                    nc.gpsimd.tensor_scalar(pool_t if k else acc, row, cact[:, k:k + 1], None, ALU.mult
                                            ).then_inc(sem("pool_scaled"), 1)
                    pool.wait_ge(sem("pool_scaled"), i + 1)
                    if i + 2 < KT * len(pieces):
                        ada_row(i + 2)
                    if k:
                        nc.gpsimd.tensor_tensor(acc, acc, pool_t, ALU.add).then_inc(sem("pool_added"), 1)
                        pool.wait_ge(sem("pool_added"), i - m)

            pool.wait_ge(sem("bias_rows_copied"), 1)
            pool.dma_start(scratch[:, :, :].rearrange("h p n -> p h n"), brows).then_inc(sem("bias_stored"), 16)
            pool.wait_ge(sem("bias_stored"), 16)
            for h in range(H):
                skew = bass.AP(scratch, h * P * 384 + P - 1, [[383, P], [1, S]])
                pool.dma_start(biasT[:, h, :], skew).then_inc(sem("bias_loaded"), 16)
            pool.wait_ge(sem("ada_taken"), 4)
            for i in range(2):
                ada_row(i)
            gate_row_loads(0, 0, 0, 3)
            ada_sums(0, len(POOL_ADA))
            pool.wait_ge(sem("gw_split"), 1)
            gw_load(pool, 1)
            pool.wait_ge(sem("x_added"), 2)
            gate_row_loads(0, 1, 1, 0)
            gate_row_loads(1, 0, 0, 1)
            gate_row_loads(1, 1, 2, 3)
            pool.wait_ge(sem("hT_lo_done"), 12)
            ada_sums(len(POOL_ADA), len(pieces))
            pool.wait_ge(sem("gw_split"), 2)
            gw_load(pool, 2)

        @block.scalar
        def _(act):
            act.dma_start(cT[:], c.rearrange("b (n p) -> p (b n)", p=P), allow_slow_non_contiguous=True
                          ).then_inc(sem("c_loaded"), 16)
            act.dma_start(K[:], tables).then_inc(sem("tables_loaded"), 16)
            for i in range(NT):
                act.dma_start(xs[:, i, :], x[0, i * P:(i + 1) * P, :]).then_inc(sem(f"x_loaded{i}"), 16)
            done = [0]

            def after(ins):
                done[0] += 1
                ins.then_inc(sem("act_step"), 1)
                act.wait_ge(sem("act_step"), done[0])

            def hi_quarter(src, w, w_free):
                if w_free is not None:
                    act.wait_ge(sem("w_used"), w_free)
                nc.scalar.activation(w_hi[:, w % SPLIT, :], src, ACT.Copy).then_inc(sem("hi_ready"), 1)

            def plan_quarter(p, q):
                w = SPLIT_AT[p, q]
                r = RAW_AT[p, q]
                act.wait_ge(sem(f"raw_loaded{r % RAW}"), 16 * (r // RAW + 1))
                hi_quarter(raw[:, r % RAW, :], w, w - SPLIT + 1 if w >= SPLIT else None)

            def ahead(p):
                for q in range(AHEAD):
                    plan_quarter(p, q)

            def root(dst, src, n, scale):
                nc.scalar.activation(dst, src, ACT.Sqrt, bias=eps[:, 0:1], scale=scale).then_inc(sem("root_done"), 1)

            roots = [0]

            def norm_token(src, junk, i):
                after(nc.scalar.activation(junk, src, ACT.Square, accum_out=small[:, i:i + 1]))
                roots[0] += 1
                root(small[:, 2 + i:3 + i], small[:, i:i + 1], roots[0], 1.0 / D)

            def between_layers(k, last, following):
                for i in range(NT):
                    if i == 0:
                        act.wait_ge(sem("y_first"), k + 1)
                    else:
                        act.wait_ge(sem("w_used"), last)
                    junk = xn[:, i, :]
                    norm_token(PS[:, 4 + 2 * i:6 + 2 * i, :], junk.rearrange("p (a b) -> p a b", a=2), i)
                    if following is not None:
                        plan_quarter(following, 2 * i)
                    act.wait_ge(sem("x_added"), NT * k + i + 1)
                    norm_token(xs[:, i, :], junk, i)
                    if following is not None and i == 0:
                        plan_quarter(following, 1)

            def fetch_sqrt():
                nc.scalar.activation(small[:, 60:61], eps[:, 0:1], ACT.Sqrt)

            turns = [0]

            def split_turned(scale, bias, taken=None):
                if taken is not None:
                    act.wait_ge(sem(taken[0]), taken[1])
                for b in range(4):
                    turns[0] += 1
                    t = turns[0]
                    act.wait_ge(sem("turned"), t)
                    if t > 2:
                        act.wait_ge(sem("hT_lo_done"), t - 2)
                    for j in range(2):
                        k = 2 * b + j
                        ins = nc.scalar.activation(htmp[:, b % 2, j * S:(j + 1) * S], PS[:, b, j * S:(j + 1) * S],
                                                   ACT.Identity, bias=bias(k), scale=scale(k))
                    after(ins)
                    nc.scalar.activation(hT_hi[:, 2 * b:2 * b + 2, :], htmp[:, b % 2, :].rearrange("p (k n) -> p k n", k=2),
                                         ACT.Copy).then_inc(sem("hT_hi_done"), 1)

            act.wait_ge(sem("c_loaded"), 16)
            nc.scalar.activation(cact[:], cT[:], ACT.Silu).then_inc(sem("cact_ready"), 1)
            for src, t, at in (
                (attn_norm_g, 2, 0),
                (mlstm_norm_g.rearrange("l (n p) -> (l n) p", p=P), 2, 2),
                (norm_g.rearrange("l f (n p) -> (l f n) p", p=P), 0, 0),
                (ada_b.rearrange("l (n p) -> (l n) p", p=P), 1, 0),
                (conv_w.rearrange("l f (n p) -> (l f n) p", p=P), 0, 64),
                (conv_b.rearrange("l (n p) -> (l n) p", p=P), 1, 96),
            ):
                n = src.shape[0]
                act.dma_start(tabs[at:at + n, t, :], src).then_inc(sem("rows_loaded"), 16)
            act.wait_ge(sem("eps_ready"), 1)
            for i in range(NT):
                act.wait_ge(sem(f"x_loaded{i}"), 16)
                norm_token(xs[:, i, :], xn[:, i, :], i)
            act.wait_ge(sem("bias_rows"), 1)
            nc.scalar.activation(brows, PS[:, 4:8, 0:384], ACT.Copy).then_inc(sem("bias_rows_copied"), 1)
            act.wait_ge(sem("cols_turned"), 1)
            after(nc.scalar.activation(colT[:].rearrange("p a b -> p (a b)")[:, 0:240], PS[:, 4, 0:240], ACT.Copy))
            nc.scalar.activation(colT[:, 2, 0:10], PS[:, 4, 2 * P:2 * P + 10], ACT.Copy).then_inc(sem("cols_ready"), 1)
            act.wait_ge(sem("lam_sums"), 1)
            nc.scalar.activation(lamc[:, 0:4], small[:, 8:12], ACT.Exp).then_inc(sem("lam_exp"), 1)

            def evacuate(l, n):
                name = W_IN[n][0]
                b = 2 * (n % 2)
                act.wait_ge(sem("w_used"), SPLIT_AT[("in", l, n), 3] + 1)
                two = PS[:, b:b + 2, :]
                if name == "aq":
                    ins = nc.scalar.activation(aqT.rearrange("p a b -> p (a b)").rearrange("p (a b) -> p a b", a=2),
                                               two, ACT.Copy, scale=float(DH) ** -0.5)
                elif name == "ak":
                    ins = nc.scalar.activation(akT.rearrange("p a b -> p (a b)").rearrange("p (a b) -> p a b", a=2),
                                               two, ACT.Copy)
                else:
                    dst = {"av": av, "mv": mv, "mo": so}[name]
                    ins = nc.scalar.activation(dst, two, ACT.Sigmoid if name == "mo" else ACT.Copy)
                ins.then_inc(sem("in_out"), 1)

            def silu_conv(l, half):
                act.wait_ge(sem("conv_done"), 2 * l + half + 1)
                v = qk[:, 4 * half:4 * half + 4, :]
                nc.scalar.activation(v, v, ACT.Silu).then_inc(sem("qk_ready"), 1)

            def log_forget(l):
                z, t = grows[:, 1, :], grows[:, 2, :]
                act.wait_ge(sem("gate_pre"), l + 1)
                after(nc.scalar.activation(t, z, ACT.Abs))
                after(nc.scalar.activation(t, t, ACT.Exp, scale=-1.0))
                nc.scalar.activation(t, t, ACT.Ln, bias=1.0).then_inc(sem("log_done"), 1)

            def decay(l, h):
                n = H * l + h
                act.wait_ge(sem("decay_logits"), n + 1)
                if n == H * l:
                    act.wait_ge(sem("gate_cols_copied"), l + 1)
                nc.scalar.activation(E[:, 0:S], PS[:, 4, 0:S], ACT.Exp, bias=acol[:, 0, h:h + 1])
                nc.scalar.activation(E[:, S:384], PS[:, 4, S:384], ACT.Exp,
                                     bias=acol[:, 1, h:h + 1]).then_inc(sem("decay_done"), 1)

            def mixer(l):
                for n in range(len(W_IN)):
                    for q in range(4):
                        if q == 3 and n > 2:
                            evacuate(l, n - 1)
                        if q == 0 and n in (3, 4):
                            silu_conv(l, n - 3)
                        if q == 1 and n == 2:
                            log_forget(l)
                        for h in range(H):
                            if 4 * (n - 4) + q == DECAY_AT[h] + 3:
                                decay(l, h)
                        if n or q >= AHEAD:
                            plan_quarter(("in", l, n), q)
                ahead(("out", l, 0))
                evacuate(l, len(W_IN) - 1)
                nc.scalar.activation(acol[:, :, 4:8], acol[:, :, 4:8], ACT.Exp, scale=-1.0).then_inc(sem("floor_ready"), 1)
                for h in range(H + 2):
                    if h < H:
                        n = H * l + h
                        act.wait_ge(sem("scores_max"), n + 1)
                        if n >= 2:
                            act.wait_ge(sem("probs_turned"), n - 1)
                        for cc in range(2):
                            for i in range(NT):
                                o, w = (0, P) if i == 0 else (P, S)
                                at = 2 * cc + i
                                ins = nc.scalar.activation(
                                    pr[:, h % 2, cc, o:o + w], PS[:, score_bank(h) + cc, o:o + w], ACT.Exp,
                                    bias=att[:, h, at:at + 1], accum_out=att[:, h, 4 + at:5 + at])
                        ins.then_inc(sem("exp_done"), 1)
                    if 1 <= h <= H:
                        n = H * l + h - 1
                        act.wait_ge(sem("probs_turned"), n + 1)
                        if n >= 1:
                            act.wait_ge(sem("attn_out"), n)
                        nc.scalar.activation(aT, PS[:, 2:4, 0:384], ACT.Copy).then_inc(sem("aT_ready"), 1)
                    if h == H:
                        act.wait_ge(sem("head_squares"), l + 1)
                        roots[0] += 1
                        root(mroot, msq, roots[0], 1.0 / P)
                    if h >= 2:
                        g = h - 2
                        act.wait_ge(sem("head_mixed"), H * l + g + 1)
                        for i in range(NT):
                            after(nc.scalar.activation(sqh, xn[:, i, g * P:(g + 1) * P], ACT.Square,
                                                       accum_out=small[:, 16 + 4 * i + g:17 + 4 * i + g]))
                roots[0] += 1
                root(small[:, 24:32], small[:, 16:24], roots[0], 1.0 / P)
                split_turned(lambda k: mixA[:, k:k + 1], lambda k: 0.0)
                for n in range(2):
                    for q in range(0 if n else AHEAD, 4):
                        plan_quarter(("out", l, n), q)
                between_layers(2 * l, SPLIT_AT[("out", l, 1), 3] + 1, ("ffn", 0, 0) if l == 0 else None)
                split_turned(lambda k: modA[:, 1, k:k + 1], lambda k: modcol[:, 24 + k:25 + k],
                             ("late_cols_taken", 1) if l else ("ada_taken", 10))

            def extras(ps, q):
                for ch in range(NCH):
                    if q == LAST_Q[("gate", ch)] + SPLIT:
                        act.wait_ge(sem("w_used"), ps.split(LAST_Q[("gate", ch)]))
                        for b in range(ps.blocks):
                            ins = nc.scalar.activation(hidden[:, b, :], PS[:, ps.gate_bank(b), :], ACT.Silu)
                        ins.then_inc(sem("silu_done"), 1)
                    if q == turn_after(ch, ps.blocks) + SPLIT:
                        act.wait_ge(sem("hidden_turned"), ps.chunk(ch))
                        for b in range(ps.blocks):
                            ins = nc.scalar.activation(sT_hi[:, :, ps.turned_cols(ch, b)],
                                                       PS[:, ps.turn_bank(b), :].rearrange("p (a b) -> p a b", a=4), ACT.Copy)
                        ins.then_inc(sem("sT_hi_done"), 1)

            ahead(("in", 0, 0))
            split_turned(lambda k: modA[:, 0, k:k + 1], lambda k: modcol[:, k:k + 1], ("ada_taken", 4))
            mixer(0)
            for q in range(PASS_Q):
                extras(dense, q)
                if q >= AHEAD:
                    plan_quarter(("ffn", 0, q // 4), q % 4)
            fetch_sqrt()
            between_layers(1, dense.split(PASS_Q - 1), ("in", 1, 0))
            split_turned(lambda k: modA[:, 0, k:k + 1], lambda k: modcol[:, k:k + 1], ("late_cols_taken", 1))
            mixer(1)
            act.wait_ge(sem("top_gap"), 1)
            nc.scalar.activation(tw[:, 2:4], tw[:, 0:2], ACT.Exp).then_inc(sem("top_exp"), 1)

            def modulate(k, n):
                if k == 0:
                    act.wait_ge(sem("gathered"), n)
                ins = nc.scalar.activation(xg[:, k * P:(k + 1) * P], PS[:, 2 + k // 4, (k % 4) * P:(k % 4 + 1) * P],
                                           ACT.Identity, bias=modcol[:, 24 + k:25 + k], scale=modA[:, 1, k:k + 1])
                if k == KT - 1:
                    ins.then_inc(sem("xg_ready"), 1)

            def expert_hi(n):
                act.wait_ge(sem("xg_ready"), n)
                nc.scalar.activation(hT_hi[:, :, 0:P], xg.rearrange("p (a b) -> p a b", a=KT), ACT.Copy
                                     ).then_inc(sem("xT_hi_done"), 1)

            def expert_rows():
                nc.scalar.activation(ye_hi, PS[:, 4:6, :].rearrange("p n (a b) -> p (n a) b", b=P), ACT.Copy,
                                     scale=gcur[:, 2:3]).then_inc(sem("ye_hi_done"), 1)

            def moe_round(r):
                g0 = (NE + 1) * r
                for k in range(KT):
                    modulate(k, g0 + 1)
                expert_hi(g0 + 1)
                with act.Fori(0, NE) as e:
                    ps = moe_pass(e, r)
                    for q in range(PASS_Q):
                        extras(ps, q)
                        if q == 4:
                            act.wait_ge(sem("w_used"), ps.split(0))
                            expert_rows()
                        if q == 28:
                            act.wait_ge(sem("comb_turned"), ps.expert())
                            nc.scalar.activation(combT[:], PS[:, 6, 0:S], ACT.Copy)
                            nc.scalar.activation(gcur[:, 2:3], PS[:, 6, S:S + 1], ACT.Copy).then_inc(sem("slot_gates"), 1)
                        if q == 32:
                            act.wait_ge(sem("slot_gates"), ps.expert())
                        if 52 <= q < 52 + KT:
                            modulate(q - 52, e + g0 + 2)
                        if q == PASS_Q - 1:
                            act.wait_ge(sem("w_used"), ps.split(LAST_Q[("up", NCH - 1)]))
                            expert_hi(e + g0 + 2)
                        act.wait_ge(sem(f"moe_loaded{q % MOE_RAW}"), ps.moe_loaded(q))
                        hi_quarter(moe_slot(q), ps.split_static(q), ps.split(q) - SPLIT)
                act.wait_ge(sem("w_used"), SPLIT_MOE + (r + 1) * NE * PASS_Q)
                expert_rows()

            moe_round(0)
            act.wait_ge(sem("flag_ready"), 1)
            over = act.value_load(flag[0:1, 0:1], min_val=0, max_val=1)
            with act.If(over > 0):
                moe_round(1)
            fetch_sqrt()
            act.wait_ge(sem("y_complete"), 1)
            for i in range(NT):
                norm_token(y_sb[:, i, :], junk, i)

        @block.vector
        def _(dve):
            done = [0]

            def after(ins):
                done[0] += 1
                ins.then_inc(sem("dve_step"), 1)
                dve.wait_ge(sem("dve_step"), done[0])

            def lo_quarter(src, w, hi):
                dve.wait_ge(sem("hi_ready"), hi)
                nc.vector.tensor_tensor(w_lo[:, w % SPLIT, :], src, w_hi[:, w % SPLIT, :],
                                        ALU.subtract).then_inc(sem("raw_used"), 1)

            def plan_quarter(p, q):
                lo_quarter(raw[:, RAW_AT[p, q] % RAW, :], SPLIT_AT[p, q], SPLIT_AT[p, q] + 1)

            roots = [0]

            def ahead(p):
                for q in range(AHEAD):
                    plan_quarter(p, q)

            def invert_root(dst, src):
                roots[0] += 1
                dve.wait_ge(sem("root_done"), roots[0])
                after(nc.vector.reciprocal(dst, src))

            def normalise(i):
                invert_root(small[:, 4 + i:5 + i], small[:, 2 + i:3 + i])
                nc.vector.tensor_scalar(xn[:, i, :], xs[:, i, :], small[:, 4 + i:5 + i], None,
                                        ALU.mult).then_inc(sem("xn_ready"), 1)

            turns = [0]

            def split_turned():
                for b in range(4):
                    turns[0] += 1
                    dve.wait_ge(sem("hT_hi_done"), turns[0])
                    nc.vector.tensor_tensor(hT_lo[:, 2 * b:2 * b + 2, :], htmp[:, b % 2, :].rearrange("p (k n) -> p k n", k=2),
                                            hT_hi[:, 2 * b:2 * b + 2, :], ALU.subtract).then_inc(sem("hT_lo_done"), 1)

            def ada_acc(l, n):
                if (l, n) in LATE_ADA:
                    return acc1[:, LATE_ADA.index((l, n)), :]
                return acc0[n % 4] if n < 5 else acc9 if n == 9 else acc56[:, n - 5, :]

            def ada_sum(l, n, q):
                acc = ada_acc(l, n)
                r = RAW_AT[("ada", l, n), q]
                dve.wait_ge(sem(f"raw_loaded{r % RAW}"), 16 * (r // RAW + 1))
                v = raw_slot(r, False)
                for j in range(2):
                    k = 2 * q + j
                    if k == 0:
                        ins = nc.vector.tensor_scalar(acc, v[:, j, :], cact[:, k:k + 1], None, ALU.mult)
                    else:
                        ins = nc.vector.scalar_tensor_tensor(acc, v[:, j, :], cact[:, k:k + 1], acc, ALU.mult, ALU.add)
                    if j == 0:
                        after(ins)
                ins.then_inc(sem("raw_used"), 1)
                dve.wait_ge(sem("raw_used"), r + 1)

            def gate_row(l, n, bank, g, gain):
                sub, half = (0 if n // 2 == 2 else 1), slice((n % 2) * NC, (n % 2 + 1) * NC)
                dve.wait_ge(sem(f"grow_loaded{2 * l + sub}"), 32)
                after(nc.vector.tensor_tensor(grow[:, g, half], PS[:, bank, :], grow[:, g, half], ALU.add))
                return nc.vector.tensor_tensor(grow[:, g, half], grow[:, g, half], ngb[:, gain, half], ALU.mult)

            def mod_columns(l, n, count, bank):
                c = slice(4 * n, 4 * (n + count))
                after(nc.vector.tensor_tensor(modcol[:, c], PS[:, bank, c],
                                              colT[:, 1, 48 * l + c.start:48 * l + c.stop], ALU.add))

            def mod_scale(l, sub):
                at, s = 8 * (4 * l + 2 * sub), 8 * (1 + 3 * sub)
                return nc.vector.scalar_tensor_tensor(modA[:, sub, :], modcol[:, s:s + 8], 1.0, colT[:, 0, at:at + 8],
                                                      ALU.add, ALU.mult)

            def ada_take(n):
                i = ADA_ORDER.index(n)
                dve.wait_ge(sem("ada_summed"), i + 1 if i < ADA_EARLY or n == 5 else len(ADA_ORDER) - 1)
                if n // 2 == 2:
                    ins = gate_row(0, n, 5 if n == 4 else 1, 0, 3)
                else:
                    c = slice(4 * n, 4 * n + 4)
                    ins = nc.vector.tensor_tensor(modcol[:, c], PS[:, 7, c], colT[:, 1, c], ALU.add)
                    if n == 6:
                        after(ins)
                        ins = mod_scale(0, 1)
                ins.then_inc(sem("ada_taken"), 1)

            def late_row(m, l, n, bank, g, gain):
                dve.wait_ge(sem("late_rows_summed"), m)
                gate_row(l, n, bank, g, gain).then_inc(sem("late_rows_taken"), 1)
                dve.wait_ge(sem("late_rows_taken"), m)

            def conv(l, half, tap):
                if tap == 0:
                    dve.wait_ge(sem("w_used"), SPLIT_AT[("in", l, half), 3] + 1)
                    if l == 0:
                        dve.wait_ge(sem("bias_stored"), 16)
                else:
                    dve.wait_ge(sem("tap_done"), 3 * (2 * l + half) + tap)
                for j in range(4):
                    n = 4 * half + j
                    psv = PS[:, 2 * half + j // 2, (j % 2) * S:(j % 2 + 1) * S]
                    wt = colT[:, 0, 64 + (4 * l + 3 - tap) * 8 + n:65 + (4 * l + 3 - tap) * 8 + n]
                    if tap == 0:
                        ins = nc.vector.tensor_scalar(qk[:, n, :], psv, wt, colT[:, 1, 96 + 8 * l + n:97 + 8 * l + n],
                                                      ALU.mult, ALU.add)
                    else:
                        ins = nc.vector.scalar_tensor_tensor(qk[:, n, tap:S], psv[:, 0:S - tap], wt, qk[:, n, tap:S],
                                                             ALU.mult, ALU.add)
                ins.then_inc(sem("tap_done" if tap < 3 else "conv_done"), 1)

            def split_gates(n, l):
                dve.wait_ge(sem("gw_loaded"), 16 * (n + 1))
                if n:
                    dve.wait_ge(sem("gates_done"), n)
                after(nc.vector.tensor_copy(gw_hi[:], gw[:]))
                nc.vector.tensor_tensor(gw_lo[:], gw[:], gw_hi[:], ALU.subtract).then_inc(sem("gw_split"), 1)

            zi, zf, lnf, cum, a_row, run_max, stab = (grows[:, i, :] for i in (0, 1, 2, 3, 4, 5, 6))

            def gate_rows_in(l):
                dve.wait_ge(sem("gates_done"), l + 1)
                after(nc.vector.memset(grows[:, 7, :], 1.0))
                nc.vector.tensor_scalar(zi, PS[0:H, 7, 0:S], gbias[:, 2 * l:2 * l + 1], None, ALU.add)
                nc.vector.tensor_scalar(zf, PS[0:H, 7, S:2 * S], gbias[:, 2 * l + 1:2 * l + 2], None, ALU.add
                                        ).then_inc(sem("gate_pre"), 1)

            def gate_chain(l):
                dve.wait_ge(sem("log_done"), l + 1)
                after(nc.vector.scalar_tensor_tensor(lnf, zf, 0.0, lnf, ALU.min, ALU.subtract))
                after(nc.vector.tensor_tensor_scan(cum, grows[:, 7, :], lnf, 0.0, ALU.mult, ALU.add))
                after(nc.vector.tensor_tensor(a_row, zi, cum, ALU.subtract))
                after(nc.vector.tensor_tensor_scan(run_max, a_row, a_row, 0.0, ALU.max, ALU.max))
                after(nc.vector.tensor_scalar(zi, run_max, -1.0, None, ALU.mult))
                nc.vector.tensor_tensor(stab, cum, run_max, ALU.add).then_inc(sem("gate_ready"), 1)

            def post(l, sub, y, k, i):
                ytmp = ytmp0 if k == 0 else ytmp1
                invert_root(small[:, 4 + i:5 + i], small[:, 2 + i:3 + i])
                after(nc.vector.scalar_tensor_tensor(ytmp.rearrange("p (a b) -> p a b", a=2), y, small[:, 4 + i:5 + i],
                                                     grow[:, (sub, 2 * sub)[l], :].rearrange("p (a b) -> p a b", a=2),
                                                     ALU.mult, ALU.mult))
                nc.vector.tensor_tensor(xs[:, i, :], xs[:, i, :], ytmp, ALU.add).then_inc(
                    sem("x_final" if k == 3 else "x_added"), 1)
                if k < 3:
                    dve.wait_ge(sem("x_added"), NT * k + i + 1)

            def between_layers(l, sub, k, following):
                for i in range(NT):
                    post(l, sub, PS[:, 4 + 2 * i:6 + 2 * i, :], k, i)
                    if following is not None:
                        plan_quarter(following, 2 * i)
                    normalise(i)
                    if following is not None and i == 0:
                        plan_quarter(following, 1)

            def heads(v):
                return v.rearrange("p (h d) -> p h d", h=H)

            def wide(v):
                return v.unsqueeze(2).to_broadcast([P, H, P])

            def mlstm_weights(l, h):
                n = H * l + h
                dve.wait_ge(sem("decay_done"), n + 1)
                dve.wait_ge(sem("mqk_done"), n + 1)
                nc.vector.scalar_tensor_tensor(Sw, PS[:, 5, 0:384], float(P) ** -0.5, E, ALU.mult, ALU.mult
                                               ).then_inc(sem("sw_done"), 1)

            def mlstm_out(l):
                dve.wait_ge(sem("mlstm_sums"), H * (l + 1))
                dve.wait_ge(sem("floor_ready"), l + 1)
                after(nc.vector.tensor_copy(dn, PS[:, 5, 384:392]))
                after(nc.vector.scalar_tensor_tensor(dn, dn, -1.0, dn, ALU.mult, ALU.max))
                dn3 = dn.rearrange("p (i h) -> p i h", i=NT)
                after(nc.vector.tensor_tensor(dn3, dn3, acol[:, :, 4:8], ALU.max))
                after(nc.vector.reciprocal(dn, dn))
                for i in range(NT):
                    nc.vector.tensor_tensor(heads(xn[:, i, NC:D]), heads(PS[:, 6 + i, :]), wide(dn[:, 4 * i:4 * i + 4]),
                                            ALU.mult).then_inc(sem("num_taken"), 1)
                    dve.wait_ge(sem("num_taken"), NT * l + i + 1)

            def mlstm_gate(l, i):
                v = xn[:, i, NC:D]
                after(nc.vector.tensor_tensor(v, v, so[:, i, :], ALU.mult))
                after(nc.vector.tensor_tensor(sq, v, v, ALU.mult))
                ins = nc.vector.tensor_reduce(msq[:, 4 * i:4 * i + 4], heads(sq), AX, ALU.add)
                if i == NT - 1:
                    ins.then_inc(sem("head_squares"), 1)
                else:
                    after(ins)

            def scores_max(l, h):
                dve.wait_ge(sem("scores_done"), H * l + h + 1)
                mx = att[:, h, 0:4].rearrange("p (c i) -> p c i", c=2)
                nc.vector.tensor_reduce(mx[:, :, 0], PS[:, score_bank(h):score_bank(h) + 2, 0:P], AX, ALU.max)
                after(nc.vector.tensor_reduce(mx[:, :, 1], PS[:, score_bank(h):score_bank(h) + 2, P:384], AX, ALU.max))
                nc.vector.tensor_scalar(att[:, h, 0:4], att[:, h, 0:4], -1.0, None, ALU.mult
                                        ).then_inc(sem("scores_max"), 1)

            def combine(l, h):
                n = H * l + h
                r = att[:, h, 4:8]
                dve.wait_ge(sem("exp_done"), n + 1)
                after(nc.vector.reciprocal(r, r))
                after(nc.vector.tensor_scalar(r[:, 2:4], r[:, 2:4], lamc[:, l:l + 1], None, ALU.mult))
                dve.wait_ge(sem("attn_out"), n + 1)
                o = slice(h * P, (h + 1) * P)
                for i in range(NT):
                    ins = nc.vector.tensor_scalar(xn[:, i, o], PS[:, 4 + h % 2, S + i * P:S + (i + 1) * P], r[:, 2 + i:3 + i], None, ALU.mult)
                after(ins)
                for i in range(NT):
                    ins = nc.vector.scalar_tensor_tensor(xn[:, i, o], PS[:, 4 + h % 2, i * P:(i + 1) * P], r[:, i:i + 1], xn[:, i, o],
                                                         ALU.mult, ALU.subtract)
                ins.then_inc(sem("head_mixed"), 1)

            def mixer(l):
                split_gates(l, l)
                for n in range(len(W_IN)):
                    for q in range(4):
                        for half in range(2):
                            if 0 <= 4 * (n - half - 1) + q - 3 < 4:
                                conv(l, half, 4 * (n - half - 1) + q - 3)
                        if q == 0 and n == 2:
                            gate_rows_in(l)
                        if q == 3 and n == 3:
                            gate_chain(l)
                        if l == 0 and n == 3 and q == 3:
                            ada_take(4)
                        if l == 0 and n in ADA_BESIDE:
                            ada_sum(0, ADA_BESIDE[n], q)
                        if q == 2 and n == 4:
                            dve.wait_ge(sem("gate_cols"), l + 1)
                            nc.vector.tensor_copy(acol[:], PS[:, 7, 0:16].rearrange("p (a b) -> p a b", a=NT)
                                                  ).then_inc(sem("gate_cols_copied"), 1)
                        for h in range(H):
                            if 4 * (n - 4) + q == DECAY_AT[h] + 3:
                                mlstm_weights(l, h)
                        if l == 1:
                            for m, (piece, bank, g, gain, at) in enumerate(LATE_ROWS_1):
                                if 4 * n + q == at:
                                    late_row(3 + m, 1, piece, bank, g, gain)
                        if n or q >= AHEAD:
                            plan_quarter(("in", l, n), q)
                ahead(("out", l, 0))
                nc.vector.tensor_scalar(mixA[:, 0:H], colT[:, 2, l:l + 1].to_broadcast([P, H]),
                                        float(1.0 - (0.8 - 0.6 * math.exp(-0.3 * l))), None, ALU.mult)
                after(nc.vector.tensor_copy(mixA[:, H:2 * H], colT[:, 2, 2 + 4 * l:6 + 4 * l]))
                mlstm_out(l)
                for h in range(H + 2):
                    if h < H:
                        scores_max(l, h)
                    if h < NT:
                        mlstm_gate(l, h)
                    if h >= 2:
                        combine(l, h - 2)
                    if h == H:
                        invert_root(mroot, mroot)
                        for i in range(NT):
                            nc.vector.tensor_tensor(heads(xn[:, i, NC:D]), heads(xn[:, i, NC:D]),
                                                    wide(mroot[:, 4 * i:4 * i + 4]), ALU.mult)
                invert_root(small[:, 24:32], small[:, 24:32])
                for i in range(NT):
                    nc.vector.tensor_tensor(heads(xn[:, i, 0:NC]), heads(xn[:, i, 0:NC]),
                                            wide(small[:, 24 + 4 * i:28 + 4 * i]), ALU.mult).then_inc(sem("mixed_ready"), 1)
                split_turned()
                for n in range(2):
                    for q in range(0 if n else AHEAD, 4):
                        plan_quarter(("out", l, n), q)
                        if l == 0 and n == 1:
                            ada_take(ADA_ORDER[ADA_EARLY + q])
                if l == 0:
                    ada_take(5)
                if l == 1:
                    split_gates(2, None)
                between_layers(l, 0, 2 * l, ("ffn", 0, 0) if l == 0 else None)
                split_turned()

            def extras(ps, q):
                for ch in range(NCH):
                    if q == LAST_Q[("up", ch)] + SPLIT:
                        dve.wait_ge(sem("w_used"), ps.split(LAST_Q[("up", ch)]))
                        dve.wait_ge(sem("silu_done"), ps.chunk(ch))
                        for b in range(ps.blocks):
                            ins = nc.vector.tensor_tensor(hidden[:, b, :], PS[:, ps.up_bank(b), :], hidden[:, b, :], ALU.mult)
                        ins.then_inc(sem("hidden_ready"), 1)
                    if q == turn_after(ch, ps.blocks) + SPLIT:
                        dve.wait_ge(sem("sT_hi_done"), ps.chunk(ch))
                        for b in range(ps.blocks):
                            ins = nc.vector.tensor_tensor(sT_lo[:, :, ps.turned_cols(ch, b)],
                                                          PS[:, ps.turn_bank(b), :].rearrange("p (a b) -> p a b", a=4),
                                                          sT_hi[:, :, ps.turned_cols(ch, b)], ALU.subtract)
                        ins.then_inc(sem("sT_lo_done"), 1)

            def relative_bias():
                nc.vector.memset(relb[32:33, :, :], 1.0)
                dve.wait_ge(sem("rel_loaded"), 16)
                nc.vector.tensor_copy(relb[0:N_BUCKETS, :, :],
                                      lamc[0:N_BUCKETS, 4:4 + H].unsqueeze(2).to_broadcast([N_BUCKETS, H, P])
                                      ).then_inc(sem("relb_ready"), 1)

            def lambda_sums():
                dve.wait_ge(sem("lam_loaded"), 16)
                lv = lamrow.rearrange("p (a b) d -> p a b d", b=2)
                after(nc.vector.tensor_tensor(lamp, lv[:, :, 0, :], lv[:, :, 1, :], ALU.mult))
                nc.vector.tensor_reduce(small[:, 8:12], lamp, AX, ALU.add).then_inc(sem("lam_sums"), 1)

            nc.vector.memset(eps[:], EPS).then_inc(sem("eps_ready"), 1)
            dve.wait_ge(sem("cact_ready"), 1)
            for n in range(4):
                for q in range(4):
                    ada_sum(0, n, q)
                if n == 0:
                    relative_bias()
                    lambda_sums()
                    for i in range(NT):
                        normalise(i)
            dve.wait_ge(sem("cols_ready"), 1)
            dve.wait_ge(sem("ada_summed"), 4)
            mod_columns(0, 0, 4, 5)
            mod_scale(0, 0).then_inc(sem("ada_taken"), 4)
            ahead(("in", 0, 0))
            split_turned()
            dve.wait_ge(sem("lam_exp"), 1)
            for l in range(L):
                lam_init = 0.8 - 0.6 * math.exp(-0.3 * l)
                after(nc.vector.scalar_tensor_tensor(lamc[:, 4 + l:5 + l], lamc[:, 2 * l:2 * l + 1], float(lam_init),
                                                     lamc[:, 2 * l + 1:2 * l + 2], ALU.add, ALU.subtract))
            after(nc.vector.tensor_copy(lamc[:, 0:2], lamc[:, 4:6]))
            dve.wait_ge(sem("gbias_loaded"), 16)
            mixer(0)
            for g in range(len(GROUPS)):
                for q in range(4):
                    extras(dense, 4 * g + q)
                    if g or q >= AHEAD:
                        plan_quarter(("ffn", 0, g), q)
                    if g in LATE_BESIDE:
                        ada_sum(*LATE_ADA[LATE_BESIDE.index(g)], q)
            late_row(1, 0, 10, 0, 1, 0)
            late_row(2, 0, 11, 1, 1, 0)
            dve.wait_ge(sem("pool_added"), (KT - 1) * (len(POOL_ADA) + len(LATE_POOL)))
            between_layers(0, 1, 1, ("in", 1, 0))
            dve.wait_ge(sem("late_cols_summed"), 1)
            mod_columns(1, 0, 4, 4)
            mod_columns(1, 6, 4, 4)
            mod_scale(1, 0)
            mod_scale(1, 1).then_inc(sem("late_cols_taken"), 1)
            split_turned()
            mixer(1)

            dve.wait_ge(sem("gates_done"), 3)
            nc.vector.tensor_copy(lgT, PS[0:NE, 6, 0:S]).then_inc(sem("logit_rows"), 1)
            nc.vector.memset(routing[:, 0:54], 0.0)
            dve.wait_ge(sem("logits_turned"), 1)
            after(nc.vector.tensor_copy(lg, PS[:, 7, 0:16].rearrange("p (a b) -> p a b", a=NT)))
            for i in range(NT):
                after(nc.vector.max(top[:, i, :], lg[:, i, :]))
                after(nc.vector.max_index(midx[:, i, :], top[:, i, :], lg[:, i, :]))
            after(nc.vector.tensor_copy(topi, midx[:]))
            nc.vector.tensor_tensor(tw[:, 0:2], top[:, :, 1], top[:, :, 0], ALU.subtract).then_inc(sem("top_gap"), 1)
            for n in range(2):
                for i in range(NT):
                    ins = nc.vector.tensor_scalar(pick[:, n, i, :], iota[:, 0:NE], topi[:, i, n:n + 1], None, ALU.is_equal)
            after(ins)
            nc.vector.tensor_tensor(sel[:, :, 0:NE], pick[:, 0], pick[:, 1], ALU.add).then_inc(sem("sel_ready"), 1)
            dve.wait_ge(sem("ranks_done"), 1)
            after(nc.vector.tensor_copy(ranks[:, :, 0:NE], PS[:, 6, 16:32].rearrange("p (a b) -> p a b", a=NT)))

            def router_rest():
                dve.wait_ge(sem("top_exp"), 1)
                after(nc.vector.tensor_scalar(tw[:, 4:6], tw[:, 2:4], 1.0, None, ALU.add))
                after(nc.vector.reciprocal(tw[:, 6:8], tw[:, 4:6]))
                after(nc.vector.tensor_tensor(tw[:, 8:10], tw[:, 6:8], tw[:, 2:4], ALU.mult))
                for i in range(NT):
                    after(nc.vector.tensor_scalar(gates[:, i, 0:NE], pick[:, 1, i, :], tw[:, 8 + i:9 + i], None, ALU.mult))
                    after(nc.vector.scalar_tensor_tensor(gates[:, i, 0:NE], pick[:, 0, i, :], tw[:, 6 + i:7 + i],
                                                         gates[:, i, 0:NE], ALU.mult, ALU.add))
                after(nc.vector.tensor_reduce(tw[:, 10:11], PS[:, 6, 32:40], AX, ALU.max))
                after(nc.vector.tensor_scalar(tw[:, 11:12], tw[:, 10:11], float(P), None, ALU.is_gt))
                nc.vector.tensor_copy(flag[:], tw[:, 11:12]).then_inc(sem("flag_ready"), 1)
                after(nc.vector.memset(y_sb, 0.0))

            def onehots(dst, weight, col):
                for i in range(NT):
                    ins = nc.vector.tensor_scalar(dst[:, i, :], iota, ranks[:, i, col], weight[:, i, col],
                                                  ALU.is_equal, ALU.mult)
                return ins

            def expert_lo(n):
                dve.wait_ge(sem("xT_hi_done"), n)
                nc.vector.tensor_tensor(hT_lo[:, :, 0:P], xg.rearrange("p (a b) -> p a b", a=KT), hT_hi[:, :, 0:P],
                                        ALU.subtract).then_inc(sem("xT_ready"), 1)

            def rows_lo(n):
                dve.wait_ge(sem("ye_hi_done"), n)
                nc.vector.scalar_tensor_tensor(ye_lo, PS[:, 4:6, :].rearrange("p n (a b) -> p (n a) b", b=P),
                                               gcur[:, 2:3], ye_hi, ALU.mult, ALU.subtract).then_inc(sem("ye_ready"), 1)

            def add_scattered(i, n):
                dve.wait_ge(sem("scattered"), NT * n + i - 1)
                b = (6, 2)[i]
                ins = nc.vector.tensor_tensor(y_sb[:, i, :].rearrange("p (a b) -> p a b", a=2), PS[:, b:b + 2, :],
                                              y_sb[:, i, :].rearrange("p (a b) -> p a b", a=2), ALU.add)
                if i == NT - 1:
                    ins.then_inc(sem("y_added"), 1)
                    dve.wait_ge(sem("y_added"), n)

            def moe_round(r):
                g0 = (NE + 1) * r
                if r:
                    nc.vector.tensor_scalar(ranks, ranks, -float(P), None, ALU.add).then_inc(sem("ranks_moved"), 1)
                    dve.wait_ge(sem("ranks_moved"), 1)
                onehots(disp, sel, slice(0, 1)).then_inc(sem("disp_ready"), 1)
                nc.vector.tensor_scalar(combT[:], K[:, 384:640], 0.0, None, ALU.mult)
                nc.vector.memset(gcur[:, 2:3], 0.0).then_inc(sem("zeros_ready"), 1)
                if r == 0:
                    router_rest()
                expert_lo(g0 + 1)
                with dve.Fori(0, NE) as e:
                    ps = moe_pass(e, r)
                    for q in range(PASS_Q):
                        extras(ps, q)
                        if q in (10, 13):
                            add_scattered((q - 10) // 3, e + g0 + 1)
                        if q == 4:
                            nc.vector.tensor_copy(gcur[:, 0:NT], gates[:, :, bass.ds(e, 1)])
                            onehots(comb, sel, bass.ds(e, 1)).then_inc(sem("comb_ready"), 1)
                        if q == 6:
                            rows_lo(e + g0 + 1)
                        if q == 36:
                            onehots(disp, sel, bass.ds(e + 1, 1)).then_inc(sem("disp_ready"), 1)
                        if q == PASS_Q - 1:
                            expert_lo(e + g0 + 2)
                        lo_quarter(moe_slot(q), ps.split_static(q), ps.split(q))
                rows_lo(g0 + NE + 1)
                for i in range(NT):
                    add_scattered(i, g0 + NE + 1)

            moe_round(0)
            over = dve.value_load(flag[0:1, 0:1], min_val=0, max_val=1)
            with dve.If(over > 0):
                moe_round(1)
            nc.vector.memset(small[:, 58:59], 0.0).then_inc(sem("y_complete"), 1)
            for i in range(NT):
                post(1, 1, y_sb[:, i, :].rearrange("p (a b) -> p a b", a=2), 3, i)

        @block.tensor
        def _(pe):
            def three(dst, a_hi, a_lo, b_hi, b_lo, start, stop):
                nc.tensor.matmul(dst, a_hi, b_hi, start=start, stop=False, skip_group_check=True)
                nc.tensor.matmul(dst, a_hi, b_lo, start=False, stop=False, skip_group_check=True)
                return nc.tensor.matmul(dst, a_lo, b_hi, start=False, stop=stop, skip_group_check=True)

            def mm(dst, a, b, start=True, stop=True):
                return nc.tensor.matmul(dst, a, b, start=start, stop=stop, skip_group_check=True)

            def split_view(w):
                return (w_hi[:, w % SPLIT, :].rearrange("p (k n) -> p k n", k=2),
                        w_lo[:, w % SPLIT, :].rearrange("p (k n) -> p k n", k=2))

            turned = [0]

            def turn(src_sem, counts):
                for i in range(NT):
                    pe.wait_ge(sem(src_sem), counts[i])
                    if i == 0 and turned[0]:
                        pe.wait_ge(sem("hT_lo_done"), turned[0])
                    if i == 0 and turned[0] == 8:
                        pe.wait_ge(sem("ada_taken"), len(ADA_ORDER))
                    if i == 0 and turned[0] == 12:
                        pe.wait_ge(sem("late_rows_taken"), 2)
                    for b in range(4):
                        for j in range(2):
                            k = 2 * b + j
                            ins = nc.tensor.transpose(PS[:, b, j * S + i * P:j * S + (i + 1) * P],
                                                      xn[:, i, k * P:(k + 1) * P], ident)
                        if i == NT - 1:
                            ins.then_inc(sem("turned"), 1)
                turned[0] += 4

            def split_ready(q=3):
                pe.wait_ge(sem("hT_lo_done"), turned[0] - 3 + max(q, 1))

            def ada_reduce(n):
                if n in POOL_ADA:
                    m = POOL_ADA.index(n)
                    pe.wait_ge(sem("pool_added"), (KT - 1) * (m + 1))
                    acc = accp[:, m, :]
                else:
                    pe.wait_ge(sem("raw_used"), RAW_AT[("ada", 0, n), 3] + 1)
                    acc = acc0[n % 4] if n < 5 else acc9 if n == 9 else acc56[:, n - 5, :]
                if n > 3:
                    pe.wait_ge(sem("ada_taken"), min(ADA_ORDER.index(n), ADA_EARLY))
                if n // 2 == 2:
                    mm(PS[:, 5 if n == 4 else 1, :], ones, acc).then_inc(sem("ada_summed"), 1)
                else:
                    columns(acc, n, 7 if n >= 6 else 5).then_inc(sem("ada_summed"), 1)

            def columns(acc, n, bank):
                for j in range(4):
                    ins = mm(PS[:, bank, 4 * n + j:4 * n + j + 1], acc[:, j * P:(j + 1) * P], ones[:, 0:1])
                return ins

            def late_rows(first, rows):
                for m, (l, n, bank) in enumerate(rows):
                    mm(PS[:, bank, :], ones, acc1[:, LATE_ADA.index((l, n)), :]).then_inc(sem("late_rows_summed"), 1)

            def small_rows(l, dsts):
                pe.wait_ge(sem("gw_split"), l + 1)
                n = 8 // len(dsts)
                for i, dst in enumerate(dsts):
                    c = slice(i * n, (i + 1) * n)
                    for k in range(KT):
                        split_ready(k // 2)
                        ins = three(dst, gw_hi[:, k, c], gw_lo[:, k, c], hT_hi[:, k, :], hT_lo[:, k, :], k == 0, k == KT - 1)
                ins.then_inc(sem("gates_done"), 1)

            def token_quarter(w, q, banks, tiles=range(NT)):
                hi, lo = split_view(w)
                for i in tiles:
                    for j in range(2):
                        k = 2 * q + j
                        ins = three(PS[:, banks[i], :], hT_hi[:, k, i * P:(i + 1) * P], hT_lo[:, k, i * P:(i + 1) * P],
                                    hi[:, j, :], lo[:, j, :], k == 0, k == KT - 1)
                return ins

            def feature_quarter(w, q, b):
                hi, lo = split_view(w)
                for j in range(2):
                    k = 2 * q + j
                    for f in range(4):
                        ins = three(PS[:, b + f // 2, (f % 2) * S:(f % 2 + 1) * S], hi[:, j, f * P:(f + 1) * P],
                                    lo[:, j, f * P:(f + 1) * P], hT_hi[:, k, :], hT_lo[:, k, :],
                                    k == 0 and f % 2 == 0, k == KT - 1)
                return ins

            def piece_free(l, n):
                if n < 2:
                    return
                m = n - 2
                if m < 2:
                    pe.wait_ge(sem("conv_done"), 2 * l + m + 1)
                else:
                    pe.wait_ge(sem("in_out"), 5 * l + m - 1)

            def mlstm_logits(l, h):
                n = H * l + h
                if h >= 1:
                    pe.wait_ge(sem("sw_done"), n)
                else:
                    pe.wait_ge(sem("qk_ready"), 2 * (l + 1))
                    if l == 0:
                        pe.wait_ge(sem("ada_taken"), ADA_EARLY)
                    else:
                        pe.wait_ge(sem("late_rows_taken"), 6)
                nm = grows[:, 0, :]
                hs = headsel[:, h * P:(h + 1) * P]
                mm(PS[:, 4, 0:S], hs, nm, True, False)
                mm(PS[:, 4, 0:P], ident, negm, False, True)
                mm(PS[:, 4, S:384], hs, nm[:, P:S], False, False)
                mm(PS[:, 4, S:384], ident, negm, False, True).then_inc(sem("decay_logits"), 1)
                mm(PS[:, 5, 0:S], qk[:, H + h, 0:P], qk[:, h, :])
                mm(PS[:, 5, S:384], qk[:, H + h, P:S], qk[:, h, P:S]).then_inc(sem("mqk_done"), 1)

            def mlstm_sums(l, h):
                pe.wait_ge(sem("sw_done"), H * l + h + 1)
                if h == 0:
                    pe.wait_ge(sem("gate_cols_copied"), l + 1)
                    pe.wait_ge(sem("in_out"), 5 * l + 1)
                vh = lambda i: mv[:, i, h * P:(h + 1) * P]
                for i in range(NT):
                    for dst, rhs in ((PS[:, 6 + i, h * P:(h + 1) * P], vh),
                                     (PS[:, 5, 384 + 4 * i + h:385 + 4 * i + h], lambda _: ones[:, 0:1])):
                        if i == 0:
                            ins = mm(dst, Sw[:, 0:P], rhs(0))
                        else:
                            mm(dst, Sw[:, P:S], rhs(0), True, False)
                            ins = mm(dst, Sw[:, S:384], rhs(1), False, True)
                ins.then_inc(sem("mlstm_sums"), 1)

            def scores(l, h):
                if h >= 2:
                    pe.wait_ge(sem("exp_done"), H * l + h - 1)
                elif h == 1:
                    pe.wait_ge(sem("num_taken"), NT * (l + 1))
                elif l == 0:
                    pe.wait_ge(sem("bias_loaded"), 16 * H)
                for cc in range(2):
                    a, b = slice(cc * DH, (cc + 1) * DH), score_bank(h) + cc
                    mm(PS[:, b, 0:P], ident, biasT[:, h, P:S], True, False)
                    mm(PS[:, b, P:384], ident, biasT[:, h, :], False, False)
                    mm(PS[:, b, 0:P], aqT[a, h, 0:P], akT[a, h, 0:P], False, True)
                    ins = mm(PS[:, b, P:384], aqT[a, h, P:S], akT[a, h, :], False, True)
                ins.then_inc(sem("scores_done"), 1)

            def turn_probs(l, h):
                pe.wait_ge(sem("exp_done"), H * l + h + 1)
                for cc in range(2):
                    for j in range(3):
                        ins = nc.tensor.transpose(PS[:, 2 + cc, j * P:(j + 1) * P],
                                                  pr[:, h % 2, cc, j * P:(j + 1) * P], ident)
                ins.then_inc(sem("probs_turned"), 1)

            def attn_sums(l, h):
                pe.wait_ge(sem("aT_ready"), H * l + h + 1)
                if h >= 2:
                    pe.wait_ge(sem("head_mixed"), H * l + h - 1)
                vh = lambda i: av[:, i, h * P:(h + 1) * P]
                for cc in range(2):
                    o = PS[:, 4 + h % 2, 2 * cc * P:2 * (cc + 1) * P]
                    mm(o[:, 0:P], aT[:, cc, 0:P], vh(0))
                    mm(o[:, P:S], aT[:, cc, P:S], vh(0), True, False)
                    ins = mm(o[:, P:S], aT[:, cc, S:384], vh(1), False, True)
                ins.then_inc(sem("attn_out"), 1)

            def mixer(l):
                for n, (name, _) in enumerate(W_IN):
                    piece_free(l, n)
                    b = 2 * (n % 2)
                    for q in range(4):
                        for h in range(H):
                            if 4 * (n - 4) + q == DECAY_AT[h]:
                                mlstm_logits(l, h)
                            if 4 * (n - 4) + q == DECAY_AT[h] + 1:
                                mlstm_sums(l, h)
                        w = SPLIT_AT[("in", l, n), q]
                        pe.wait_ge(sem("raw_used"), RAW_AT[("in", l, n), q] + 1)
                        if n == 0:
                            split_ready(q)
                        if name in FEATURE_MAJOR:
                            ins = feature_quarter(w, q, b)
                        else:
                            ins = token_quarter(w, q, (b, b + 1))
                        ins.then_inc(sem("w_used"), 1)
                    if n == 0:
                        small_rows(l, [PS[0:H, 7, 0:S], PS[0:H, 7, S:2 * S]])
                    if l == 0 and n == 2:
                        ada_reduce(4)
                    if l == 1 and n == 2:
                        pe.wait_ge(sem("late_rows_taken"), 5)
                        late_rows(5, [(1, LATE_ROWS_1[3][0], LATE_ROWS_1[3][1])])
                    if n == 3:
                        pe.wait_ge(sem("gate_ready"), l + 1)
                        for i in range(NT):
                            mm(PS[:, 7, 8 * i:8 * i + 4], grows[:, 4, i * P:(i + 1) * P], ident[0:H, 0:H])
                            ins = mm(PS[:, 7, 8 * i + 4:8 * i + 8], grows[:, 6, i * P:(i + 1) * P], ident[0:H, 0:H])
                        ins.then_inc(sem("gate_cols"), 1)
                pe.wait_ge(sem("in_out"), 5 * (l + 1))
                scores(l, 0)
                scores(l, 1)
                for h in range(H):
                    turn_probs(l, h)
                    if h + 2 < H:
                        scores(l, h + 2)
                    attn_sums(l, h)
                if l == 0:
                    for m in ADA_ORDER[ADA_EARLY:-1]:
                        ada_reduce(m)
                turn("mixed_ready", (NT * l + 1, NT * l + 2))
                for q in range(4):
                    w = SPLIT_AT[("out", l, 0), q]
                    pe.wait_ge(sem("raw_used"), RAW_AT[("out", l, 0), q] + 1)
                    split_ready(q)
                    token_quarter(w, q, (4, 6)).then_inc(sem("w_used"), 1)
                if l == 0:
                    ada_reduce(5)
                for i in range(NT):
                    if l == 0 and i == NT - 1:
                        pe.wait_ge(sem("ada_taken"), len(ADA_ORDER) - 1)
                    for q in range(4):
                        pe.wait_ge(sem("raw_used"), RAW_AT[("out", l, 1), q] + 1)
                        ins = token_quarter(SPLIT_AT[("out", l, 1), q], q, (5, 7), [i])
                        if i == NT - 1:
                            ins.then_inc(sem("w_used"), 1)
                        elif q == 3:
                            ins.then_inc(sem("y_first"), 1)
                turn("xn_ready", (4 * l + 3, 4 * l + 4))

            def hidden_quarter(ps, q, tile=None):
                what, ch = GROUPS[q // 4]
                qq = q % 4
                w = ps.split_static(q)
                pe.wait_ge(sem("raw_used"), ps.raw(q))
                if ps.e is None and q < 4:
                    split_ready(q)
                if qq == 0 and what == "gate" and ch == 1:
                    pe.wait_ge(sem("silu_done"), ps.chunk(0))
                if qq == 0 and what == "up" and ch > 0 and ps.blocks == 2:
                    pe.wait_ge(sem("sT_lo_done"), ps.chunk(ch - 1))
                if qq == 0 and what == "down" and tile != 1:
                    pe.wait_ge(sem("sT_lo_done"), ps.chunk(ch))
                if what == "down":
                    for b in ps.blocks_of(tile):
                        c = ps.turned_cols(ch, b)
                        for n in range(2):
                            ins = three(PS[:, 4 + 2 * b + n, :], sT_hi[:, qq, c], sT_lo[:, qq, c],
                                        w_hi[:, w % SPLIT, n * NC:(n + 1) * NC], w_lo[:, w % SPLIT, n * NC:(n + 1) * NC],
                                        ch == 0 and qq == 0, ch == NCH - 1 and qq == 3)
                else:
                    hi, lo = split_view(w)
                    for b in range(ps.blocks):
                        bank = ps.gate_bank(b) if what == "gate" else ps.up_bank(b)
                        for j in range(2):
                            k = 2 * qq + j
                            ins = three(PS[:, bank, :], hT_hi[:, k, b * P:(b + 1) * P], hT_lo[:, k, b * P:(b + 1) * P],
                                        hi[:, j, :], lo[:, j, :], k == 0, k == KT - 1)
                if tile != 0:
                    ins.then_inc(sem("w_used"), 1)
                elif qq == 3:
                    ins.then_inc(sem("y_first"), 1)
                for c2 in range(NCH):
                    if q == turn_after(c2, ps.blocks):
                        pe.wait_ge(sem("hidden_ready"), ps.chunk(c2))
                        for b in range(ps.blocks):
                            for f in range(4):
                                ins = nc.tensor.transpose(PS[:, ps.turn_bank(b), f * P:(f + 1) * P],
                                                          hidden[:, b, f * P:(f + 1) * P], ident)
                        ins.then_inc(sem("hidden_turned"), 1)

            pe.wait_ge(sem("tables_loaded"), 16)
            pe.wait_ge(sem("relb_ready"), 1)
            for h in range(H):
                ins = mm(PS[:, 4 + h, 0:384], relb[:, h, :], onehot)
            ins.then_inc(sem("bias_rows"), 1)
            turn("xn_ready", (1, 2))
            pe.wait_ge(sem("rows_loaded"), 16 * 6)
            pe.wait_ge(sem("bias_rows_copied"), 1)
            for t, n in ((0, 128), (1, 112), (2, 10)):
                ins = nc.tensor.transpose(PS[:, 4, t * P:t * P + n], tabs[0:n, t, :], ident[0:n, 0:n])
            ins.then_inc(sem("cols_turned"), 1)
            for n in range(4):
                ada_reduce(n)
            mixer(0)
            for q in range(PASS_Q - 4):
                hidden_quarter(dense, q)
            late_rows(0, ((0, 10, 0), (0, 11, 1)))
            for i in range(NT):
                for q in range(PASS_Q - 4, PASS_Q):
                    hidden_quarter(dense, q, i)
            pe.wait_ge(sem("pool_added"), (KT - 1) * (len(POOL_ADA) + len(LATE_POOL)))
            pe.wait_ge(sem("x_added"), 3)
            for n in (0, 1, 2, 3, 6, 7, 8, 9):
                ins = columns(acc1[:, LATE_ADA.index((1, n)), :], n, 4)
            ins.then_inc(sem("late_cols_summed"), 1)
            turn("xn_ready", (5, 6))
            pe.wait_ge(sem("late_cols_taken"), 1)
            late_rows(2, [(1, piece, bank) for piece, bank, *_ in LATE_ROWS_1[:3]])
            mixer(1)
            small_rows(2, [PS[0:NE, 6, 0:S]])
            pe.wait_ge(sem("logit_rows"), 1)
            for i in range(NT):
                ins = nc.tensor.transpose(PS[:, 7, 8 * i:8 * i + 8], lgT[:, i * P:(i + 1) * P], ident[0:NE, 0:NE])
            ins.then_inc(sem("logits_turned"), 1)
            pe.wait_ge(sem("sel_ready"), 1)
            mm(PS[:, 6, 16:24], before, sel[:, 0, 0:NE])
            mm(PS[:, 6, 24:32], ones, sel[:, 0, 0:NE], True, False)
            mm(PS[:, 6, 24:32], before, sel[:, 1, 0:NE], False, True)
            mm(PS[:, 6, 32:40], ones, sel[:, 0, 0:NE], True, False)
            mm(PS[:, 6, 32:40], ones, sel[:, 1, 0:NE], False, True).then_inc(sem("ranks_done"), 1)

            def gather():
                for k in range(KT):
                    for i in range(NT):
                        ins = mm(PS[:, 2 + k // 4, (k % 4) * P:(k % 4 + 1) * P], xn[:, i, k * P:(k + 1) * P], disp[:, i, :],
                                 k % 4 == 0 and i == 0, i == NT - 1)
                ins.then_inc(sem("gathered"), 1)

            def scatter():
                for i in range(NT):
                    for n in range(2):
                        dst, c = PS[:, (6 if i == 0 else 2) + n, :], slice(4 * n, 4 * n + 4)
                        mm(dst, combT[:, i * P:(i + 1) * P], ye_hi[:, c, :], True, False)
                        ins = mm(dst, combT[:, i * P:(i + 1) * P], ye_lo[:, c, :], False, True)
                    ins.then_inc(sem("scattered"), 1)

            def moe_round(r):
                g0 = (NE + 1) * r
                if r:
                    pe.wait_ge(sem("y_added"), g0)
                pe.wait_ge(sem("disp_ready"), g0 + 1)
                gather()
                pe.wait_ge(sem("zeros_ready"), r + 1)
                for n in range(2):
                    for j in range(2):
                        mm(PS[:, 4 + n, j * S:(j + 1) * S], combT[:, 0:P], combT[:])
                with pe.Fori(0, NE) as e:
                    ps = moe_pass(e, r)
                    pe.wait_ge(sem("xT_ready"), e + g0 + 1)
                    for q in range(PASS_Q):
                        if q == 7:
                            pe.wait_ge(sem("ye_ready"), e + g0 + 1)
                            scatter()
                        if q == 20:
                            pe.wait_ge(sem("comb_ready"), ps.expert())
                            pe.wait_ge(sem("y_added"), e + g0 + 1)
                            for i in range(NT):
                                nc.tensor.transpose(PS[:, 6, i * P:(i + 1) * P], comb[:, i, :], ident)
                            for i in range(NT):
                                ins = mm(PS[:, 6, S:S + 1], comb[:, i, :], gcur[:, i:i + 1], i == 0, i == NT - 1)
                            ins.then_inc(sem("comb_turned"), 1)
                        if q == 48:
                            pe.wait_ge(sem("disp_ready"), e + g0 + 2)
                            gather()
                        hidden_quarter(ps, q)
                pe.wait_ge(sem("ye_ready"), g0 + NE + 1)
                scatter()

            moe_round(0)
            pe.wait_ge(sem("flag_ready"), 1)
            over = pe.value_load(flag[0:1, 0:1], min_val=0, max_val=1)
            with pe.If(over > 0):
                moe_round(1)
            pe.wait_ge(sem("y_complete"), 1)


_INS = ["x", "c", "rel_bias", "ada_w", "ada_b", "norm_g", "w_in", "gate_b", "conv_w", "conv_b", "lam_vec",
        "attn_norm_g", "mlstm_norm_g", "w_out", "ffn_w1", "ffn_w3", "ffn_w2", "router_w", "moe_w1", "moe_w3", "moe_w2"]


def kernel(**inputs):
    import concourse.bacc as bacc
    from concourse.bass_utils import run_bass_kernel_spmd

    nc = bacc.Bacc("TRN2", target_bir_lowering=False, num_devices=1)
    arrays, args = {}, []
    for name in _INS + ["tables"]:
        a = shape_constants() if name == "tables" else np.ascontiguousarray(inputs[name])
        arrays[f"in_{name}"] = a
        args.append(nc.dram_tensor(f"in_{name}", a.shape, mybir.dt.from_np(a.dtype), kind="ExternalInput").ap())
    args.append(nc.dram_tensor("out_0", (1, S, D), F32, kind="ExternalOutput").ap())
    trunk(nc, *args)
    r = run_bass_kernel_spmd(nc, [arrays], core_ids=[0])
    return r.results[0]["out_0"]
```
